# Optimizing a Trainium2 kernel written in Bass

```python
import jax, jax.numpy as jnp
from jax import lax
import numpy as np

D_MODEL = 1024
BATCH = 1
SEQ = 1024
DEPTH = 1

HG_HEADS = 8
HG_KEY = 128
HG_VAL = D_MODEL // HG_HEADS
HG_FDIM = HG_HEADS * HG_KEY
HG_VDIM = HG_HEADS * HG_VAL
HG_CHUNK = 64
ATT_GROUPS = ((128, 1), (512, 4), (2048, 16))
N_GROUPS = 3
ATT_HEADS = 8
ATT_HEAD_DIM = 64
ATT_DIM = ATT_HEADS * ATT_HEAD_DIM
ROPE_THETA = 10000.0
N_BRANCH = 2
NORM_EPS = 1e-6
IN_SIZES = (HG_FDIM, HG_FDIM, HG_VDIM, HG_VDIM, 3 * N_GROUPS * ATT_DIM, ATT_DIM, N_BRANCH * D_MODEL)
IN_COLS = HG_FDIM * 2 + HG_VDIM * 2 + 3 * N_GROUPS * ATT_DIM + ATT_DIM + N_BRANCH * D_MODEL
IN_SPLITS = (HG_FDIM, 2 * HG_FDIM, 2 * HG_FDIM + HG_VDIM, 2 * HG_FDIM + 2 * HG_VDIM,
             2 * HG_FDIM + 2 * HG_VDIM + 3 * N_GROUPS * ATT_DIM,
             2 * HG_FDIM + 2 * HG_VDIM + 3 * N_GROUPS * ATT_DIM + ATT_DIM)

kernel_name = "hybrid_hgrn2_dilated_attn_gated_merge"

def rmsnorm(x, w):
    xf = x.astype(jnp.float32)
    y = xf * lax.rsqrt(jnp.mean(xf * xf, axis=-1, keepdims=True) + NORM_EPS)
    return (y * w.astype(jnp.float32)).astype(x.dtype)

def rope_tables(positions, dim):
    inv_freq = ROPE_THETA ** (-jnp.arange(0, dim, 2, dtype=jnp.float32) / dim)
    ang = positions.astype(jnp.float32)[..., None] * inv_freq
    return jnp.cos(ang), jnp.sin(ang)

def apply_rope(t, cos, sin):
    c = cos[:, :, None, None, :]
    s = sin[:, :, None, None, :]
    t1, t2 = jnp.split(t, 2, axis=-1)
    return jnp.concatenate([t1 * c - t2 * s, t2 * c + t1 * s], axis=-1)

def hgrn2_chunked(q, k, logf, v):
    B, S, H, K = q.shape
    V = v.shape[-1]
    C = HG_CHUNK
    nC = S // C

    def chunks(t):
        return t.reshape(B, nC, C, H, t.shape[-1]).transpose(1, 0, 3, 2, 4)

    causal = jnp.tril(jnp.ones((C, C), dtype=bool))

    def step(state, xs):
        qc, kc, gc, vc = xs
        b = jnp.cumsum(gc, axis=2)
        diff = b[:, :, :, None, :] - b[:, :, None, :, :]
        decay = jnp.exp(jnp.where(causal[:, :, None], diff, -jnp.inf))
        scores = jnp.einsum('bhtk,bhtsk,bhsk->bhts', qc, decay, kc)
        o = (jnp.einsum('bhts,bhsv->bhtv', scores, vc)
             + jnp.einsum('bhtk,bhkv->bhtv', qc * jnp.exp(b), state))
        b_last = b[:, :, -1:, :]
        state = (jnp.exp(b_last)[:, :, 0, :, None] * state
                 + jnp.einsum('bhsk,bhsv->bhkv', kc * jnp.exp(b_last - b), vc))
        return state, o

    s0 = jnp.zeros((B, H, K, V), jnp.float32)
    _, o = lax.scan(step, s0, (chunks(q), chunks(k), chunks(logf), chunks(v)))
    return o.transpose(1, 0, 3, 2, 4).reshape(B, S, H, V)

def dilated_window_attention(q, k, v, window, dilation):
    B, S, H, E = q.shape
    n = window // dilation
    M = S // dilation
    nblk = -(-M // n)
    Mp = nblk * n

    def to_residue(t):
        t = t.reshape(B, M, dilation, H, E).transpose(0, 2, 3, 1, 4)
        return jnp.pad(t, ((0, 0), (0, 0), (0, 0), (0, Mp - M), (0, 0)))

    def key_blocks(t):
        t = jnp.pad(t, ((0, 0), (0, 0), (0, 0), (n, 0), (0, 0))).reshape(B, dilation, H, nblk + 1, n, E)
        return jnp.concatenate([t[:, :, :, :-1], t[:, :, :, 1:]], axis=-2)

    qb = to_residue(q).reshape(B, dilation, H, nblk, n, E)
    kb = key_blocks(to_residue(k))
    vb = key_blocks(to_residue(v))
    s = jnp.einsum('brhcqe,brhcke->brhcqk', qb, kb) * (E ** -0.5)
    i = jnp.arange(n)[:, None]
    j = jnp.arange(2 * n)[None, :]
    dist = i + n - j
    c = jnp.arange(nblk)[:, None, None]
    valid = (dist >= 0) & (dist <= n) & (c * n - n + j >= 0)
    s = jnp.where(valid, s, -jnp.inf)
    m = jnp.max(s, axis=-1)
    p = jnp.exp(s - m[..., None])
    l = jnp.sum(p, axis=-1)
    o = jnp.einsum('brhcqk,brhcke->brhcqe', p, vb)

    def back(t):
        rest = t.shape[5:]
        t = t.reshape(B, dilation, H, Mp, *rest)[:, :, :, :M]
        t = jnp.moveaxis(t, 3, 1)
        return t.reshape(B, S, H, *rest)

    return back(o), back(m), back(l)

def hybrid_layer(x, cos, sin, norm_w, w_in, lb, hgrn_norm_w, w_branch_a, w_branch_b, w_out):
    B, S, _ = x.shape
    h = rmsnorm(x, norm_w)
    z = h @ w_in
    hq, hf, hi, hg, aqkv, ag, gates = jnp.split(z, IN_SPLITS, axis=-1)

    f = lb + (1.0 - lb) * jax.nn.sigmoid(hf.astype(jnp.float32))
    shp = (B, S, HG_HEADS, HG_KEY)
    q_a = jax.nn.silu(hq.astype(jnp.float32)).reshape(shp)
    o_a = hgrn2_chunked(q_a, (1.0 - f).reshape(shp), jnp.log(f).reshape(shp),
                        hi.astype(jnp.float32).reshape(B, S, HG_HEADS, HG_VAL))
    o_a = rmsnorm(o_a, hgrn_norm_w) * jax.nn.silu(hg.astype(jnp.float32)).reshape(B, S, HG_HEADS, HG_VAL)
    y_a = o_a.reshape(B, S, HG_VDIM).astype(x.dtype) @ w_branch_a

    aqkv = aqkv.astype(jnp.float32).reshape(B, S, 3, N_GROUPS, ATT_HEADS, ATT_HEAD_DIM)
    q_b = apply_rope(aqkv[:, :, 0], cos, sin)
    k_b = apply_rope(aqkv[:, :, 1], cos, sin)
    v_b = aqkv[:, :, 2]
    outs, maxes, dens = [], [], []
    for g, (window, dilation) in enumerate(ATT_GROUPS):
        o_g, m_g, l_g = dilated_window_attention(q_b[:, :, g], k_b[:, :, g], v_b[:, :, g], window, dilation)
        outs.append(o_g)
        maxes.append(m_g)
        dens.append(l_g)
    ms = jnp.stack(maxes)
    wts = jnp.exp(ms - jnp.max(ms, axis=0))
    den = jnp.sum(wts * jnp.stack(dens), axis=0)
    num = jnp.sum(wts[..., None] * jnp.stack(outs), axis=0)
    o_b = (num / den[..., None]).reshape(B, S, ATT_DIM) * jax.nn.silu(ag.astype(jnp.float32))
    y_b = o_b.astype(x.dtype) @ w_branch_b

    g_a, g_b = jnp.split(jax.nn.sigmoid(gates), N_BRANCH, axis=-1)
    merged = g_a * y_a + g_b * y_b
    return x + merged @ w_out

def setup_inputs(seed: int = 0) -> dict:
    key = jax.random.key(seed)
    ks = jax.random.split(key, 12)
    x = jax.random.normal(ks[0], (BATCH, SEQ, D_MODEL), jnp.float32)
    offsets = jax.random.randint(ks[1], (BATCH, 1), 0, 4096, dtype=jnp.int32)
    positions = offsets + jnp.arange(SEQ, dtype=jnp.int32)[None, :]
    norm_w = 1.0 + 0.02 * jax.random.normal(ks[2], (DEPTH, D_MODEL), jnp.float32)
    w_in = jax.random.normal(ks[3], (DEPTH, D_MODEL, IN_COLS), jnp.float32) * D_MODEL ** -0.5
    lb_logits = 0.5 * jax.random.normal(ks[4], (DEPTH + 1, HG_FDIM), jnp.float32)
    hgrn_norm_w = 1.0 + 0.02 * jax.random.normal(ks[5], (DEPTH, HG_VAL), jnp.float32)
    w_branch_a = jax.random.normal(ks[6], (DEPTH, HG_VDIM, D_MODEL), jnp.float32) * HG_VDIM ** -0.5
    w_branch_b = jax.random.normal(ks[7], (DEPTH, ATT_DIM, D_MODEL), jnp.float32) * ATT_DIM ** -0.5
    w_out = jax.random.normal(ks[8], (DEPTH, D_MODEL, D_MODEL), jnp.float32) * D_MODEL ** -0.5
    final_norm_w = 1.0 + 0.02 * jax.random.normal(ks[9], (D_MODEL,), jnp.float32)
    return {"x": x, "positions": positions, "norm_w": norm_w, "w_in": w_in, "lb_logits": lb_logits,
            "hgrn_norm_w": hgrn_norm_w, "w_branch_a": w_branch_a, "w_branch_b": w_branch_b,
            "w_out": w_out, "final_norm_w": final_norm_w}

def reference(x, positions, norm_w, w_in, lb_logits, hgrn_norm_w, w_branch_a, w_branch_b, w_out, final_norm_w):
    cos, sin = rope_tables(positions, ATT_HEAD_DIM)
    lower_bounds = jnp.cumsum(jax.nn.softmax(lb_logits.astype(jnp.float32), axis=0), axis=0)
    for layer in range(DEPTH):
        x = hybrid_layer(x, cos, sin, norm_w[layer], w_in[layer], lower_bounds[layer], hgrn_norm_w[layer],
                         w_branch_a[layer], w_branch_b[layer], w_out[layer])
    return rmsnorm(x, final_norm_w)


_drawn_inputs = setup_inputs


def setup_inputs(seed=0):
    import zlib

    import numpy as np

    out = dict(_drawn_inputs(seed))
    spreads = {}
    factors = {'norm_w': 5.93, 'lb_logits': 3.166, 'hgrn_norm_w': 23.616, 'final_norm_w': 8.113}
    for name, (base, spread) in spreads.items():
        noise = np.random.default_rng([zlib.crc32(name.encode()), seed]).standard_normal(out[name].shape)
        drawn = base * np.exp(spread * noise) if base else spread * noise
        out[name] = __import__('jax').numpy.asarray(drawn.astype(out[name].dtype))
    for name, factor in factors.items():
        out[name] = (out[name] * factor).astype(out[name].dtype)
    return out
```

```python
import numpy as np
from contextlib import ExitStack

import concourse.bass as bass
from concourse import mybir

P = 128
D_MODEL = 1024
SEQ = 1024
KT = D_MODEL // P
HEADS = 8
NB = SEQ // P
HALF = SEQ // 2
GROUPS = 3
DILATIONS = (1, 4, 16)
PAIRS = 4
EDIM = 64
HG_CHUNKS = 6
AT_CHUNKS = 10
N_HG = HEADS * HG_CHUNKS
N_AT = PAIRS * AT_CHUNKS
N_IN = N_HG + N_AT
LEVELS = (64, 32, 16, 8, 4, 2)
EPS = 1e-6
NEG = -1e30
ROPE_THETA = 10000.0
TINY = 2.0 ** -64


def chunk_columns():
    hq, hf, hi, hg = (n * D_MODEL for n in range(4))
    qkv = 4 * D_MODEL
    att = GROUPS * 8 * EDIM
    ag = qkv + 3 * att
    gates = ag + 8 * EDIM
    cols = []
    for h in range(HEADS):
        cols += [hf + P * h, hq + P * h, hi + P * h, hg + P * h, gates + P * h, gates + D_MODEL + P * h]
    for p in range(PAIRS):
        for g in range(GROUPS):
            cols += [qkv + s * att + g * 512 + P * p for s in (0, 1)]
        cols += [qkv + 2 * att + g * 512 + P * p for g in range(GROUPS)]
        cols += [ag + P * p]
    return cols


def shape_constants():
    s = np.arange(P)[:, None]
    level = np.zeros((8, P, P), np.float32)
    c = np.arange(64)[None, :]
    for j, span in enumerate((1, 0) + LEVELS):
        if span:
            t = (c // span) * 2 * span + span + c % span
            level[j] = np.tile((t // (2 * span) == s // (2 * span)) & (s % (2 * span) < span), (1, 2))
        else:
            level[j] = np.eye(P)
    i = np.arange(P)[None, :]
    own = np.where(i >= s, 0.0, NEG)
    after = np.where(s >= i, 0.0, NEG)
    same = np.where((i >= s) & (i // 64 == s // 64), 0.0, NEG)
    mask_t = np.concatenate([own, after, same, same], 1).astype(np.float32)
    mask_n = np.concatenate([after.T, own.T, same.T], 1).astype(np.float32)
    reset = np.ones((P, SEQ), np.float32)
    reset[:, ::P] = 0.0
    inv = (ROPE_THETA ** (-np.arange(0, EDIM, 2, dtype=np.float32) / np.float32(EDIM))).astype(np.float32)
    sign = np.where(np.arange(P) % EDIM < EDIM // 2, -1.0, 1.0)
    col = np.stack([np.tile(inv, 4), sign, np.full(P, EPS), np.full(P, 1.0 / P)], 1).astype(np.float32)
    sel = np.zeros((2, 2, P), np.float32)
    sel[0, 0] = sel[1, 1] = 1.0
    return {
        "c_level": np.ascontiguousarray(level.transpose(1, 0, 2)),
        "c_mask_t": mask_t, "c_mask_n": mask_n, "c_reset": reset, "c_col": col,
        "c_ident": np.eye(P, dtype=np.float32), "c_sel": sel,
    }



def build(nc, d, out):
    f32, f32r, bf16 = mybir.dt.float32, mybir.dt.float32r, mybir.dt.bfloat16
    u8, i32 = mybir.dt.uint8, mybir.dt.int32
    ACT = mybir.ActivationFunctionType
    ALU = mybir.AluOpType
    AX = mybir.AxisListType
    ctx = ExitStack()
    with ctx:
        sem = lambda name: ctx.enter_context(nc.semaphore(name))

        top = [0]

        def place(name, shape, dt=f32):
            n = int(np.prod(shape[1:])) * {f32: 4, f32r: 4, i32: 4, bf16: 2, u8: 1}[dt]
            t = nc.alloc_sbuf_tensor_at(name, shape, dt, offset=top[0])
            top[0] += (n + 31) // 32 * 32
            assert top[0] <= nc.sbuf_usable_end // 32 * 32, (name, top[0])
            return t

        top[0] = (nc.sbuf_base + 31) // 32 * 32
        ident = place("ident", [P, P])
        col = place("col", [P, 4])
        norm_w = place("norm_w", [P, KT])
        w_stage = [place(f"w_stage{s}", [P, KT, P]) for s in range(2)]
        w_hi = [place(f"w_hi{s}", [P, KT, P], f32r) for s in range(2)]
        w_lo = [place(f"w_lo{s}", [P, KT, P], f32r) for s in range(2)]
        cos_t = place("cos_t", [P, SEQ])
        sin_t = place("sin_t", [P, SEQ])
        mask_n = place("mask_n", [P, 3 * P])
        mask_b = place("mask_b", [P, 4 * P], bf16)
        ident_b = place("ident_b", [P, P], bf16)
        sel = place("sel", [2, 2, P], f32r)
        shift = place("shift", [2, SEQ], f32r)
        h_hi = place("h_hi", [P, KT, SEQ], f32r)
        h_lo = place("h_lo", [P, KT, SEQ], f32r)
        phase_base = top[0]
        x_in = place("x_in", [P, NB, D_MODEL])
        x_sq = place("x_sq", [P, D_MODEL])
        x_ss = place("x_ss", [P, NB])
        x_ln = place("x_ln", [P, NB])
        x_rs = place("x_rs", [P, NB])
        top[0] = phase_base
        level_mask = place("level_mask", [P, 8, HALF], u8)
        reset = place("reset", [P, SEQ])
        lb_in = place("lb_in", [P, 2, HEADS])
        lb = place("lb", [P, 6, HEADS])
        hgw = place("hgw", [P, 1])
        inv128 = place("inv128", [P, P])
        ff = place("ff", [P, SEQ])
        kk = place("kk", [P, SEQ])
        lf = place("lf", [P, SEQ])
        bb = place("bb", [P, SEQ])
        qq = place("qq", [P, SEQ])
        vt = place("vt", [P, SEQ])
        vv = place("vv", [P, NB, P])
        gg = place("gg", [P, SEQ])
        dd = [place(f"dd{s}", [P, SEQ]) for s in range(2)]
        ee = [place(f"ee{s}", [P, SEQ]) for s in range(2)]
        q_lv = [place(f"q_lv{s}", [P, HALF]) for s in range(2)]
        k_lv = [place(f"k_lv{s}", [P, SEQ]) for s in range(2)]
        q_one = place("q_one", [P, HALF])
        eb = place("eb", [P, SEQ])
        q_in = place("q_in", [P, SEQ])
        k_out = place("k_out", [P, SEQ])
        k_tok = place("k_tok", [P, NB, P])
        scores = place("scores", [P, NB, P])
        state = place("state", [P, NB, P])
        o_sq = place("o_sq", [P, SEQ])
        o_rs = place("o_rs", [P, SEQ])
        o_a = place("o_a", [P, SEQ])
        gate = [place(f"gate{s}", [P, SEQ]) for s in range(2)]

        top[0] = phase_base
        qk_hi = [[place(f"qk_hi{g}{s}", [P, SEQ], f32r) for s in range(2)] for g in range(GROUPS)]
        qk_lo = [[place(f"qk_lo{g}{s}", [P, SEQ], f32r) for s in range(2)] for g in range(GROUPS)]
        zz = [place(f"zz{s}", [P, SEQ]) for s in range(2)]
        z_swap = place("z_swap", [P, SEQ])
        roped = place("roped", [P, SEQ])
        vb = place("vb", [P, GROUPS, NB, 3 * EDIM])
        pt = [place(f"pt{s}", [P, HALF]) for s in range(2)]
        acc = [place(f"acc{h}", [P, SEQ]) for h in range(2)]
        s_ag = place("s_ag", [P, SEQ])
        m_all = place("m_all", [P, 2 * GROUPS * NB])
        m_t = place("m_t", [2 * GROUPS * NB, P])
        junk = place("junk", [P, 2, 2 * P])
        rejoin = top[0]
        v_t = place("v_t", [P, SEQ])
        r_den = place("r_den", [P, SEQ])
        o_b = place("o_b", [P, SEQ])
        top[0] = rejoin
        m_rows = place("m_rows", [2, GROUPS, SEQ])
        oa_hi, oa_lo = h_hi, h_lo
        top[0] = phase_base
        ob_hi = place("ob_hi", [P, PAIRS, SEQ], f32r)
        ob_lo = place("ob_lo", [P, PAIRS, SEQ], f32r)
        mg_hi = place("mg_hi", [P, KT, SEQ], f32r)
        mg_lo = place("mg_lo", [P, KT, SEQ], f32r)
        wq_hi = place("wq_hi", [P, KT, 2 * P], f32r)
        wq_lo = place("wq_lo", [P, KT, 2 * P], f32r)
        part = place("part", [P, SEQ])
        o_stat = place("o_stat", [P, 3, NB])
        g_in = [cos_t, sin_t]
        top[0] = phase_base
        yy = place("yy", [P, NB, D_MODEL])
        fnw = part

        z_ps = [ctx.enter_context(nc.psum_tensor(f"z_ps{s}", [P, HALF], f32)) for s in range(2)]
        pa, pb, pc = (ctx.enter_context(nc.psum_tensor(n, [P, 2, HALF], f32)) for n in ("pa", "pb", "pc"))

        gate_d = nc.dram_tensor("gate_d", [2, HEADS, P, SEQ], f32).ap()
        o_a_d = nc.dram_tensor("o_a_d", [HEADS, P, SEQ], f32).ap()

        o_b_d = nc.dram_tensor("o_b_d", [PAIRS, P, SEQ], f32).ap()
        m_d = nc.dram_tensor("m_d", [PAIRS, 2 * GROUPS * NB, P], f32).ap()

        const_in = sem("const_in")
        x_loaded = [sem(f"x_loaded{t}") for t in range(NB)]
        ss_done, rs_ln_done, rs_done, xn_done = sem("ss_done"), sem("rs_ln_done"), sem("rs_done"), sem("xn_done")
        xt_made, h_hi_done, h_lo_done = sem("xt_made"), sem("h_hi_done"), sem("h_lo_done")
        w_loaded = [sem(f"w_loaded{s}") for s in range(2)]
        w_hi_done, w_lo_done = sem("w_hi_done"), sem("w_lo_done")
        z_made = [sem(f"z_made{s}") for s in range(2)]
        z_taken = [sem(f"z_taken{s}") for s in range(2)]
        mask_done = sem("mask_done")
        lb_step, init_done = sem("lb_step"), sem("init_done")
        f_done, k_done, ln_done, b_done = sem("f_done"), sem("k_done"), sem("ln_done"), sem("b_done")
        eb_done, d_done, e_done = sem("eb_done"), sem("d_done"), sem("e_done")
        q_in_done, q_one_done, lv_done = sem("q_in_done"), sem("q_one_done"), sem("lv_done")
        k_out_done, kt_made, kt_taken = sem("k_out_done"), sem("kt_made"), sem("kt_taken")
        vt_made, v_taken, upd_made = sem("vt_made"), sem("v_taken"), sem("upd_made")
        lvl_made, lvl_taken, s_done = sem("lvl_made"), sem("lvl_taken"), sem("s_done")
        pv_made, sq_done, ms_made, ms_ln = sem("pv_made"), sem("sq_done"), sem("ms_made"), sem("ms_ln")
        ors_done, on_done, oa_done = sem("ors_done"), sem("on_done"), sem("oa_done")
        oa_stored = sem("oa_stored")
        gate_stored = [sem(f"gate_stored{s}") for s in range(2)]

        rope_step, sin_done = sem("rope_step"), sem("sin_done")
        vb_done = sem("vb_done")
        swapped, rope_a, rope_b, rope_sum = sem("swapped"), sem("rope_a"), sem("rope_b"), sem("rope_sum")
        qk_hi_done, qk_lo_done = sem("qk_hi_done"), sem("qk_lo_done")
        avt_made, av_taken = sem("avt_made"), sem("av_taken")
        mx_made, mx_taken, mt_made, mt_taken = sem("mx_made"), sem("mx_taken"), sem("mt_made"), sem("mt_taken")
        m_stored, m_loaded, mj_done, shift_done = sem("m_stored"), sem("m_loaded"), sem("mj_done"), sem("shift_done")
        st_made, pt_done, pu_made = sem("st_made"), sem("pt_done"), sem("pu_made")
        ob_taken = sem("ob_taken")
        den_ln, den_done, den_ag, ob_done, ob_stored = sem("den_ln"), sem("den_done"), sem("den_ag"), sem("ob_done"), sem("ob_stored")
        br_loaded = [sem(f"br_loaded{s}") for s in range(2)]
        br_hi_done, br_lo_done = sem("br_hi_done"), sem("br_lo_done")
        g_loaded = [sem(f"g_loaded{s}") for s in range(2)]
        ya_done, yb_done, mg_sum, mg_hi_done, mg_lo_done = sem("ya_done"), sem("yb_done"), sem("mg_sum"), sem("mg_hi_done"), sem("mg_lo_done")
        y_loaded = [sem(f"y_loaded{t}") for t in range(NB)]
        fnw_loaded = sem("fnw_loaded")
        qa_made, qa_taken, pb_made, pb_taken = sem("qa_made"), sem("qa_taken"), sem("pb_made"), sem("pb_taken")
        oss_done, oln_done, ors2_done, out_done = sem("oss_done"), sem("oln_done"), sem("ors2_done"), sem("out_done")
        out_stored = sem("out_stored")

        block = ctx.enter_context(nc.Block())
        first = lambda i: isinstance(i, int) and i == 0

        def value(eng, v):
            return v if isinstance(v, int) else eng.to_reg(v)


        UNITS = [(g, h, m) for g in range(GROUPS) for h in range(2) for m in range(4 if g < 2 else 2)]
        N_UNITS = len(UNITS)
        UNIT_SLOTS = {2: (0, 1, 2), 3: (3, 4, 5), 4: (6, 7), 5: (8, 9), 6: (10, 11), 7: (12, 13), 8: (14, 15),
                      9: (16, 17), 10: (18, 19)}
        SUM_AFTER = [1, 3, 5, 7, 9, 11, 13, 15, 16, 17, 18, 19]
        SUM_SLOTS = {3: (0,), 4: (1,), 5: (2,), 6: (3,), 7: (4,), 8: (5,), 9: (6,), 10: (7, 8), 11: (9, 10), 12: (11,)}
        N_SUMS = len(SUM_AFTER)
        MAX_SLOTS = {8 + u: (u // 4, u % 4) for u in range(8)} | {16: (2, 0), 17: (2, 1)}
        N_MAX = 2 * GROUPS * NB
        max_count = lambda u: 2 * u if u <= 16 else 32 + 4 * (u - 16)

        def unit_keys(g, m):
            if g == 0:
                return [(c, 256 * (c - 2 * m), 2 if c < NB - 1 else 1) for c in (2 * m, 2 * m + 1)]
            if g == 1:
                return [(2 * m, 0, 2), (2 * m + 1, 256, 1)]
            return [(4 * m + c, P * c, 1) for c in range(4)]

        def max_queries(g, m):
            if g == 2:
                return [(4 * m + c, P * c, False) for c in range(4)]
            return [(c, 256 * (c % 2), c > 0 if g == 0 else c % 2 == 1) for c in (2 * m, 2 * m + 1)]

        def by_residue(ap, g):
            return ap.rearrange("p (i r) -> p r i", r=DILATIONS[g])

        @block.sync
        def _(sp):
            def load_w(n, s, src):
                sp.dma_start(w_stage[s][:, 0:src.shape[1], :], src).then_inc(w_loaded[s], 16)

            for t in range(NB):
                sp.dma_start(x_in[:, t, :], d["x"][P * t:P * (t + 1), :]).then_inc(x_loaded[t], 16)
                if t == 0:
                    for s, src in ((ident, "c_ident"), (col, "c_col"), (norm_w, "norm_w")):
                        sp.dma_start(s[:], d[src]).then_inc(const_in, 16)
            load_w(0, 0, d["w_in"][0])
            load_w(1, 1, d["w_in"][1])
            sp.wait_ge(xt_made, 2 * KT)
            for s, src in ((reset, "c_reset"), (lb_in, "lb_logits"), (hgw, "hgrn_norm_w"), (mask_n, "c_mask_n")):
                sp.dma_start(s[:], d[src]).then_inc(const_in, 16)
            sp.dma_start(lf[:].bitcast(i32), d["positions"].to_broadcast([P, SEQ])).then_inc(const_in, 16)
            sp.dma_start(vt[:].rearrange("p (m c) -> p m c", c=P), d["c_level"]).then_inc(const_in, 16)
            sp.dma_start(bb[:, 0:4 * P], d["c_mask_t"]).then_inc(const_in, 16)
            sp.dma_start(qq[0:2, 0:2 * P].rearrange("p (a b) -> p a b", a=2), d["c_sel"]).then_inc(const_in, 16)

            def hgrn(i, prev, cur):
                for c in range(HG_CHUNKS):
                    if cur:
                        n = i * HG_CHUNKS + c
                        split = value(sp, n + 1)
                        sp.wait_ge(const_in, 48)
                        sp.wait_ge(w_lo_done, split)
                        sp.dma_start(w_stage[c % 2][:], d["w_in"][bass.ds(n + 2, 1)].rearrange("a p k c -> (a p) k c")).then_inc(w_loaded[c % 2], 16)
                    if prev and c == 1:
                        taken = value(sp, i * HG_CHUNKS)
                        sp.wait_ge(const_in, 48)
                        for s in range(2):
                            sp.wait_ge(z_taken[s], taken)
                        sp.dma_start(gate_d[1, bass.ds(i - 1, 1)].rearrange("a p t -> (a p) t"), gate[1][:]).then_inc(gate_stored[1], 16)
                    if prev and c == 4:
                        sp.wait_ge(const_in, 48)
                        sp.wait_ge(oa_done, i)
                        sp.dma_start(o_a_d[bass.ds(i - 1, 1)].rearrange("a p t -> (a p) t"), o_a[:]).then_inc(oa_stored, 16)
                    if cur and c == 5:
                        taken = value(sp, i * HG_CHUNKS + 5)
                        sp.wait_ge(const_in, 48)
                        for s in range(2):
                            sp.wait_ge(z_taken[s], taken)
                        sp.dma_start(gate_d[0, bass.ds(i, 1)].rearrange("a p t -> (a p) t"), gate[0][:]).then_inc(gate_stored[0], 16)

            hgrn(0, False, True)
            with sp.Fori(1, HEADS) as i:
                hgrn(i, True, True)
            hgrn(HEADS, True, False)
            sp.wait_ge(oa_stored, 16 * HEADS)
            for s in range(2):
                sp.wait_ge(gate_stored[s], 16 * HEADS)

            def load_stage(n, s):
                if isinstance(n, int) and n >= N_IN:
                    n -= N_IN
                    if n < 16:
                        src = d["w_a"][n // 2] if n % 2 == 0 else d["w_b"][n // 2]
                    elif n < 24:
                        src = d["w_out"][n - 16]
                    else:
                        return
                    sp.dma_start(w_stage[s][:, 0:src.shape[1], :], src).then_inc(w_loaded[s], 16)
                else:
                    sp.dma_start(w_stage[s][:], d["w_in"][bass.ds(n, 1)].rearrange("a p k c -> (a p) k c")).then_inc(w_loaded[s], 16)

            def attention(i, prev, cur, last_of_all=False):
                for c in range(AT_CHUNKS):
                    n = N_HG + i * AT_CHUNKS + c
                    if cur:
                        split = value(sp, n + 1)
                        sp.wait_ge(const_in, 48)
                        sp.wait_ge(w_lo_done, split)
                        load_stage(n + 2, c % 2)
                    if prev and c == 0:
                        sp.wait_ge(const_in, 48)
                        sp.wait_ge(mt_taken, i)
                        sp.dma_start(m_d[bass.ds(i - 1, 1)].rearrange("a m q -> (a m) q"), m_t[:]).then_inc(m_stored, 16)
                        stored, ob_out = value(sp, 16 * i), value(sp, 16 * i - 16)
                        sp.wait_ge(const_in, 48)
                        sp.wait_ge(m_stored, stored)
                        if not isinstance(i, int) or i > 1:
                            sp.wait_ge(ob_stored, ob_out)
                        sp.dma_start(m_rows[:], m_d[bass.ds(i - 1, 1)].rearrange("a (h g b) q -> (a h) g (b q)", h=2, g=GROUPS)).then_inc(m_loaded, 16)
                    if cur and 1 <= c <= 6:
                        taken, rotated = value(sp, n), value(sp, i * 6 + c - 1)
                        sp.wait_ge(const_in, 48)
                        for s in range(2):
                            sp.wait_ge(z_taken[s], taken)
                        if c > 1 or not first(i):
                            sp.wait_ge(rope_sum, rotated)
                        for q in range(4):
                            o = q ^ 1
                            sp.dma_start(z_swap[32 * q:32 * q + 32, :], zz[(c - 1) % 2][32 * o:32 * o + 32, :]).then_inc(swapped, 16)
                    if prev and c == 8:
                        done = value(sp, 2 * i)
                        sp.wait_ge(const_in, 48)
                        sp.wait_ge(ob_done, done)
                        sp.dma_start(o_b_d[bass.ds(i - 1, 1)].rearrange("a p t -> (a p) t"), o_b[:]).then_inc(ob_stored, 16)

            attention(0, False, True)
            with sp.Fori(1, PAIRS - 1) as i:
                attention(i, True, True)
            attention(PAIRS - 1, True, True)
            attention(PAIRS, True, False)

            sp.wait_ge(ob_stored, 16 * PAIRS)
            for t in range(HEADS + PAIRS):
                if t >= 2:
                    sp.wait_ge(br_lo_done, t - 1)
                src = o_a_d[t] if t < HEADS else o_b_d[t - HEADS]
                sp.dma_start(g_in[t % 2][:], src).then_inc(br_loaded[t % 2], 16)
            sp.wait_ge(br_lo_done, HEADS + PAIRS)
            for j in range(KT):
                n = N_IN + 2 * j
                for c in range(2):
                    if j:
                        sp.wait_ge(mg_sum, j)
                    sp.dma_start(g_in[c][:], gate_d[c, j]).then_inc(g_loaded[c], 16)
                    sp.wait_ge(w_lo_done, n + c + 1)
                    load_stage(n + c + 2, c)
            for c in range(6):
                sp.wait_ge(w_lo_done, N_IN + 16 + c + 1)
                load_stage(N_IN + 16 + c + 2, c % 2)
                if c == 0:
                    sp.wait_ge(z_made[1], N_IN + 16)
                    for t in range(NB):
                        sp.dma_start(yy[:, t, :], d["x"][P * t:P * (t + 1), :]).then_inc(y_loaded[t], 16)
                    sp.wait_ge(mg_lo_done, KT)
                    sp.dma_start(fnw[:], d["final_norm_w"].to_broadcast([P, D_MODEL])).then_inc(fnw_loaded, 16)
            for t in range(NB):
                sp.wait_ge(out_done, t + 1)
                sp.dma_start(out[P * t:P * (t + 1), :], yy[:, t, :]).then_inc(out_stored, 16)
            sp.wait_ge(out_stored, 16 * NB)

        @block.gpsimd
        def _(pool):
            pool.wait_ge(const_in, 11 * 16)
            for m in range(8):
                src = vt[:, P * m:P * (m + 1)].rearrange("p (a c) -> p a c", a=1).to_broadcast([P, 4, P])
                nc.gpsimd.tensor_copy(level_mask[:, m, :].rearrange("p (a c) -> p a c", c=P), src).then_inc(mask_done, 1)

        @block.tensor
        def _(pe):
            pe.wait_ge(const_in, 48)
            for k in range(KT):
                for hf in range(2):
                    u = 2 * k + hf
                    if k == 0:
                        pe.wait_ge(xn_done, 4 * hf + 4)
                    if u >= 4:
                        pe.wait_ge(h_lo_done, u - 3)
                    dst = (pa, pb)[k % 2]
                    for t in range(4):
                        last = nc.tensor.transpose(dst[:, hf, P * t:P * (t + 1)],
                                                   x_in[:, 4 * hf + t, P * k:P * (k + 1)], ident[:])
                    last.then_inc(xt_made, 1)

            def project(n, s, hf):
                if hf == 0:
                    pe.wait_ge(w_lo_done, n + 1)
                if not (isinstance(n, int) and n == 0):
                    pe.wait_ge(z_taken[hf], n)
                t = slice(HALF * hf, HALF * (hf + 1))
                for k in range(KT):
                    nc.tensor.matmul(z_ps[hf][:], w_hi[s][:, k, :], h_hi[:, k, t], start=k == 0, stop=False)
                    nc.tensor.matmul(z_ps[hf][:], w_hi[s][:, k, :], h_lo[:, k, t], start=False, stop=False)
                    last = nc.tensor.matmul(z_ps[hf][:], w_lo[s][:, k, :], h_hi[:, k, t], start=False, stop=k == KT - 1)
                last.then_inc(z_made[hf], 1)

            def level_product(i, j):
                dst = pb[:, j % 2, :]
                if j >= 2:
                    pe.wait_ge(lvl_taken, i * 9 + (j - 1))
                elif not isinstance(i, int) or i > 0:
                    pe.wait_ge(lvl_taken, i * 9 + (0 if j == 0 else -1))
                if j == 0:
                    pe.wait_ge(q_one_done, i + 1)
                    for c in range(NB):
                        last = nc.tensor.matmul(dst[:, 64 * c:64 * c + 64], kk[:, P * c:P * c + P], q_one[:, 64 * c:64 * c + 64], start=True, stop=True)
                elif j <= 2:
                    for c in range(4):
                        b = slice(P * (4 * (j - 1) + c), P * (4 * (j - 1) + c + 1))
                        last = nc.tensor.matmul(dst[:, P * c:P * c + P], kk[:, b], qq[:, b], start=True, stop=True)
                else:
                    u = j - 3
                    pe.wait_ge(lv_done, i * 6 + u + 1)
                    for c in range(NB):
                        last = nc.tensor.matmul(dst[:, 64 * c:64 * c + 64], k_lv[u % 2][:, P * c:P * c + P], q_lv[u % 2][:, 64 * c:64 * c + 64], start=True, stop=True)
                last.then_inc(lvl_made, 1)

            def hgrn_cur(i, slot):
                if slot == 5:
                    pe.wait_ge(k_out_done, i + 1)
                    if not isinstance(i, int) or i > 0:
                        pe.wait_ge(ms_ln, i * 2)
                    for c in range(NB):
                        last = nc.tensor.transpose(pa[:, c // 4, P * (c % 4):P * (c % 4 + 1)], k_out[:, P * c:P * c + P], ident[:])
                    last.then_inc(kt_made, 1)
                    level_product(i, 0)
                    level_product(i, 1)
                elif slot == 6:
                    level_product(i, 2)
                    level_product(i, 3)
                elif slot >= 7:
                    level_product(i, slot - 3)
                if slot == 7:
                    pe.wait_ge(kt_taken, i * 2 + 2)
                    for s in range(2):
                        pe.wait_ge(z_taken[s], i * HG_CHUNKS + 3)
                    for c in range(NB):
                        last = nc.tensor.transpose(pa[:, c // 4, P * (c % 4):P * (c % 4 + 1)], vt[:, P * c:P * c + P], ident[:])
                    last.then_inc(vt_made, 1)
                if slot == 9:
                    pe.wait_ge(v_taken, i * 2 + 2)
                    if not isinstance(i, int) or i > 0:
                        pe.wait_ge(on_done, i)
                    for c in range(NB - 1):
                        last = nc.tensor.matmul(pc[:, c // 4, P * (c % 4):P * (c % 4 + 1)], k_tok[:, c, :], vv[:, c, :], start=True, stop=True)
                    last.then_inc(upd_made, 1)

            def hgrn_tail(i, slot):
                if slot == 1:
                    pe.wait_ge(lvl_taken, i * 9)
                    pe.wait_ge(s_done, i * 7)
                    for c in range(NB):
                        o = pc[:, c // 4, P * (c % 4):P * (c % 4 + 1)]
                        last = nc.tensor.matmul(o, vv[:, c, :], scores[:, c, :], start=True, stop=c == 0)
                        if c:
                            last = nc.tensor.matmul(o, state[:, c, :], q_in[:, P * c:P * c + P], start=False, stop=True)
                    last.then_inc(pv_made, 1)
                if slot == 3:
                    pe.wait_ge(sq_done, i * 2)
                    for hf in range(2):
                        last = nc.tensor.matmul(pa[:, hf, :], inv128[:], o_sq[:, HALF * hf:HALF * (hf + 1)], start=True, stop=True)
                    last.then_inc(ms_made, 1)

            pe.wait_ge(h_lo_done, 2 * KT)
            pe.wait_ge(init_done, 4)

            def hgrn(i, prev, cur):
                for slot in range(2 * HG_CHUNKS):
                    if cur:
                        project(i * HG_CHUNKS + slot // 2, slot // 2 % 2, slot % 2)
                        hgrn_cur(i, slot)
                    if prev:
                        hgrn_tail(i, slot)

            hgrn(0, False, True)
            with pe.Fori(1, HEADS) as i:
                hgrn(i, True, True)
            hgrn(HEADS, True, False)

            def maxima(i, g, m, h):
                u = 2 * (g * 4 + m) + h
                rows = slice(EDIM * h, EDIM * (h + 1))
                if u >= 2:
                    pe.wait_ge(mx_taken, i * N_MAX + max_count(u - 1))
                elif not first(i):
                    pe.wait_ge(mx_taken, i * N_MAX)
                pe.wait_ge(qk_hi_done, i * 6 + 2 * g + 2)
                for blk, at, before in max_queries(g, m):
                    lo = blk - 1 if before else blk
                    at += 0 if before or g == 2 else P
                    last = nc.tensor.matmul(pa[:, h, at:at + P * (blk + 1 - lo)], qk_hi[g][0][rows, P * blk:P * blk + P],
                                            qk_hi[g][1][rows, P * lo:P * blk + P], start=True, stop=True)
                last.then_inc(mx_made, 1)

            def scores_t(i, u):
                g, h, m = UNITS[u]
                rows = slice(EDIM * h, EDIM * (h + 1))
                base = (i - 1) * N_UNITS
                if u == 0:
                    pe.wait_ge(shift_done, i)
                if u >= 2:
                    pe.wait_ge(pt_done, base + u - 1)
                pe.wait_ge(qk_lo_done, i * 6)
                for blk, at, n in unit_keys(g, m):
                    dst = pb[:, u % 2, at:at + P * n]
                    ks, qs = slice(P * blk, P * blk + P), slice(P * blk, P * (blk + n))
                    nc.tensor.matmul(dst, qk_hi[g][1][rows, ks], qk_hi[g][0][rows, qs], start=True, stop=False)
                    nc.tensor.matmul(dst, qk_hi[g][1][rows, ks], qk_lo[g][0][rows, qs], start=False, stop=False)
                    nc.tensor.matmul(dst, qk_lo[g][1][rows, ks], qk_hi[g][0][rows, qs], start=False, stop=False)
                    mask = mask_b[:, 0:P * n] if g < 2 else mask_b[:, 2 * P:3 * P]
                    nc.tensor.matmul(dst, ident_b[:], mask, start=False, stop=False)
                    if g == 0:
                        row = shift[:, qs]
                    elif g == 1:
                        row = shift[:].rearrange("p (n i r) -> p n r i", n=2, r=4)[:, blk % 2:blk % 2 + n, blk // 2, :]
                    else:
                        row = shift[:].rearrange("p (i r) -> p r i", r=16)[:, 2 * blk:2 * blk + 2, :]
                    last = nc.tensor.matmul(dst, sel[:, h, :], row, start=False, stop=True)
                last.then_inc(st_made, 1)

            def weighted(i, u):
                g, h, m = UNITS[u]
                pe.wait_ge(pt_done, (i - 1) * N_UNITS + u + 1)
                made = (i - 1) * N_SUMS
                for blk, at, n in unit_keys(g, m):
                    for q in range(n):
                        bank = (blk + q) // 4
                        opens = (blk + q) % 4 == 0 and q == (1 if g == 0 and blk else 0)
                        closes = (blk + q) % 4 == 3 and q == 0
                        if opens:
                            k = (2 * g + h) * 2 + bank
                            if k >= 2:
                                pe.wait_ge(ob_taken, made + k - 1)
                        last = nc.tensor.matmul(pc[:, bank, P * ((blk + q) % 4):P * ((blk + q) % 4 + 1)], vb[:, g, blk, EDIM * h:EDIM * h + P],
                                                pt[u % 2][:, at + P * q:at + P * q + P], start=opens, stop=closes)
                last.then_inc(pu_made, 1)

            def attention(i, prev, cur):
                for slot in range(2 * AT_CHUNKS):
                    c = slot // 2
                    if cur:
                        project(N_HG + i * AT_CHUNKS + c, c % 2, slot % 2)
                    if prev:
                        for u in UNIT_SLOTS.get(slot, ()):
                            scores_t(i, u)
                            if u:
                                weighted(i, u - 1)
                        if slot == 11:
                            weighted(i, N_UNITS - 1)
                    if cur and slot in MAX_SLOTS:
                        for h in range(2):
                            maxima(i, *MAX_SLOTS[slot], h)
                    if cur and slot in (14, 16, 18):
                        g = (slot - 14) // 2
                        for s in range(2):
                            pe.wait_ge(z_taken[s], N_HG + i * AT_CHUNKS + 7 + g)
                        if g:
                            pe.wait_ge(av_taken, i * 6 + 2 * g)
                        for b in range(NB):
                            last = nc.tensor.transpose(pb[:, b // 4, P * (b % 4):P * (b % 4 + 1)], v_t[:, P * b:P * b + P], ident[:])
                        last.then_inc(avt_made, 1)
                    if cur and slot == 18:
                        maxed, summed = value(pe, i * N_MAX + N_MAX), value(pe, i * N_SUMS)
                        pe.wait_ge(const_in, 48)
                        pe.wait_ge(mx_taken, maxed)
                        if prev:
                            pe.wait_ge(ob_taken, summed)
                        nc.tensor.transpose(pc[0:2 * GROUPS * NB, 0, 0:P], m_all[:], ident[:]).then_inc(mt_made, 1)

            pe.wait_ge(on_done, HEADS)
            attention(0, False, True)
            with pe.Fori(1, PAIRS - 1) as i:
                attention(i, True, True)
            attention(PAIRS - 1, True, True)
            attention(PAIRS, True, False)

            for j in range(KT):
                for b in range(2):
                    n = N_IN + 2 * j + b
                    src_hi, src_lo = (oa_hi, oa_lo) if b == 0 else (ob_hi, ob_lo)
                    kt = HEADS if b == 0 else PAIRS
                    pe.wait_ge(br_lo_done, HEADS + PAIRS * b)
                    pe.wait_ge(w_lo_done, n + 1)
                    for hf in range(2):
                        pe.wait_ge(z_taken[hf], n)
                        t = slice(HALF * hf, HALF * (hf + 1))
                        dst = z_ps[hf][:] if b == 0 else pc[:, hf, :]
                        for k in range(kt):
                            nc.tensor.matmul(dst, w_hi[b][:, k, :], src_hi[:, k, t], start=k == 0, stop=False)
                            nc.tensor.matmul(dst, w_hi[b][:, k, :], src_lo[:, k, t], start=False, stop=False)
                            last = nc.tensor.matmul(dst, w_lo[b][:, k, :], src_hi[:, k, t], start=False, stop=k == kt - 1)
                        last.then_inc(z_made[hf], 1)

            def out_product(dst, t, w_h, w_l, cols):
                tt = slice(P * t, P * t + P)
                for k in range(KT):
                    nc.tensor.matmul(dst, mg_hi[:, k, tt], w_h[:, k, cols], start=k == 0, stop=False)
                    nc.tensor.matmul(dst, mg_hi[:, k, tt], w_l[:, k, cols], start=False, stop=False)
                    last = nc.tensor.matmul(dst, mg_lo[:, k, tt], w_h[:, k, cols], start=False, stop=k == KT - 1)
                return last

            pe.wait_ge(mg_lo_done, KT)
            pe.wait_ge(w_lo_done, N_IN + 18)
            for t in range(NB):
                if t >= 2:
                    pe.wait_ge(qa_taken, t - 1)
                out_product(z_ps[t % 2][:, 0:2 * P], t, wq_hi, wq_lo, slice(0, 2 * P)).then_inc(qa_made, 1)
            pe.wait_ge(w_lo_done, N_IN + 24)
            for t in range(NB):
                dst = (pa, pb)[t % 2]
                if t >= 2:
                    pe.wait_ge(pb_taken, 2 * t - 2)
                out_product(dst[:, 0, :], t, oa_hi, oa_lo, slice(2 * P, 6 * P)).then_inc(pb_made, 1)
                out_product(dst[:, 1, 0:2 * P], t, oa_hi, oa_lo, slice(6 * P, 8 * P)).then_inc(pb_made, 1)

        @block.scalar
        def _(act):
            act.wait_ge(const_in, 48)
            for t in range(NB):
                act.wait_ge(x_loaded[t], 16)
                if t:
                    act.wait_ge(ss_done, t)
                nc.scalar.activation(x_sq[:], x_in[:, t, :], ACT.Square, accum_out=x_ss[:, t:t + 1]).then_inc(ss_done, 1)
                act.wait_ge(ss_done, t + 1)
                nc.scalar.activation(x_ln[:, t:t + 1], x_ss[:, t:t + 1], ACT.Ln, scale=1.0 / D_MODEL, bias=col[:, 2:3]).then_inc(rs_ln_done, 1)
                act.wait_ge(rs_ln_done, t + 1)
                nc.scalar.activation(x_rs[:, t:t + 1], x_ln[:, t:t + 1], ACT.Exp, scale=-0.5).then_inc(rs_done, 1)
            for u in range(2 * KT):
                k, hf = u // 2, u % 2
                act.wait_ge(xt_made, u + 1)
                nc.scalar.activation(h_hi[:, k, HALF * hf:HALF * (hf + 1)], (pa, pb)[k % 2][:, hf, :], ACT.Copy,
                                     scale=norm_w[:, k:k + 1]).then_inc(h_hi_done, 1)

            def split_hi(n, s):
                if not isinstance(n, int) or n >= 2:
                    act.wait_ge(z_made[1], n - 1)
                act.wait_ge(w_loaded[s], w_count(n, s))
                nc.scalar.activation(w_hi[s][:], w_stage[s][:], ACT.Copy).then_inc(w_hi_done, 1)

            def w_count(n, s):
                return 16 * (n // 2 + 1) if isinstance(n, int) else (n - s) * 8 + 16

            def take(n, hf, dst, func, **kw):
                act.wait_ge(z_made[hf], n + 1)
                nc.scalar.activation(dst[:, HALF * hf:HALF * (hf + 1)], z_ps[hf][:], func, **kw).then_inc(z_taken[hf], 1)

            split_hi(0, 0)
            act.wait_ge(rope_step, 15)
            nc.scalar.activation(cos_t[:], dd[1][:], ACT.Sin).then_inc(sin_done, 1)
            nc.scalar.activation(sin_t[:], dd[0][:], ACT.Sin).then_inc(sin_done, 1)
            act.wait_ge(lb_step, 3)
            nc.scalar.activation(lb[:, 1:3, :], lb[:, 1:3, :], ACT.Exp).then_inc(lb_step, 1)

            def level_exp(i, u):
                act.wait_ge(d_done, i * 7 + u + 1)
                nc.scalar.activation(ee[u % 2][:], dd[u % 2][:], ACT.Exp).then_inc(e_done, 1)

            def hgrn_cur(i, slot):
                if slot == 2:
                    act.wait_ge(f_done, i + 1)
                    nc.scalar.activation(lf[:], ff[:], ACT.Ln).then_inc(ln_done, 1)
                if slot == 3:
                    act.wait_ge(b_done, i + 1)
                    nc.scalar.activation(eb[:], bb[:], ACT.Exp).then_inc(eb_done, 1)
                if 4 <= slot <= 10:
                    level_exp(i, slot - 4)
                if slot == 6:
                    act.wait_ge(kt_made, i + 1)
                    for hf in range(2):
                        nc.scalar.activation(k_tok[:, 4 * hf:4 * hf + 4, :], pa[:, hf, :].rearrange("p (c k) -> p c k", k=P), ACT.Copy).then_inc(kt_taken, 1)
                if slot == 8:
                    act.wait_ge(vt_made, i + 1)
                    for hf in range(2):
                        nc.scalar.activation(vv[:, 4 * hf:4 * hf + 4, :], pa[:, hf, :].rearrange("p (c k) -> p c k", k=P), ACT.Copy).then_inc(v_taken, 1)

            def hgrn_tail(i, slot):
                if slot == 2:
                    act.wait_ge(pv_made, i)
                    for hf in range(2):
                        nc.scalar.activation(o_sq[:, HALF * hf:HALF * (hf + 1)], pc[:, hf, :], ACT.Square).then_inc(sq_done, 1)
                if slot == 4:
                    act.wait_ge(ms_made, i)
                    for hf in range(2):
                        nc.scalar.activation(o_rs[:, HALF * hf:HALF * (hf + 1)], pa[:, hf, :], ACT.Ln, bias=col[:, 2:3]).then_inc(ms_ln, 1)
                    act.wait_ge(ms_ln, i * 2)
                    nc.scalar.activation(o_rs[:], o_rs[:], ACT.Exp, scale=-0.5).then_inc(ors_done, 1)

            evacs = ((ff, ACT.Sigmoid), (qq, ACT.Silu), (vt, ACT.Copy), (gg, ACT.Silu), (gate[0], ACT.Sigmoid), (gate[1], ACT.Sigmoid))

            def hgrn(i, prev, cur):
                for slot in range(2 * HG_CHUNKS):
                    c, hf = slot // 2, slot % 2
                    if cur and hf == 0:
                        split_hi(i * HG_CHUNKS + c + 1, (c + 1) % 2)
                    if prev:
                        hgrn_tail(i, slot)
                    if cur:
                        hgrn_cur(i, slot)
                        if slot == 6 and prev:
                            act.wait_ge(oa_done, i)
                        if c >= 4 and hf == 0 and prev:
                            act.wait_ge(gate_stored[c - 4], 16 * i)
                        take(i * HG_CHUNKS + c, hf, *evacs[c])

            hgrn(0, False, True)
            with act.Fori(1, HEADS) as i:
                hgrn(i, True, True)
            hgrn(HEADS, True, False)

            def attention(i, prev, cur):
                for slot in range(2 * AT_CHUNKS):
                    c, hf = slot // 2, slot % 2
                    n = N_HG + i * AT_CHUNKS + c
                    if cur and hf == 0:
                        split_hi(n + 1, (c + 1) % 2)
                    if cur and slot >= 5 and hf == 1 and slot <= 15:
                        j = (slot - 5) // 2
                        act.wait_ge(rope_sum, i * 6 + j + 1)
                        if prev:
                            act.wait_ge(st_made, (i - 1) * N_UNITS + (8, 16, 20)[j // 2])
                        nc.scalar.activation(qk_hi[j // 2][j % 2][:], roped[:], ACT.Copy).then_inc(qk_hi_done, 1)
                    if cur and slot in (15, 17, 19):
                        g = (slot - 15) // 2
                        act.wait_ge(avt_made, i * 3 + g + 1)
                        for b in range(2):
                            dst = vb[:, g, 4 * b:4 * b + 4, :].rearrange("p c (x e) -> p c x e", e=EDIM)[:, :, 0:3:2, :]
                            nc.scalar.activation(dst, pb[:, b, :].rearrange("p (c x e) -> p c x e", c=4, x=2), ACT.Copy).then_inc(av_taken, 1)
                    if prev and slot == 13:
                        act.wait_ge(ob_taken, i * N_SUMS)
                        nc.scalar.activation(r_den[0:EDIM, :], acc[0][EDIM:P, :], ACT.Ln).then_inc(den_ln, 1)
                        nc.scalar.activation(r_den[EDIM:P, :], acc[1][0:EDIM, :], ACT.Ln).then_inc(den_ln, 1)
                        act.wait_ge(den_ln, 2 * i)
                        nc.scalar.activation(r_den[:], r_den[:], ACT.Exp, scale=-1.0).then_inc(den_done, 1)
                    if cur:
                        if c < 6:
                            if not first(i) or c >= 2:
                                act.wait_ge(rope_sum, i * 6 + c - 1)
                            take(n, hf, zz[c % 2], ACT.Copy, scale=0.125 if c % 2 == 0 else 1.0)
                        elif c < 9:
                            g = c - 6
                            act.wait_ge(z_made[hf], n + 1)
                            if hf == 0 and (g or prev):
                                act.wait_ge(avt_made, i * 3 + g)
                            if g == 0 and hf == 0 and prev:
                                act.wait_ge(shift_done, i)
                            r = DILATIONS[g]
                            w = HALF // r
                            dst = v_t[:].rearrange("p (r i) -> p r i", r=r)[:, :, w * hf:w * (hf + 1)]
                            nc.scalar.activation(dst, z_ps[hf][:].rearrange("p (i r) -> p r i", r=r), ACT.Copy).then_inc(z_taken[hf], 1)
                        else:
                            if prev and hf == 0:
                                act.wait_ge(ob_done, 2 * i)
                            take(n, hf, s_ag, ACT.Silu)
                    if prev:
                        for u in UNIT_SLOTS.get(slot, ()):
                            act.wait_ge(st_made, (i - 1) * N_UNITS + u + 1)
                            cols = sum(P * k for _, _, k in unit_keys(UNITS[u][0], UNITS[u][2]))
                            if u >= 2:
                                act.wait_ge(pu_made, (i - 1) * N_UNITS + u - 1)
                            nc.scalar.activation(pt[u % 2][:, 0:cols], pb[:, u % 2, 0:cols], ACT.Exp).then_inc(pt_done, 1)
                    if cur and slot == 19:
                        act.wait_ge(mt_made, i + 1)
                        if prev:
                            act.wait_ge(m_stored, 16 * i)
                        nc.scalar.activation(m_t[:], pc[0:2 * GROUPS * NB, 0, 0:P], ACT.Copy, scale=-1.0).then_inc(mt_taken, 1)

            act.wait_ge(oa_stored, 16 * HEADS)
            for s in range(2):
                act.wait_ge(gate_stored[s], 16 * HEADS)
            act.wait_ge(vb_done, 1)
            attention(0, False, True)
            with act.Fori(1, PAIRS - 1) as i:
                attention(i, True, True)
            attention(PAIRS - 1, True, True)
            attention(PAIRS, True, False)

            for t in range(HEADS + PAIRS):
                act.wait_ge(br_loaded[t % 2], 16 * (t // 2 + 1))
                dst = oa_hi[:, t, :] if t < HEADS else ob_hi[:, t - HEADS, :]
                nc.scalar.activation(dst, g_in[t % 2][:], ACT.Copy).then_inc(br_hi_done, 1)

            def split_out_hi(n):
                c = n - N_IN - 16
                act.wait_ge(w_loaded[n % 2], w_count(n, n % 2))
                if c == 2:
                    act.wait_ge(z_made[1], N_IN + 16)
                dst = wq_hi if c < 2 else oa_hi
                nc.scalar.activation(dst[:, :, P * c:P * c + P], w_stage[n % 2][:], ACT.Copy).then_inc(w_hi_done, 1)

            for j in range(KT):
                for b in range(2):
                    n = N_IN + 2 * j + b + 1
                    if n < N_IN + 16:
                        kt = HEADS if n % 2 == 0 else PAIRS
                        act.wait_ge(z_made[1], n - 1)
                        act.wait_ge(w_loaded[n % 2], w_count(n, n % 2))
                        nc.scalar.activation(w_hi[n % 2][:, 0:kt, :], w_stage[n % 2][:, 0:kt, :], ACT.Copy).then_inc(w_hi_done, 1)
                    else:
                        split_out_hi(n)
                act.wait_ge(mg_sum, j + 1)
                nc.scalar.activation(mg_hi[:, j, :], part[:], ACT.Copy).then_inc(mg_hi_done, 1)
            for c in range(1, 8):
                split_out_hi(N_IN + 16 + c)
            for t in range(NB):
                act.wait_ge(pb_taken, 2 * t + 2)
                nc.scalar.activation(g_in[0][:], yy[:, t, :], ACT.Square, accum_out=o_stat[:, 0, t:t + 1]).then_inc(oss_done, 1)
                act.wait_ge(oss_done, t + 1)
                nc.scalar.activation(o_stat[:, 1, t:t + 1], o_stat[:, 0, t:t + 1], ACT.Ln, scale=1.0 / D_MODEL, bias=col[:, 2:3]).then_inc(oln_done, 1)
                act.wait_ge(oln_done, t + 1)
                nc.scalar.activation(o_stat[:, 2, t:t + 1], o_stat[:, 1, t:t + 1], ACT.Exp, scale=-0.5).then_inc(ors2_done, 1)

        @block.vector
        def _(dve):
            for t in range(NB):
                dve.wait_ge(rs_done, t + 1)
                nc.vector.tensor_scalar(x_in[:, t, :], x_in[:, t, :], x_rs[:, t:t + 1], None, ALU.mult).then_inc(xn_done, 1)
            for u in range(2 * KT):
                k, hf = u // 2, u % 2
                dve.wait_ge(h_hi_done, u + 1)
                t = slice(HALF * hf, HALF * (hf + 1))
                nc.vector.scalar_tensor_tensor(h_lo[:, k, t], (pa, pb)[k % 2][:, hf, :], norm_w[:, k:k + 1],
                                               h_hi[:, k, t].bitcast(f32), ALU.mult, ALU.subtract).then_inc(h_lo_done, 1)

            def split_lo(n, s):
                dve.wait_ge(w_hi_done, n + 1)
                nc.vector.tensor_tensor(w_lo[s][:], w_stage[s][:], w_hi[s][:].bitcast(f32), ALU.subtract).then_inc(w_lo_done, 1)

            split_lo(0, 0)
            nc.vector.memset(k_lv[0][:], 0.0).then_inc(init_done, 1)
            nc.vector.memset(k_lv[1][:], 0.0).then_inc(init_done, 1)
            nc.vector.memset(scores[:], 0.0).then_inc(init_done, 1)
            dve.wait_ge(const_in, 11 * 16)

            def link(ins):
                steps[0] += 1
                ins.then_inc(rope_step, 1)
                dve.wait_ge(rope_step, steps[0])

            steps = [0]
            two_pi = 2 * np.pi
            parts = [6.28125, float(np.float32(np.floor((two_pi - 6.28125) * 2 ** 20) / 2 ** 20))]
            parts.append(float(np.float32(two_pi - parts[0] - parts[1])))
            magic = 1.5 * 2 ** 23
            lim = float(np.nextafter(np.float32(np.pi), np.float32(0)))
            link(nc.vector.tensor_copy(ee[1][:], lf[:].bitcast(i32)))
            link(nc.vector.tensor_scalar(ee[1][:], ee[1][:], col[:, 0:1], None, ALU.mult))
            for s in range(2):
                link(nc.vector.tensor_scalar(ee[0][:], ee[1][:], 1.0 / two_pi, 0.25 * s, ALU.mult, ALU.add))
                link(nc.vector.tensor_scalar(ee[0][:], ee[0][:], magic, magic, ALU.add, ALU.subtract))
                link(nc.vector.scalar_tensor_tensor(dd[s][:], ee[0][:], -parts[0], ee[1][:], ALU.mult, ALU.add))
                link(nc.vector.scalar_tensor_tensor(dd[s][:], ee[0][:], -parts[1], dd[s][:], ALU.mult, ALU.add))
                link(nc.vector.scalar_tensor_tensor(dd[s][:], ee[0][:], -parts[2], dd[s][:], ALU.mult, ALU.add))
                if s:
                    link(nc.vector.tensor_scalar(dd[s][:], dd[s][:], float(np.pi / 2), None, ALU.add))
                link(nc.vector.tensor_scalar(dd[s][:], dd[s][:], lim, -lim, ALU.min, ALU.max))
            dve.wait_ge(sin_done, 2)
            nc.vector.tensor_scalar(sin_t[:], sin_t[:], col[:, 1:2], None, ALU.mult).then_inc(rope_step, 1)
            nc.vector.tensor_copy(mask_b[:], bb[:, 0:4 * P]).then_inc(rope_step, 1)
            nc.vector.tensor_copy(ident_b[:], ident[:]).then_inc(rope_step, 1)
            nc.vector.tensor_copy(sel[:], qq[0:2, 0:2 * P].rearrange("p (a b) -> p a b", a=2)).then_inc(rope_step, 1)
            dve.wait_ge(rope_step, 19)
            nc.vector.tensor_scalar(inv128[:], reset[:, 0:P], 0.0, 1.0 / P, ALU.mult, ALU.add).then_inc(init_done, 1)
            dve.wait_ge(init_done, 4)
            nc.vector.tensor_tensor(lb[:, 0, :], lb_in[:, 0, :], lb_in[:, 1, :], ALU.max).then_inc(lb_step, 1)
            dve.wait_ge(lb_step, 1)
            for r in range(2):
                nc.vector.tensor_tensor(lb[:, 1 + r, :], lb_in[:, r, :], lb[:, 0, :], ALU.subtract).then_inc(lb_step, 1)
            dve.wait_ge(lb_step, 4)
            nc.vector.tensor_tensor(lb[:, 3, :], lb[:, 1, :], lb[:, 2, :], ALU.add).then_inc(lb_step, 1)
            dve.wait_ge(lb_step, 5)
            nc.vector.reciprocal(lb[:, 3, :], lb[:, 3, :]).then_inc(lb_step, 1)
            dve.wait_ge(lb_step, 6)
            nc.vector.tensor_tensor(lb[:, 4, :], lb[:, 1, :], lb[:, 3, :], ALU.mult).then_inc(lb_step, 1)
            dve.wait_ge(lb_step, 7)
            nc.vector.tensor_scalar(lb[:, 5, :], lb[:, 4, :], -1.0, 1.0, ALU.mult, ALU.add).then_inc(lb_step, 1)
            dve.wait_ge(lb_step, 8)
            nc.vector.tensor_scalar(lb[:, 4, :], lb[:, 4, :], TINY, None, ALU.max).then_inc(lb_step, 1)
            dve.wait_ge(lb_step, 9)
            dve.wait_ge(mask_done, 8)

            def exponents(i, u):
                if u == 0:
                    b = bb[:].rearrange("p (c t) -> p c t", t=P)
                    nc.vector.tensor_tensor(dd[0][:].rearrange("p (c t) -> p c t", t=P), b[:, :, P - 1:P].to_broadcast([P, NB, P]), b, ALU.subtract).then_inc(d_done, 1)
                    return
                span = LEVELS[u - 1]
                n = HALF // span
                b = bb[:].rearrange("p (n two l) -> p n two l", two=2, l=span)
                mid = b[:, :, 0, span - 1:span].to_broadcast([P, n, span])
                dst = dd[u % 2][:].rearrange("p (two n l) -> p two n l", two=2, l=span)
                nc.vector.tensor_tensor(dst[:, 0], b[:, :, 1, :], mid, ALU.subtract)
                nc.vector.tensor_tensor(dst[:, 1], mid, b[:, :, 0, :], ALU.subtract).then_inc(d_done, 1)

            def level_factors(i, u):
                dve.wait_ge(e_done, i * 7 + u + 1)
                if u == 0:
                    nc.vector.tensor_tensor(k_out[:], kk[:], ee[0][:], ALU.mult).then_inc(k_out_done, 1)
                    return
                span = LEVELS[u - 1]
                s = (u - 1) % 2
                if u >= 3:
                    dve.wait_ge(lvl_made, i * 9 + u + 1)
                e = ee[u % 2][:].rearrange("p (two n l) -> p two n l", two=2, l=span)
                cut = lambda t: t[:].rearrange("p (n two l) -> p n two l", two=2, l=span)
                nc.vector.tensor_tensor(q_lv[s][:].rearrange("p (n l) -> p n l", l=span), cut(qq)[:, :, 1, :], e[:, 0], ALU.mult)
                nc.vector.tensor_tensor(cut(k_lv[s])[:, :, 0, :], cut(kk)[:, :, 0, :], e[:, 1], ALU.mult).then_inc(lv_done, 1)

            def pick(i, j):
                made, taken = value(dve, i * 9 + j + 1), value(dve, i * 9 + j)
                if j in (1, 2):
                    dst, m = scores[:, 4 * (j - 1):4 * j, :], 1
                    src = pb[:, j % 2, :].rearrange("p (c t) -> p c t", t=P)
                    mask = level_mask[:, 1, :].rearrange("p (c t) -> p c t", t=P)
                else:
                    span = 1 if j == 0 else LEVELS[j - 3]
                    m = 0 if j == 0 else j - 1
                    dst = scores[:].rearrange("p c t -> p (c t)").rearrange("p (n two l) -> p n two l", two=2, l=span)[:, :, 1, :]
                    src = pb[:, j % 2, :].rearrange("p (n l) -> p n l", l=span)
                    mask = level_mask[:, m, :].rearrange("p (n l) -> p n l", l=span)
                dve.wait_ge(mask_done, 8)
                dve.wait_ge(lvl_made, made)
                if not isinstance(i, int) or i * 9 + j > 0:
                    dve.wait_ge(lvl_taken, taken)
                nc.vector.copy_predicated(dst, mask, src).then_inc(lvl_taken, 1)

            def hgrn_cur(i, slot):
                if slot == 2:
                    for s in range(2):
                        dve.wait_ge(z_taken[s], i * HG_CHUNKS + 1)
                    head = bass.ds(i, 1)
                    nc.vector.tensor_scalar(ff[:], ff[:], lb[:, 5, head], lb[:, 4, head], ALU.mult, ALU.add).then_inc(f_done, 1)
                    dve.wait_ge(f_done, i + 1)
                    nc.vector.tensor_scalar(kk[:], ff[:], -1.0, 1.0, ALU.mult, ALU.add).then_inc(k_done, 1)
                    dve.wait_ge(ln_done, i + 1)
                    nc.vector.tensor_tensor_scan(bb[:], reset[:], lf[:], 0.0, ALU.mult, ALU.add).then_inc(b_done, 1)
                    dve.wait_ge(b_done, i + 1)
                if slot == 4:
                    for s in range(2):
                        dve.wait_ge(z_taken[s], i * HG_CHUNKS + 2)
                    if not isinstance(i, int) or i > 0:
                        dve.wait_ge(pv_made, i)
                    odd = lambda t: t[:].rearrange("p (n two) -> p n two", two=2)[:, :, 1]
                    nc.vector.tensor_tensor(q_one[:], odd(qq), odd(ff), ALU.mult).then_inc(q_one_done, 1)
                    dve.wait_ge(eb_done, i + 1)
                    nc.vector.tensor_tensor(q_in[:], qq[:], eb[:], ALU.mult).then_inc(q_in_done, 1)
                if 4 <= slot <= 10:
                    level_factors(i, slot - 4)
                if 3 <= slot <= 9:
                    exponents(i, slot - 3)
                if slot in (6, 7):
                    pick(i, 2 * (slot - 6))
                    pick(i, 2 * (slot - 6) + 1)
                elif slot >= 8:
                    pick(i, slot - 4)
                if slot == 10:
                    dve.wait_ge(upd_made, i + 1)
                    for c in range(1, NB):
                        src = pc[:, (c - 1) // 4, P * ((c - 1) % 4):P * ((c - 1) % 4 + 1)]
                        if c == 1:
                            nc.vector.tensor_copy(state[:, c, :], src).then_inc(s_done, 1)
                        else:
                            dve.wait_ge(s_done, i * 7 + c - 1)
                            nc.vector.scalar_tensor_tensor(state[:, c, :], state[:, c - 1, :], eb[:, P * c - 1:P * c], src, ALU.mult, ALU.add).then_inc(s_done, 1)

            def hgrn_tail(i, slot):
                if slot == 0:
                    pick(i - 1, 8)
                if slot == 5:
                    dve.wait_ge(ors_done, i)
                    if not isinstance(i, int) or i > 1:
                        dve.wait_ge(oa_stored, 16 * i - 16)
                    for hf in range(2):
                        t = slice(HALF * hf, HALF * (hf + 1))
                        last = nc.vector.tensor_tensor(o_a[:, t], pc[:, hf, :], o_rs[:, t], ALU.mult)
                    last.then_inc(on_done, 1)
                    dve.wait_ge(on_done, i)
                    nc.vector.scalar_tensor_tensor(o_a[:], o_a[:], hgw[:], gg[:], ALU.mult, ALU.mult).then_inc(oa_done, 1)

            def hgrn(i, prev, cur):
                for slot in range(2 * HG_CHUNKS):
                    if cur and slot % 2 == 0:
                        split_lo(i * HG_CHUNKS + slot // 2 + 1, (slot // 2 + 1) % 2)
                    if prev:
                        hgrn_tail(i, slot)
                    if cur:
                        hgrn_cur(i, slot)

            hgrn(0, False, True)
            with dve.Fori(1, HEADS) as i:
                hgrn(i, True, True)
            hgrn(HEADS, True, False)

            dve.wait_ge(oa_stored, 16 * HEADS)
            for s in range(2):
                dve.wait_ge(gate_stored[s], 16 * HEADS)
            nc.vector.memset(vb[:], 1.0).then_inc(vb_done, 1)

            def row_max(i, g, m, h):
                u = 2 * (g * 4 + m) + h
                todo = max_queries(g, m)
                for k, (blk, at, before) in enumerate(todo):
                    lo, w = (at, 2 * P) if before else (at if g == 2 else at + P, P)
                    mask = mask_n[:, 2 * P:] if g == 2 else mask_n[:, 2 * P - w:2 * P]
                    at_m = (h * GROUPS + g) * NB + blk
                    done = max_count(u) + k
                    made, written = value(dve, i * 20 + u + 1), value(dve, i * N_MAX + done - 1)
                    dve.wait_ge(const_in, 11 * 16)
                    if k == 0:
                        dve.wait_ge(mx_made, made)
                    if not first(i) or done >= 2:
                        dve.wait_ge(mx_taken, written)
                    nc.vector.tensor_tensor_reduce(out=junk[:, done % 2, 0:w], in0=pa[:, h, lo:lo + w], in1=mask, scale=1.0, scalar=NEG,
                                                       op0=ALU.add, op1=ALU.max, accum_out=m_all[:, at_m:at_m + 1]).then_inc(mx_taken, 1)

            def attention(i, prev, cur):
                for slot in range(2 * AT_CHUNKS):
                    c, hf = slot // 2, slot % 2
                    n = N_HG + i * AT_CHUNKS + c
                    if prev:
                        for k in SUM_SLOTS.get(slot, ()):
                            g, h, b = k // 4, k // 2 % 2, k % 2
                            dve.wait_ge(pu_made, (i - 1) * N_UNITS + SUM_AFTER[k] + 1)
                            if g == 0:
                                nc.vector.tensor_copy(acc[h][:, HALF * b:HALF * (b + 1)], pc[:, b, :]).then_inc(ob_taken, 1)
                            else:
                                r = DILATIONS[g]
                                dst = by_residue(acc[h][:], g)[:, r // 2 * b:r // 2 * (b + 1), :]
                                dve.wait_ge(ob_taken, (i - 1) * N_SUMS + k)
                                nc.vector.tensor_tensor(dst, pc[:, b, :].rearrange("p (r i) -> p r i", r=r // 2), dst, ALU.add).then_inc(ob_taken, 1)
                    if cur and hf == 0:
                        split_lo(n + 1, (c + 1) % 2)
                    if prev and slot == 1:
                        dve.wait_ge(m_loaded, 16 * i)
                        r4 = m_rows[:, 1, :].rearrange("p (r i) -> p i r", r=4)
                        r16 = m_rows[:, 2, :].rearrange("p (r i) -> p i r", r=16)
                        r1 = m_rows[:, 0, :]
                        nc.vector.tensor_tensor(r1.rearrange("p (i r) -> p i r", r=4), r1.rearrange("p (i r) -> p i r", r=4), r4, ALU.min).then_inc(mj_done, 1)
                        dve.wait_ge(mj_done, i)
                        nc.vector.tensor_tensor(shift[:].rearrange("p (i r) -> p i r", r=16), r1.rearrange("p (i r) -> p i r", r=16), r16, ALU.min).then_inc(shift_done, 1)
                    if cur and 4 <= slot <= 14 and hf == 0:
                        j = (slot - 4) // 2
                        dve.wait_ge(swapped, (i * 6 + j + 1) * 64)
                        nc.vector.tensor_tensor(zz[j % 2][:], zz[j % 2][:], cos_t[:], ALU.mult).then_inc(rope_a, 1)
                        nc.vector.tensor_tensor(z_swap[:], z_swap[:], sin_t[:], ALU.mult).then_inc(rope_b, 1)
                        dve.wait_ge(rope_a, i * 6 + j + 1)
                        dve.wait_ge(rope_b, i * 6 + j + 1)
                        r = DILATIONS[j // 2]
                        nat = lambda t: t[:].rearrange("p (i r) -> p i r", r=r)
                        nc.vector.tensor_tensor(roped[:].rearrange("p (r i) -> p i r", r=r), nat(zz[j % 2]), nat(z_swap), ALU.add).then_inc(rope_sum, 1)
                    if cur and 5 <= slot <= 15 and hf == 1:
                        j = (slot - 5) // 2
                        dve.wait_ge(qk_hi_done, i * 6 + j + 1)
                        nc.vector.tensor_tensor(qk_lo[j // 2][j % 2][:], roped[:], qk_hi[j // 2][j % 2][:].bitcast(f32), ALU.subtract).then_inc(qk_lo_done, 1)
                    if cur and slot - 1 in MAX_SLOTS:
                        for h in range(2):
                            row_max(i, *MAX_SLOTS[slot - 1], h)
                    if prev and slot == 14:
                        dve.wait_ge(den_done, i)
                        nc.vector.tensor_tensor(r_den[:], r_den[:], s_ag[:], ALU.mult).then_inc(den_ag, 1)
                        dve.wait_ge(den_ag, i)
                        if not isinstance(i, int) or i > 1:
                            dve.wait_ge(ob_stored, 16 * i - 16)
                        for h in range(2):
                            rows = slice(EDIM * h, EDIM * (h + 1))
                            nc.vector.tensor_tensor(o_b[rows, :], acc[h][rows, :], r_den[rows, :], ALU.mult).then_inc(ob_done, 1)

            attention(0, False, True)
            with dve.Fori(1, PAIRS - 1) as i:
                attention(i, True, True)
            attention(PAIRS - 1, True, True)
            attention(PAIRS, True, False)

            for t in range(HEADS + PAIRS):
                dve.wait_ge(br_hi_done, t + 1)
                lo, hi = (oa_lo[:, t, :], oa_hi[:, t, :]) if t < HEADS else (ob_lo[:, t - HEADS, :], ob_hi[:, t - HEADS, :])
                nc.vector.tensor_tensor(lo, g_in[t % 2][:], hi.bitcast(f32), ALU.subtract).then_inc(br_lo_done, 1)

            def split_out_lo(n):
                c = n - N_IN - 16
                dve.wait_ge(w_hi_done, n + 1)
                hi, lo = (wq_hi, wq_lo) if c < 2 else (oa_hi, oa_lo)
                cols = slice(P * c, P * c + P)
                nc.vector.tensor_tensor(lo[:, :, cols], w_stage[n % 2][:], hi[:, :, cols].bitcast(f32), ALU.subtract).then_inc(w_lo_done, 1)

            for j in range(KT):
                for b in range(2):
                    n = N_IN + 2 * j + b
                    if n + 1 < N_IN + 16:
                        kt = HEADS if (n + 1) % 2 == 0 else PAIRS
                        s = (n + 1) % 2
                        dve.wait_ge(w_hi_done, n + 2)
                        nc.vector.tensor_tensor(w_lo[s][:, 0:kt, :], w_stage[s][:, 0:kt, :], w_hi[s][:, 0:kt, :].bitcast(f32), ALU.subtract).then_inc(w_lo_done, 1)
                    else:
                        split_out_lo(n + 1)
                    dve.wait_ge(g_loaded[b], 16 * (j + 1))
                    if b == 0 and j:
                        dve.wait_ge(mg_lo_done, j)
                    for hf in range(2):
                        t = slice(HALF * hf, HALF * (hf + 1))
                        dve.wait_ge(z_made[hf], n + 1)
                        if b == 0:
                            nc.vector.tensor_tensor(part[:, t], z_ps[hf][:], g_in[0][:, t], ALU.mult).then_inc(z_taken[hf], 1)
                        else:
                            nc.vector.tensor_tensor(g_in[1][:, t], pc[:, hf, :], g_in[1][:, t], ALU.mult).then_inc(z_taken[hf], 1)
                for hf in range(2):
                    dve.wait_ge(z_taken[hf], N_IN + 2 * j + 2)
                nc.vector.tensor_tensor(part[:], part[:], g_in[1][:], ALU.add).then_inc(mg_sum, 1)
                dve.wait_ge(mg_hi_done, j + 1)
                nc.vector.tensor_tensor(mg_lo[:, j, :], part[:], mg_hi[:, j, :].bitcast(f32), ALU.subtract).then_inc(mg_lo_done, 1)
            split_out_lo(N_IN + 17)
            for t in range(NB):
                dve.wait_ge(qa_made, t + 1)
                dve.wait_ge(y_loaded[t], 16)
                nc.vector.tensor_tensor(yy[:, t, 0:2 * P], z_ps[t % 2][:, 0:2 * P], yy[:, t, 0:2 * P], ALU.add).then_inc(qa_taken, 1)
                if t < 6:
                    split_out_lo(N_IN + 18 + t)
            dve.wait_ge(fnw_loaded, 16)
            for t in range(NB + 1):
                if t < NB:
                    src = (pa, pb)[t % 2]
                    dve.wait_ge(pb_made, 2 * t + 1)
                    nc.vector.tensor_tensor(yy[:, t, 2 * P:6 * P], src[:, 0, :], yy[:, t, 2 * P:6 * P], ALU.add).then_inc(pb_taken, 1)
                    dve.wait_ge(pb_made, 2 * t + 2)
                    nc.vector.tensor_tensor(yy[:, t, 6 * P:], src[:, 1, 0:2 * P], yy[:, t, 6 * P:], ALU.add).then_inc(pb_taken, 1)
                if t:
                    dve.wait_ge(ors2_done, t)
                    nc.vector.scalar_tensor_tensor(yy[:, t - 1, :], yy[:, t - 1, :], o_stat[:, 2, t - 1:t], fnw[:], ALU.mult, ALU.mult).then_inc(out_done, 1)


def kernel(**inputs):
    import concourse.bacc as bacc
    from concourse.bass_utils import run_bass_kernel_spmd

    f = {k: np.asarray(v) for k, v in inputs.items()}
    w = f["w_in"][0].reshape(KT, P, -1)
    arrays = {
        "x": f["x"][0],
        "positions": f["positions"],
        "norm_w": f["norm_w"][0].reshape(KT, P).T,
        "w_in": np.stack([w[:, :, c:c + P].transpose(1, 0, 2) for c in chunk_columns()]),
        "lb_logits": f["lb_logits"].reshape(2, HEADS, P).transpose(2, 0, 1),
        "hgrn_norm_w": f["hgrn_norm_w"][0].reshape(P, 1),
        "w_a": f["w_branch_a"][0].reshape(8, P, 8, P).transpose(2, 1, 0, 3),
        "w_b": f["w_branch_b"][0].reshape(4, P, 8, P).transpose(2, 1, 0, 3),
        "w_out": f["w_out"][0].reshape(8, P, 8, P).transpose(2, 1, 0, 3),
        "final_norm_w": f["final_norm_w"].reshape(1, D_MODEL),
    } | shape_constants()
    arrays = {k: np.ascontiguousarray(v) for k, v in arrays.items()}
    nc = bacc.Bacc("TRN2", target_bir_lowering=False, num_devices=1, dynamic_dma_scratch_size=1024)
    d = {k: nc.dram_tensor(k, v.shape, mybir.dt.from_np(v.dtype), kind="ExternalInput").ap() for k, v in arrays.items()}
    out = nc.dram_tensor("out", (SEQ, D_MODEL), mybir.dt.float32, kind="ExternalOutput").ap()
    build(nc, d, out)
    r = run_bass_kernel_spmd(nc, [arrays], core_ids=[0])
    return r.results[0]["out"].reshape(1, SEQ, D_MODEL)
```

```python
import numpy as np
from contextlib import ExitStack

import concourse.bass as bass
from concourse import mybir

P = 128
D_MODEL = 1024
SEQ = 1024
KT = D_MODEL // P
HEADS = 8
NB = SEQ // P
HALF = SEQ // 2
GROUPS = 3
DILATIONS = (1, 4, 16)
PAIRS = 4
EDIM = 64
HG_CHUNKS = 6
AT_CHUNKS = 10
N_HG = HEADS * HG_CHUNKS
N_AT = PAIRS * AT_CHUNKS
N_IN = N_HG + N_AT
LEVELS = (64, 32, 16, 8, 4, 2)
EPS = 1e-6
NEG = -1e30
ROPE_THETA = 10000.0
TINY = 2.0 ** -64


def chunk_columns():
    hq, hf, hi, hg = (n * D_MODEL for n in range(4))
    qkv = 4 * D_MODEL
    att = GROUPS * 8 * EDIM
    ag = qkv + 3 * att
    gates = ag + 8 * EDIM
    cols = []
    for h in range(HEADS):
        cols += [hf + P * h, hq + P * h, hi + P * h, hg + P * h, gates + P * h, gates + D_MODEL + P * h]
    for p in range(PAIRS):
        for g in range(GROUPS):
            cols += [qkv + s * att + g * 512 + P * p for s in (0, 1)]
        cols += [qkv + 2 * att + g * 512 + P * p for g in range(GROUPS)]
        cols += [ag + P * p]
    return cols


def shape_constants():
    s = np.arange(P)[:, None]
    level = np.zeros((2 + len(LEVELS[2:]), P, P), np.float32)
    c = np.arange(64)[None, :]
    level[0] = np.tile((s == 2 * c) | (s == 2 * c + 1), (1, 2))
    level[1] = np.tile(s == 2 * c, (1, 2))
    for j, span in enumerate(LEVELS[2:]):
        t = (c // span) * 2 * span + span + c % span
        level[j + 2] = np.tile((t // (2 * span) == s // (2 * span)) & (s % (2 * span) < span), (1, 2))
    i = np.arange(P)[None, :]
    own = np.where(i >= s, 0.0, NEG)
    after = np.where(s >= i, 0.0, NEG)
    same = np.where((i >= s) & (i // 64 == s // 64), 0.0, NEG)
    mask_t = np.concatenate([own, after, own, same], 1).astype(np.float32)
    mask_n = np.concatenate([after.T, own.T, same.T], 1).astype(np.float32)
    reset = np.ones((P, SEQ), np.float32)
    reset[:, ::P] = 0.0
    inv = (ROPE_THETA ** (-np.arange(0, EDIM, 2, dtype=np.float32) / np.float32(EDIM))).astype(np.float32)
    sign = np.where(np.arange(P) % EDIM < EDIM // 2, -1.0, 1.0)
    col = np.stack([np.tile(inv, 4), sign, np.full(P, EPS), np.full(P, 1.0 / P)], 1).astype(np.float32)
    sel = np.zeros((2, 2, P), np.float32)
    sel[0, 0] = sel[1, 1] = 1.0
    return {
        "c_level": np.ascontiguousarray(level.transpose(1, 0, 2)),
        "c_mask_t": mask_t, "c_mask_n": mask_n, "c_reset": reset, "c_col": col,
        "c_ident": np.eye(P, dtype=np.float32), "c_sel": sel,
    }



def build(nc, d, out):
    f32, f32r, bf16 = mybir.dt.float32, mybir.dt.float32r, mybir.dt.bfloat16
    u8, i32 = mybir.dt.uint8, mybir.dt.int32
    ACT = mybir.ActivationFunctionType
    ALU = mybir.AluOpType
    AX = mybir.AxisListType
    ctx = ExitStack()
    with ctx:
        sem = lambda name: ctx.enter_context(nc.semaphore(name))

        top = [0]

        def place(name, shape, dt=f32):
            n = int(np.prod(shape[1:])) * {f32: 4, f32r: 4, i32: 4, bf16: 2, u8: 1}[dt]
            t = nc.alloc_sbuf_tensor_at(name, shape, dt, offset=top[0])
            top[0] += (n + 31) // 32 * 32
            assert top[0] <= nc.sbuf_usable_end // 32 * 32, (name, top[0])
            return t

        top[0] = (nc.sbuf_base + 31) // 32 * 32
        ident = place("ident", [P, P])
        col = place("col", [P, 4])
        norm_w = place("norm_w", [P, KT])
        w_stage = [place(f"w_stage{s}", [P, KT, P]) for s in range(2)]
        w_hi = [place(f"w_hi{s}", [P, KT, P], f32r) for s in range(2)]
        w_lo = [place(f"w_lo{s}", [P, KT, P], f32r) for s in range(2)]
        cos_t = place("cos_t", [P, SEQ])
        sin_t = place("sin_t", [P, SEQ])
        mask_n = place("mask_n", [P, 3 * P])
        mask_b = place("mask_b", [P, 4 * P], bf16)
        ident_b = place("ident_b", [P, P], bf16)
        sel = place("sel", [2, 2, P], f32r)
        shift = place("shift", [2, SEQ], f32r)
        x_ss = place("x_ss", [P, NB])
        x_rms = place("x_rms", [P, NB])
        x_rs = place("x_rs", [P, NB])
        h_hi = place("h_hi", [P, KT, SEQ], f32r)
        h_lo = place("h_lo", [P, KT, SEQ], f32r)
        phase_base = top[0]
        level_mask = place("level_mask", [P, 6, HALF], u8)
        reset = place("reset", [P, SEQ])
        lb_in = place("lb_in", [P, 2, HEADS])
        lb = place("lb", [P, 6, HEADS])
        hgw = place("hgw", [P, 1])
        inv128 = place("inv128", [P, P])
        ff = place("ff", [P, SEQ])
        kk = place("kk", [P, SEQ])
        lf = place("lf", [P, SEQ])
        bb = place("bb", [P, SEQ])
        qq = place("qq", [P, SEQ])
        vt = place("vt", [P, SEQ])
        vv = place("vv", [P, NB, P])
        gg = place("gg", [P, SEQ])
        dd = [place(f"dd{s}", [P, SEQ]) for s in range(2)]
        ee = [place(f"ee{s}", [P, SEQ]) for s in range(2)]
        q_lv = [place(f"q_lv{s}", [P, HALF]) for s in range(2)]
        k_lv = [place(f"k_lv{s}", [P, SEQ]) for s in range(2)]
        k_one = place("k_one", [P, SEQ])
        eb = place("eb", [P, SEQ])
        q_in = place("q_in", [P, SEQ])
        late_base = top[0]
        k_out = place("k_out", [P, SEQ])
        k_tok = place("k_tok", [P, NB, P])
        scores = place("scores", [P, NB, P])
        state = place("state", [P, NB, P])
        o_sq = place("o_sq", [P, SEQ])
        o_rs = place("o_rs", [P, SEQ])
        o_a = place("o_a", [P, SEQ])
        gate = [place(f"gate{s}", [P, SEQ]) for s in range(2)]

        top[0] = late_base
        x_in = place("x_in", [P, NB, D_MODEL])
        x_sq = lf
        level_in, mask_t_in, sel_in = gg, vv, vv
        pos_in, turns, less = vt, o_sq, o_a

        top[0] = phase_base
        qk_hi = [[place(f"qk_hi{g}{s}", [P, SEQ], f32r) for s in range(2)] for g in range(GROUPS)]
        qk_lo = [[place(f"qk_lo{g}{s}", [P, SEQ], f32r) for s in range(2)] for g in range(2)]
        qk_full = [place(f"qk_full{s}", [P, SEQ]) for s in range(2)]
        zz = [place(f"zz{s}", [P, SEQ]) for s in range(2)]
        z_swap = place("z_swap", [P, SEQ])
        roped = place("roped", [P, SEQ])
        vb = place("vb", [P, GROUPS, NB, 3 * EDIM])
        pt = [place(f"pt{s}", [P, HALF]) for s in range(2)]
        acc = [place(f"acc{h}", [P, SEQ]) for h in range(2)]
        s_ag = place("s_ag", [P, SEQ])
        m_all = place("m_all", [P, 2 * GROUPS * NB])
        m_t = place("m_t", [2 * GROUPS * NB, P])
        junk = place("junk", [P, 2, 2 * P])
        rejoin = top[0]
        v_t = place("v_t", [P, SEQ])
        r_den = place("r_den", [P, SEQ])
        o_b = place("o_b", [P, SEQ])
        top[0] = rejoin
        m_rows = place("m_rows", [2, GROUPS, SEQ])
        oa_hi, oa_lo = h_hi, h_lo
        top[0] = phase_base
        ob_hi = place("ob_hi", [P, PAIRS, SEQ], f32r)
        ob_lo = place("ob_lo", [P, PAIRS, SEQ], f32r)
        mg_hi = place("mg_hi", [P, KT, SEQ], f32r)
        mg_lo = place("mg_lo", [P, KT, SEQ], f32r)
        wq_hi = place("wq_hi", [P, KT, 2 * P], f32r)
        wq_lo = place("wq_lo", [P, KT, 2 * P], f32r)
        part = place("part", [P, SEQ])
        o_stat = place("o_stat", [P, 3, NB])
        g_in = [cos_t, sin_t]
        br_in = [cos_t, sin_t, zz[0], zz[1]]
        top[0] = phase_base
        yy = place("yy", [P, NB, D_MODEL])
        fnw = part

        z_ps = [ctx.enter_context(nc.psum_tensor(f"z_ps{s}", [P, HALF], f32)) for s in range(2)]
        pa, pb, pc = (ctx.enter_context(nc.psum_tensor(n, [P, 2, HALF], f32)) for n in ("pa", "pb", "pc"))

        gate_d = nc.dram_tensor("gate_d", [2, HEADS, P, SEQ], f32).ap()
        o_a_d = nc.dram_tensor("o_a_d", [HEADS, P, SEQ], f32).ap()

        o_b_d = nc.dram_tensor("o_b_d", [PAIRS, P, SEQ], f32).ap()
        m_d = nc.dram_tensor("m_d", [PAIRS, 2 * GROUPS * NB, P], f32).ap()

        const_in, lb_loaded, hg_loaded, pos_loaded, mask_loaded = (sem(n) for n in ("const_in", "lb_loaded", "hg_loaded", "pos_loaded", "mask_loaded"))
        x_loaded = [sem(f"x_loaded{t}") for t in range(NB)]
        ss_act, ss_dve, rms_done, rs_done, xn_done = (sem(n) for n in ("ss_act", "ss_dve", "rms_done", "rs_done", "xn_done"))
        xt_made, h_hi_done, h_lo_done = sem("xt_made"), sem("h_hi_done"), sem("h_lo_done")
        w_loaded = [sem(f"w_loaded{s}") for s in range(2)]
        w_hi_done, w_lo_done = sem("w_hi_done"), sem("w_lo_done")
        z_made = [sem(f"z_made{s}") for s in range(2)]
        z_taken = [sem(f"z_taken{s}") for s in range(2)]
        mask_done = sem("mask_done")
        lb_step, init_done = sem("lb_step"), sem("init_done")
        f_done, k_done, ln_done, b_done = sem("f_done"), sem("k_done"), sem("ln_done"), sem("b_done")
        eb_done, d_done, e_done = sem("eb_done"), sem("d_done"), sem("e_done")
        q_in_done, k_one_done, lv_done = sem("q_in_done"), sem("k_one_done"), sem("lv_done")
        k_out_done, kt_made, kt_taken = sem("k_out_done"), sem("kt_made"), sem("kt_taken")
        vt_made, v_taken, upd_made = sem("vt_made"), sem("v_taken"), sem("upd_made")
        lvl_made, lvl_taken, s_done = sem("lvl_made"), sem("lvl_taken"), sem("s_done")
        pv_made, sq_done, ms_made, ms_ln = sem("pv_made"), sem("sq_done"), sem("ms_made"), sem("ms_ln")
        ors_done, on_done, oa_done = sem("ors_done"), sem("on_done"), sem("oa_done")
        oa_stored = sem("oa_stored")
        gate_stored = [sem(f"gate_stored{s}") for s in range(2)]

        rope_step, sin_done = sem("rope_step"), sem("sin_done")
        vb_done = sem("vb_done")
        swapped, rope_a, rope_b, rope_sum = sem("swapped"), sem("rope_a"), sem("rope_b"), sem("rope_sum")
        qk_hi_done, qk_lo_done = sem("qk_hi_done"), sem("qk_lo_done")
        avt_made, av_taken = sem("avt_made"), sem("av_taken")
        mx_made, mx_taken, mt_made, mt_taken = sem("mx_made"), sem("mx_taken"), sem("mt_made"), sem("mt_taken")
        m_stored, m_loaded, mj_done, shift_done = sem("m_stored"), sem("m_loaded"), sem("mj_done"), sem("shift_done")
        st_made, pt_done, pu_made = sem("st_made"), sem("pt_done"), sem("pu_made")
        ob_taken = sem("ob_taken")
        den_ln, den_done, den_ag, ob_done, ob_stored = sem("den_ln"), sem("den_done"), sem("den_ag"), sem("ob_done"), sem("ob_stored")
        br_loaded = [sem(f"br_loaded{s}") for s in range(4)]
        br_hi_done, br_lo_done = sem("br_hi_done"), sem("br_lo_done")
        g_loaded = [sem(f"g_loaded{s}") for s in range(2)]
        ya_done, yb_done, mg_sum, mg_hi_done, mg_lo_done = sem("ya_done"), sem("yb_done"), sem("mg_sum"), sem("mg_hi_done"), sem("mg_lo_done")
        y_loaded = [sem(f"y_loaded{t}") for t in range(NB)]
        fnw_loaded = sem("fnw_loaded")
        qa_made, qa_taken, pb_made, pb_taken = sem("qa_made"), sem("qa_taken"), sem("pb_made"), sem("pb_taken")
        oss_done, orms_done, ors2_done, out_done = sem("oss_done"), sem("orms_done"), sem("ors2_done"), sem("out_done")
        out_stored = sem("out_stored")

        block = ctx.enter_context(nc.Block())
        ACT_SQUARES, DVE_SQUARES = (0, 2, 6, 7), (1, 3, 4, 5)
        first = lambda i: isinstance(i, int) and i == 0

        def value(eng, v):
            return v if isinstance(v, int) else eng.to_reg(v)


        UNITS = [(g, h, m) for g in range(GROUPS) for h in range(2) for m in range(4 if g < 2 else 2)]
        N_UNITS = len(UNITS)
        UNIT_SLOTS = {2: (0, 1, 2), 3: (3, 4, 5), 4: (6, 7), 5: (8, 9), 6: (10, 11), 7: (12, 13), 8: (14, 15),
                      9: (16, 17), 10: (18, 19)}
        SUM_AFTER = [1, 3, 5, 7, 9, 11, 13, 15, 16, 17, 18, 19]
        SUM_SLOTS = {3: (0,), 4: (1,), 5: (2,), 6: (3,), 7: (4,), 8: (5,), 9: (6,), 10: (7, 8), 11: (9, 10), 12: (11,)}
        N_SUMS = len(SUM_AFTER)
        ROPE_STEPS = 22
        MASKS = 10
        N_BR = HEADS + PAIRS
        N_UNIT_HG = 2 + len(LEVELS)
        MAX_SLOTS = {8 + u: ((u // 4, u % 4),) for u in range(8)} | {16: ((2, 0), (2, 1))}
        N_MAX = 2 * GROUPS * NB
        max_count = lambda u: 2 * u if u <= 16 else 32 + 4 * (u - 16)

        def unit_keys(g, m):
            if g == 0:
                return [(c, 256 * (c - 2 * m), 2 if c < NB - 1 else 1) for c in (2 * m, 2 * m + 1)]
            if g == 1:
                return [(2 * m, 0, 2), (2 * m + 1, 256, 1)]
            return [(4 * m + c, P * c, 1) for c in range(4)]

        def max_queries(g, m):
            if g == 2:
                return [(4 * m + c, P * c, False) for c in range(4)]
            return [(c, 256 * (c % 2), c > 0 if g == 0 else c % 2 == 1) for c in (2 * m, 2 * m + 1)]

        def by_residue(ap, g):
            return ap.rearrange("p (i r) -> p r i", r=DILATIONS[g])

        @block.sync
        def _(sp):
            def load_w(n, s, src):
                sp.dma_start(w_stage[s][:, 0:src.shape[1], :], src).then_inc(w_loaded[s], 16)

            def load_x(t):
                sp.dma_start(x_in[:, t, :], d["x"][P * t:P * (t + 1), :]).then_inc(x_loaded[t], 16)

            load_x(0)
            for s, src in ((ident, "c_ident"), (col, "c_col"), (norm_w, "norm_w")):
                sp.dma_start(s[:], d[src]).then_inc(const_in, 16)
            sp.dma_start(lb_in[:], d["lb_logits"]).then_inc(lb_loaded, 16)
            for t in range(1, 4):
                load_x(t)
            load_w(0, 0, d["w_in"][0])
            for t in range(4, NB):
                load_x(t)
            load_w(1, 1, d["w_in"][1])
            sp.dma_start(pos_in[:].bitcast(i32), d["positions"].to_broadcast([P, SEQ])).then_inc(pos_loaded, 16)
            for s, src in ((reset, "c_reset"), (hgw, "hgrn_norm_w")):
                sp.dma_start(s[:], d[src]).then_inc(hg_loaded, 16)
            sp.dma_start(level_in[:, 0:6 * P].rearrange("p (m c) -> p m c", c=P), d["c_level"]).then_inc(mask_loaded, 16)
            sp.dma_start(mask_t_in[:, 0:4, :].rearrange("p a b -> p (a b)"), d["c_mask_t"]).then_inc(mask_loaded, 16)
            sp.dma_start(sel_in[0:2, 4:6, :], d["c_sel"]).then_inc(mask_loaded, 16)
            sp.dma_start(mask_n[:], d["c_mask_n"]).then_inc(mask_loaded, 16)

            def hgrn(i, prev, cur):
                for c in range(HG_CHUNKS):
                    if cur:
                        n = i * HG_CHUNKS + c
                        split = value(sp, n + 1)
                        sp.wait_ge(const_in, 48)
                        sp.wait_ge(w_lo_done, split)
                        sp.dma_start(w_stage[c % 2][:], d["w_in"][bass.ds(n + 2, 1)].rearrange("a p k c -> (a p) k c")).then_inc(w_loaded[c % 2], 16)
                    if prev and c == 1:
                        taken = value(sp, i * HG_CHUNKS)
                        sp.wait_ge(const_in, 48)
                        for s in range(2):
                            sp.wait_ge(z_taken[s], taken)
                        sp.dma_start(gate_d[1, bass.ds(i - 1, 1)].rearrange("a p t -> (a p) t"), gate[1][:]).then_inc(gate_stored[1], 16)
                    if prev and c == 4:
                        sp.wait_ge(const_in, 48)
                        sp.wait_ge(oa_done, i)
                        sp.dma_start(o_a_d[bass.ds(i - 1, 1)].rearrange("a p t -> (a p) t"), o_a[:]).then_inc(oa_stored, 16)
                    if cur and c == 5:
                        taken = value(sp, i * HG_CHUNKS + 5)
                        sp.wait_ge(const_in, 48)
                        for s in range(2):
                            sp.wait_ge(z_taken[s], taken)
                        sp.dma_start(gate_d[0, bass.ds(i, 1)].rearrange("a p t -> (a p) t"), gate[0][:]).then_inc(gate_stored[0], 16)

            hgrn(0, False, True)
            with sp.Fori(1, HEADS) as i:
                hgrn(i, True, True)
            def load_stage(n, s):
                if isinstance(n, int) and n >= N_IN:
                    n -= N_IN
                    if n < 16:
                        src = d["w_a"][n // 2] if n % 2 == 0 else d["w_b"][n // 2]
                    elif n < 24:
                        src = d["w_out"][n - 16]
                    else:
                        return
                    sp.dma_start(w_stage[s][:, 0:src.shape[1], :], src).then_inc(w_loaded[s], 16)
                else:
                    sp.dma_start(w_stage[s][:], d["w_in"][bass.ds(n, 1)].rearrange("a p k c -> (a p) k c")).then_inc(w_loaded[s], 16)

            def attention(i, prev, cur):
                for c in range(AT_CHUNKS):
                    n = N_HG + i * AT_CHUNKS + c
                    if cur:
                        split = value(sp, n + 1)
                        sp.wait_ge(const_in, 48)
                        sp.wait_ge(w_lo_done, split)
                        load_stage(n + 2, c % 2)
                    if first(i) and c == 1:
                        for s in range(2):
                            sp.wait_ge(z_taken[s], N_HG)
                        sp.dma_start(gate_d[1, HEADS - 1], gate[1][:]).then_inc(gate_stored[1], 16)
                        sp.wait_ge(lvl_made, N_UNIT_HG * HEADS)
                    if first(i) and c == 4:
                        sp.wait_ge(oa_done, HEADS)
                        sp.dma_start(o_a_d[HEADS - 1], o_a[:]).then_inc(oa_stored, 16)
                    if cur and c == 9:
                        if first(i):
                            sp.wait_ge(oa_stored, 16 * HEADS)
                            for s in range(2):
                                sp.wait_ge(gate_stored[s], 16 * HEADS)
                        maxed = value(sp, i + 1)
                        sp.wait_ge(const_in, 48)
                        sp.wait_ge(mt_taken, maxed)
                        sp.dma_start(m_d[bass.ds(i, 1)].rearrange("a m q -> (a m) q"), m_t[:]).then_inc(m_stored, 16)
                        stored, ob_out, v_turned = value(sp, 16 * i + 16), value(sp, 16 * i), value(sp, 3 * i + 3)
                        sp.wait_ge(const_in, 48)
                        sp.wait_ge(m_stored, stored)
                        sp.wait_ge(avt_made, v_turned)
                        if prev:
                            sp.wait_ge(ob_stored, ob_out)
                        sp.dma_start(m_rows[:], m_d[bass.ds(i, 1)].rearrange("a (h g b) q -> (a h) g (b q)", h=2, g=GROUPS)).then_inc(m_loaded, 16)
                    if cur and 1 <= c <= 6:
                        taken, rotated = value(sp, n), value(sp, i * 6 + c - 1)
                        sp.wait_ge(const_in, 48)
                        for s in range(2):
                            sp.wait_ge(z_taken[s], taken)
                        if c > 1 or not first(i):
                            sp.wait_ge(rope_sum, rotated)
                        for q in range(4):
                            o = q ^ 1
                            sp.dma_start(z_swap[32 * q:32 * q + 32, :], zz[(c - 1) % 2][32 * o:32 * o + 32, :]).then_inc(swapped, 16)
                    if prev and cur and c == 8:
                        done = value(sp, 2 * i)
                        sp.wait_ge(const_in, 48)
                        sp.wait_ge(ob_done, done)
                        sp.dma_start(o_b_d[bass.ds(i - 1, 1)].rearrange("a p t -> (a p) t"), o_b[:]).then_inc(ob_stored, 16)

            attention(0, False, True)
            with sp.Fori(1, PAIRS - 1) as i:
                attention(i, True, True)
            attention(PAIRS - 1, True, True)

            sp.wait_ge(rope_sum, 6 * PAIRS)
            for t in range(N_BR - 1):
                if t >= 4:
                    sp.wait_ge(br_lo_done, t - 3)
                src = o_a_d[t] if t < HEADS else o_b_d[t - HEADS]
                sp.dma_start(br_in[t % 4][:], src).then_inc(br_loaded[t % 4], 16)
            sp.wait_ge(br_lo_done, N_BR - 1)
            for j in range(KT):
                n = N_IN + 2 * j
                for c in range(2):
                    if j:
                        sp.wait_ge(mg_sum, j)
                    sp.dma_start(g_in[c][:], gate_d[c, j]).then_inc(g_loaded[c], 16)
                    sp.wait_ge(w_lo_done, n + c + 1)
                    load_stage(n + c + 2, c)
            for c in range(6):
                sp.wait_ge(w_lo_done, N_IN + 16 + c + 1)
                load_stage(N_IN + 16 + c + 2, c % 2)
                if c == 0:
                    sp.wait_ge(z_made[1], N_IN + 16)
                    for t in range(NB):
                        sp.dma_start(yy[:, t, :], d["x"][P * t:P * (t + 1), :]).then_inc(y_loaded[t], 16)
                    sp.wait_ge(mg_lo_done, KT)
                    sp.dma_start(fnw[:], d["final_norm_w"].to_broadcast([P, D_MODEL])).then_inc(fnw_loaded, 16)
            for t in range(NB):
                sp.wait_ge(out_done, t + 1)
                sp.dma_start(out[P * t:P * (t + 1), :], yy[:, t, :]).then_inc(out_stored, 16)
            sp.wait_ge(out_stored, 16 * NB)

        @block.gpsimd
        def _(pool):
            for t in k_lv:
                nc.gpsimd.memset(t[:], 0.0).then_inc(init_done, 1)
            nc.gpsimd.memset(inv128[:], 1.0 / P).then_inc(init_done, 1)
            steps = [0]

            def link(ins):
                steps[0] += 1
                ins.then_inc(rope_step, 1)
                pool.wait_ge(rope_step, steps[0])

            pool.wait_ge(const_in, 48)
            pool.wait_ge(pos_loaded, 16)
            link(nc.gpsimd.tensor_copy(cos_t[:], pos_in[:].bitcast(i32)))
            link(nc.gpsimd.tensor_scalar(cos_t[:], cos_t[:], col[:, 0:1], None, ALU.mult))
            pool.wait_ge(mask_loaded, 4 * 16)
            for m in range(6):
                src = level_in[:, P * m:P * (m + 1)].rearrange("p (a c) -> p a c", a=1).to_broadcast([P, 4, P])
                nc.gpsimd.tensor_copy(level_mask[:, m, :].rearrange("p (a c) -> p a c", c=P), src).then_inc(mask_done, 1)
            pool.wait_ge(xt_made, 2 * KT)
            nc.gpsimd.memset(scores[:], 0.0).then_inc(mask_done, 1)
            nc.gpsimd.tensor_copy(mask_b[:], mask_t_in[:, 0:4, :].rearrange("p a b -> p (a b)")).then_inc(mask_done, 1)
            nc.gpsimd.tensor_copy(sel[:], sel_in[0:2, 4:6, :]).then_inc(mask_done, 1)
            nc.gpsimd.tensor_copy(ident_b[:], ident[:]).then_inc(mask_done, 1)

            two_pi = 2 * np.pi
            parts = [6.28125, float(np.float32(np.floor((two_pi - 6.28125) * 2 ** 20) / 2 ** 20))]
            parts.append(float(np.float32(two_pi - parts[0] - parts[1])))
            magic = 1.5 * 2 ** 23
            lim = float(np.nextafter(np.float32(np.pi), np.float32(0)))
            for s, dst in ((0, sin_t), (1, cos_t)):
                link(nc.gpsimd.tensor_scalar(turns[:], cos_t[:], 1.0 / two_pi, 0.25 * s, ALU.mult, ALU.add))
                link(nc.gpsimd.tensor_scalar(turns[:], turns[:], magic, magic, ALU.add, ALU.subtract))
                for n, part_of_turn in enumerate(parts):
                    link(nc.gpsimd.tensor_scalar(less[:], turns[:], -part_of_turn, None, ALU.mult))
                    link(nc.gpsimd.tensor_tensor(dst[:], less[:], (dst if n else cos_t)[:], ALU.add))
                if s:
                    link(nc.gpsimd.tensor_scalar(dst[:], dst[:], float(np.pi / 2), None, ALU.add))
                link(nc.gpsimd.tensor_scalar(dst[:], dst[:], lim, -lim, ALU.min, ALU.max))
                if s == 0:
                    link(nc.gpsimd.tensor_scalar(dst[:], dst[:], col[:, 1:2], None, ALU.mult))
            assert steps[0] == ROPE_STEPS
            pool.wait_ge(pv_made, HEADS)
            pool.wait_ge(lvl_made, N_UNIT_HG * HEADS)
            nc.gpsimd.memset(vb[:], 1.0).then_inc(vb_done, 1)

        @block.tensor
        def _(pe):
            def x_transpose(u):
                k, hf = u % KT, u // KT
                if u >= 4:
                    pe.wait_ge(h_lo_done, u - 3)
                for t in range(4):
                    last = nc.tensor.transpose((pa, pb)[u // 2 % 2][:, u % 2, P * t:P * (t + 1)],
                                               x_in[:, 4 * hf + t, P * k:P * (k + 1)], ident[:])
                last.then_inc(xt_made, 1)

            pe.wait_ge(const_in, 48)
            for hf in range(2):
                t = slice(HALF * hf, HALF * (hf + 1))
                pe.wait_ge(xn_done, 4 * hf + 4)
                for k in range(4):
                    x_transpose(KT * hf + k)
                pe.wait_ge(w_lo_done, 1)
                for k in range(KT):
                    pe.wait_ge(h_lo_done, KT * hf + k + 1)
                    nc.tensor.matmul(z_ps[hf][:], w_hi[0][:, k, :], h_hi[:, k, t], start=k == 0, stop=False)
                    nc.tensor.matmul(z_ps[hf][:], w_hi[0][:, k, :], h_lo[:, k, t], start=False, stop=False)
                    last = nc.tensor.matmul(z_ps[hf][:], w_lo[0][:, k, :], h_hi[:, k, t], start=False, stop=k == KT - 1)
                    if k < 4:
                        x_transpose(KT * hf + k + 4)
                last.then_inc(z_made[hf], 1)

            def project(n, s, hf):
                if hf == 0:
                    pe.wait_ge(w_lo_done, n + 1)
                pe.wait_ge(z_taken[hf], n)
                t = slice(HALF * hf, HALF * (hf + 1))
                for k in range(KT):
                    nc.tensor.matmul(z_ps[hf][:], w_hi[s][:, k, :], h_hi[:, k, t], start=k == 0, stop=False)
                    nc.tensor.matmul(z_ps[hf][:], w_hi[s][:, k, :], h_lo[:, k, t], start=False, stop=False)
                    last = nc.tensor.matmul(z_ps[hf][:], w_lo[s][:, k, :], h_hi[:, k, t], start=False, stop=k == KT - 1)
                last.then_inc(z_made[hf], 1)

            def level_product(i, j):
                dst = pb[:, j % 2, :]
                if j >= 2 or not first(i):
                    pe.wait_ge(lvl_taken, i * N_UNIT_HG + (j - 1))
                if j == 0:
                    pe.wait_ge(k_one_done, i + 1)
                    for s in range(2):
                        pe.wait_ge(z_taken[s], i * HG_CHUNKS + 2)
                elif j >= 2:
                    pe.wait_ge(lv_done, i * 6 + (j - 1))
                for c in range(NB):
                    if j < 2:
                        k_side = (k_one, kk)[j][:, P * c:P * c + P]
                        q_side = qq[:, P * c:P * c + P].rearrange("p (n two) -> p n two", two=2)[:, :, 1 - j]
                    else:
                        k_side, q_side = k_lv[j % 2][:, P * c:P * c + P], q_lv[j % 2][:, 64 * c:64 * c + 64]
                    if 2 <= j < 4:
                        span = LEVELS[j - 2]
                        for g in range(64 // span):
                            last = nc.tensor.matmul(dst[2 * span * g:2 * span * g + span, 64 * c + span * g:64 * c + span * (g + 1)],
                                                    k_side[:, 2 * span * g:2 * span * g + span], q_side[:, span * g:span * (g + 1)],
                                                    start=True, stop=True)
                        continue
                    last = nc.tensor.matmul(dst[:, 64 * c:64 * c + 64], k_side, q_side, start=True, stop=True)
                last.then_inc(lvl_made, 1)

            def hgrn_cur(i, slot):
                if slot == 5:
                    pe.wait_ge(k_out_done, i + 1)
                    if not isinstance(i, int) or i > 0:
                        pe.wait_ge(ms_ln, i * 2)
                    for c in range(NB):
                        last = nc.tensor.transpose(pa[:, c // 4, P * (c % 4):P * (c % 4 + 1)], k_out[:, P * c:P * c + P], ident[:])
                    last.then_inc(kt_made, 1)
                    level_product(i, 0)
                    level_product(i, 1)
                elif slot >= 6:
                    level_product(i, slot - 4)
                if slot == 7:
                    pe.wait_ge(kt_taken, i * 2 + 2)
                    for s in range(2):
                        pe.wait_ge(z_taken[s], i * HG_CHUNKS + 3)
                    for c in range(NB):
                        last = nc.tensor.transpose(pa[:, c // 4, P * (c % 4):P * (c % 4 + 1)], vt[:, P * c:P * c + P], ident[:])
                    last.then_inc(vt_made, 1)
                if slot == 9:
                    pe.wait_ge(v_taken, i * 2 + 2)
                    if not isinstance(i, int) or i > 0:
                        pe.wait_ge(on_done, i)
                    for c in range(NB - 1):
                        last = nc.tensor.matmul(pc[:, c // 4, P * (c % 4):P * (c % 4 + 1)], k_tok[:, c, :], vv[:, c, :], start=True, stop=True)
                    last.then_inc(upd_made, 1)

            def hgrn_tail(i, slot):
                if slot == 1:
                    pe.wait_ge(lvl_taken, i * N_UNIT_HG)
                    pe.wait_ge(s_done, i * 7)
                    for c in range(NB):
                        o = pc[:, c // 4, P * (c % 4):P * (c % 4 + 1)]
                        last = nc.tensor.matmul(o, vv[:, c, :], scores[:, c, :], start=True, stop=c == 0)
                        if c:
                            last = nc.tensor.matmul(o, state[:, c, :], q_in[:, P * c:P * c + P], start=False, stop=True)
                    last.then_inc(pv_made, 1)
                if slot == 3:
                    pe.wait_ge(sq_done, i * 2)
                    for hf in range(2):
                        last = nc.tensor.matmul(pa[:, hf, :], inv128[:], o_sq[:, HALF * hf:HALF * (hf + 1)], start=True, stop=True)
                    last.then_inc(ms_made, 1)

            pe.wait_ge(init_done, 3)

            def hgrn(i, prev, cur):
                for slot in range(2 * HG_CHUNKS):
                    if cur:
                        if not first(i) or slot >= 2:
                            project(i * HG_CHUNKS + slot // 2, slot // 2 % 2, slot % 2)
                        hgrn_cur(i, slot)
                    if prev:
                        hgrn_tail(i, slot)

            hgrn(0, False, True)
            with pe.Fori(1, HEADS) as i:
                hgrn(i, True, True)

            def maxima(i, g, m, h):
                u = 2 * (g * 4 + m) + h
                rows = slice(EDIM * h, EDIM * (h + 1))
                if u >= 2:
                    pe.wait_ge(mx_taken, i * N_MAX + max_count(u - 1))
                elif not first(i):
                    pe.wait_ge(mx_taken, i * N_MAX)
                pe.wait_ge(qk_hi_done, i * 6 + 2 * g + 2)
                for blk, at, before in max_queries(g, m):
                    lo = blk - 1 if before else blk
                    at += 0 if before or g == 2 else P
                    last = nc.tensor.matmul(pa[:, h, at:at + P * (blk + 1 - lo)], qk_hi[g][0][rows, P * blk:P * blk + P],
                                            qk_hi[g][1][rows, P * lo:P * blk + P], start=True, stop=True)
                last.then_inc(mx_made, 1)

            def scores_t(i, u):
                g, h, m = UNITS[u]
                rows = slice(EDIM * h, EDIM * (h + 1))
                base = (i - 1) * N_UNITS
                if u == 0:
                    pe.wait_ge(shift_done, i)
                    pe.wait_ge(av_taken, i * 6)
                if u >= 2:
                    pe.wait_ge(pt_done, base + u - 1)
                pe.wait_ge(qk_lo_done, i * 4)
                pe.wait_ge(rope_sum, i * 6)
                units = unit_keys(g, m)
                cols = sum(P * n for _, _, n in units)
                bank = pb[:, u % 2, 0:cols]
                twice = lambda ap, n: ap.rearrange("p (a c) -> p a c", a=1).to_broadcast([P, n, ap.shape[1]])
                mask = twice(mask_b[:, 3 * P:], 4) if g == 2 else mask_b[:, 0:cols] if cols == 3 * P else twice(mask_b[:, 0:2 * P], 2)
                nc.tensor.matmul(bank, ident_b[:], mask, start=True, stop=False)
                if g == 2:
                    row = shift[:].rearrange("p (i r) -> p r i", r=16)[:, 8 * m:8 * m + 8, :]
                    nc.tensor.matmul(bank, sel[:, h, :], row, start=False, stop=False)
                for blk, at, n in units:
                    dst = pb[:, u % 2, at:at + P * n]
                    ks, qs = slice(P * blk, P * blk + P), slice(P * blk, P * (blk + n))
                    if g == 2:
                        last = nc.tensor.matmul(dst, qk_full[1][rows, ks], qk_full[0][rows, qs], start=False, stop=blk == units[-1][0])
                        continue
                    nc.tensor.matmul(dst, qk_hi[g][1][rows, ks], qk_hi[g][0][rows, qs], start=False, stop=False)
                    nc.tensor.matmul(dst, qk_hi[g][1][rows, ks], qk_lo[g][0][rows, qs], start=False, stop=False)
                    nc.tensor.matmul(dst, qk_lo[g][1][rows, ks], qk_hi[g][0][rows, qs], start=False, stop=False)
                    row = shift[:, qs]
                    if g == 1:
                        row = shift[:].rearrange("p (n i r) -> p n r i", n=2, r=4)[:, blk % 2:blk % 2 + n, blk // 2, :]
                    last = nc.tensor.matmul(dst, sel[:, h, :], row, start=False, stop=blk == units[-1][0])
                last.then_inc(st_made, 1)

            def weighted(i, u):
                g, h, m = UNITS[u]
                pe.wait_ge(pt_done, (i - 1) * N_UNITS + u + 1)
                made = (i - 1) * N_SUMS
                for blk, at, n in unit_keys(g, m):
                    for q in range(n):
                        bank = (blk + q) // 4
                        opens = (blk + q) % 4 == 0 and q == (1 if g == 0 and blk else 0)
                        closes = (blk + q) % 4 == 3 and q == 0
                        if opens:
                            k = (2 * g + h) * 2 + bank
                            if k >= 2:
                                pe.wait_ge(ob_taken, made + k - 1)
                        last = nc.tensor.matmul(pc[:, bank, P * ((blk + q) % 4):P * ((blk + q) % 4 + 1)], vb[:, g, blk, EDIM * h:EDIM * h + P],
                                                pt[u % 2][:, at + P * q:at + P * q + P], start=opens, stop=closes)
                last.then_inc(pu_made, 1)

            def attention(i, prev, cur):
                for slot in range(2 * AT_CHUNKS):
                    c = slot // 2
                    if cur:
                        project(N_HG + i * AT_CHUNKS + c, c % 2, slot % 2)
                    if first(i):
                        hgrn_tail(HEADS, slot)
                        if slot == 6:
                            pe.wait_ge(on_done, HEADS)
                    if prev:
                        for u in UNIT_SLOTS.get(slot, ()):
                            scores_t(i, u)
                            if u:
                                weighted(i, u - 1)
                        if slot == 11:
                            weighted(i, N_UNITS - 1)
                    if not cur:
                        for hf in range(2):
                            if 3 <= slot < 3 + HEADS:
                                branch(0, 0, hf, (slot - 3,))
                            elif 3 + HEADS <= slot < 2 + N_BR:
                                branch(0, 1, hf, (slot - 3 - HEADS,))
                    if cur:
                        for g, m in MAX_SLOTS.get(slot, ()):
                            for h in range(2):
                                maxima(i, g, m, h)
                    if cur and slot == 18:
                        maxed, summed = value(pe, i * N_MAX + N_MAX), value(pe, i * N_SUMS)
                        pe.wait_ge(const_in, 48)
                        pe.wait_ge(mx_taken, maxed)
                        if prev:
                            pe.wait_ge(ob_taken, summed)
                        nc.tensor.transpose(pc[0:2 * GROUPS * NB, 0, 0:P], m_all[:], ident[:]).then_inc(mt_made, 1)
                    if cur and slot in (14, 16, 18):
                        g = (slot - 14) // 2
                        for s in range(2):
                            pe.wait_ge(z_taken[s], N_HG + i * AT_CHUNKS + 7 + g)
                        if g:
                            pe.wait_ge(av_taken, i * 6 + 2 * g)
                        for b in range(NB):
                            last = nc.tensor.transpose(pb[:, b // 4, P * (b % 4):P * (b % 4 + 1)], v_t[:, P * b:P * b + P], ident[:])
                        last.then_inc(avt_made, 1)

            def branch(j, b, hf, ks=None):
                n = N_IN + 2 * j + b
                src_hi, src_lo = ((oa_hi, oa_lo), (ob_hi, ob_lo))[b]
                kt = (HEADS, PAIRS)[b]
                t = slice(HALF * hf, HALF * (hf + 1))
                dst = z_ps[hf][:] if b == 0 else pa[:, hf, :]
                for k in ks or range(kt):
                    if j == 0:
                        pe.wait_ge(br_lo_done, HEADS * b + k + 1)
                    if k == 0:
                        pe.wait_ge(w_lo_done, n + 1)
                        pe.wait_ge(z_taken[hf], n - b if j == 0 else n)
                    nc.tensor.matmul(dst, w_hi[b][:, k, :], src_hi[:, k, t], start=k == 0, stop=False)
                    nc.tensor.matmul(dst, w_hi[b][:, k, :], src_lo[:, k, t], start=False, stop=False)
                    last = nc.tensor.matmul(dst, w_lo[b][:, k, :], src_hi[:, k, t], start=False, stop=k == kt - 1)
                if k == kt - 1:
                    last.then_inc(z_made[hf], 1)

            pe.wait_ge(mask_done, MASKS)
            attention(0, False, True)
            with pe.Fori(1, PAIRS - 1) as i:
                attention(i, True, True)
            attention(PAIRS - 1, True, True)
            attention(PAIRS, True, False)

            for hf in range(2):
                branch(0, 1, hf, (PAIRS - 1,))
            for j in range(1, KT):
                for b in range(2):
                    for hf in range(2):
                        branch(j, b, hf)

            def out_product(dst, t, w_h, w_l, cols, ks=range(KT)):
                tt = slice(P * t, P * t + P)
                for k in ks:
                    nc.tensor.matmul(dst, mg_hi[:, k, tt], w_h[:, k, cols], start=k == 0, stop=False)
                    nc.tensor.matmul(dst, mg_hi[:, k, tt], w_l[:, k, cols], start=False, stop=False)
                    last = nc.tensor.matmul(dst, mg_lo[:, k, tt], w_h[:, k, cols], start=False, stop=k == KT - 1)
                return last

            quarter = slice(0, 2 * P)
            pe.wait_ge(w_lo_done, N_IN + 18)
            pe.wait_ge(mg_lo_done, KT - 1)
            qa_bank = (z_ps[0][:, quarter], z_ps[1][:, quarter], pb[:, 0, quarter], pb[:, 1, quarter])
            for t in range(2):
                pe.wait_ge(z_taken[t], N_IN + 16)
                out_product(qa_bank[t], t, wq_hi, wq_lo, quarter, range(KT - 1))
            pe.wait_ge(mg_lo_done, KT)
            for t in range(NB):
                if t >= 4:
                    pe.wait_ge(qa_taken, t - 3)
                out_product(qa_bank[t % 4], t, wq_hi, wq_lo, quarter, range(KT - 1 if t < 2 else 0, KT)).then_inc(qa_made, 1)
            pe.wait_ge(w_lo_done, N_IN + 24)
            pe.wait_ge(ob_taken, N_SUMS * PAIRS)
            for t in range(NB):
                dst = (pc, pa, pb)[t % 3]
                if t == 2:
                    pe.wait_ge(qa_taken, NB)
                if t >= 3:
                    pe.wait_ge(pb_taken, 2 * t - 4)
                out_product(dst[:, 0, :], t, oa_hi, oa_lo, slice(2 * P, 6 * P)).then_inc(pb_made, 1)
                out_product(dst[:, 1, 0:2 * P], t, oa_hi, oa_lo, slice(6 * P, 8 * P)).then_inc(pb_made, 1)

        @block.scalar
        def _(act):
            act.wait_ge(const_in, 48)
            def square(t):
                act.wait_ge(x_loaded[t], 16)
                if t:
                    act.wait_ge(ss_act, ACT_SQUARES.index(t))
                nc.scalar.activation(x_sq[:], x_in[:, t, :], ACT.Square, accum_out=x_ss[:, t:t + 1]).then_inc(ss_act, 1)

            def normalise(hf):
                ts = slice(4 * hf, 4 * hf + 4)
                act.wait_ge(ss_act, 2 * hf + 2)
                act.wait_ge(ss_dve, 2 * hf + 2)
                nc.scalar.activation(x_rms[:, ts], x_ss[:, ts], ACT.Sqrt, scale=1.0 / D_MODEL, bias=col[:, 2:3]).then_inc(rms_done, 1)
                act.wait_ge(rs_done, hf + 1)
                for t in (4 * hf + 2, 4 * hf + 3):
                    nc.scalar.activation(x_in[:, t, :], x_in[:, t, :], ACT.Copy, scale=x_rs[:, t:t + 1]).then_inc(xn_done, 1)

            def take_x(u):
                k, hf = u % KT, u // KT
                act.wait_ge(xt_made, u + 1)
                nc.scalar.activation(h_hi[:, k, HALF * hf:HALF * (hf + 1)], (pa, pb)[u // 2 % 2][:, u % 2, :], ACT.Copy,
                                     scale=norm_w[:, k:k + 1]).then_inc(h_hi_done, 1)

            def split_hi(n, s):
                if not isinstance(n, int) or n >= 2:
                    act.wait_ge(z_made[1], n - 1)
                act.wait_ge(w_loaded[s], w_count(n, s))
                nc.scalar.activation(w_hi[s][:], w_stage[s][:], ACT.Copy).then_inc(w_hi_done, 1)

            def w_count(n, s):
                return 16 * (n // 2 + 1) if isinstance(n, int) else (n - s) * 8 + 16

            def take(n, hf, dst, func, **kw):
                act.wait_ge(z_made[hf], n + 1)
                nc.scalar.activation(dst[:, HALF * hf:HALF * (hf + 1)], z_ps[hf][:], func, **kw).then_inc(z_taken[hf], 1)

            square(0)
            square(2)
            normalise(0)
            split_hi(0, 0)
            for u in range(KT):
                take_x(u)
                if u in (3, 7):
                    square(6 + u // 7)
            normalise(1)
            for u in range(KT, 2 * KT):
                take_x(u)
            act.wait_ge(lb_step, 3)
            nc.scalar.activation(lb[:, 1:3, :], lb[:, 1:3, :], ACT.Exp).then_inc(lb_step, 1)

            def level_exp(i, u):
                act.wait_ge(d_done, i * 7 + u + 1)
                nc.scalar.activation(ee[u % 2][:], dd[u % 2][:], ACT.Exp).then_inc(e_done, 1)

            def hgrn_cur(i, slot):
                if slot == 2:
                    act.wait_ge(f_done, i + 1)
                    nc.scalar.activation(lf[:], ff[:], ACT.Ln).then_inc(ln_done, 1)
                if slot == 3:
                    act.wait_ge(b_done, i + 1)
                    nc.scalar.activation(eb[:], bb[:], ACT.Exp).then_inc(eb_done, 1)
                if 4 <= slot <= 10:
                    level_exp(i, slot - 4)
                if slot == 6:
                    act.wait_ge(kt_made, i + 1)
                    for hf in range(2):
                        nc.scalar.activation(k_tok[:, 4 * hf:4 * hf + 4, :], pa[:, hf, :].rearrange("p (c k) -> p c k", k=P), ACT.Copy).then_inc(kt_taken, 1)
                if slot == 8:
                    act.wait_ge(vt_made, i + 1)
                    for hf in range(2):
                        nc.scalar.activation(vv[:, 4 * hf:4 * hf + 4, :], pa[:, hf, :].rearrange("p (c k) -> p c k", k=P), ACT.Copy).then_inc(v_taken, 1)

            def hgrn_tail(i, slot):
                if slot == 2:
                    act.wait_ge(pv_made, i)
                    for hf in range(2):
                        nc.scalar.activation(o_sq[:, HALF * hf:HALF * (hf + 1)], pc[:, hf, :], ACT.Square).then_inc(sq_done, 1)
                if slot == 4:
                    act.wait_ge(ms_made, i)
                    for hf in range(2):
                        nc.scalar.activation(o_rs[:, HALF * hf:HALF * (hf + 1)], pa[:, hf, :], ACT.Ln, bias=col[:, 2:3]).then_inc(ms_ln, 1)
                    act.wait_ge(ms_ln, i * 2)
                    nc.scalar.activation(o_rs[:], o_rs[:], ACT.Exp, scale=-0.5).then_inc(ors_done, 1)

            evacs = ((ff, ACT.Sigmoid), (qq, ACT.Silu), (vt, ACT.Copy), (gg, ACT.Silu), (gate[0], ACT.Sigmoid), (gate[1], ACT.Sigmoid))

            def hgrn(i, prev, cur):
                for slot in range(2 * HG_CHUNKS):
                    c, hf = slot // 2, slot % 2
                    if cur and hf == 0:
                        split_hi(i * HG_CHUNKS + c + 1, (c + 1) % 2)
                    if prev:
                        hgrn_tail(i, slot)
                    if cur:
                        hgrn_cur(i, slot)
                        if first(i) and slot == 4:
                            act.wait_ge(rope_step, 1)
                        if first(i) and slot == 6:
                            act.wait_ge(mask_done, MASKS)
                        if slot == 6 and prev:
                            act.wait_ge(oa_done, i)
                        if c >= 4 and hf == 0 and prev:
                            act.wait_ge(gate_stored[c - 4], 16 * i)
                        take(i * HG_CHUNKS + c, hf, *evacs[c])

            hgrn(0, False, True)
            act.wait_ge(rope_step, ROPE_STEPS)
            with act.Fori(1, HEADS) as i:
                hgrn(i, True, True)
            nc.scalar.activation(cos_t[:], cos_t[:], ACT.Sin).then_inc(sin_done, 1)
            nc.scalar.activation(sin_t[:], sin_t[:], ACT.Sin).then_inc(sin_done, 1)

            def attention(i, prev, cur):
                for slot in range(2 * AT_CHUNKS):
                    c, hf = slot // 2, slot % 2
                    n = N_HG + i * AT_CHUNKS + c
                    if cur and hf == 0:
                        split_hi(n + 1, (c + 1) % 2)
                    if first(i):
                        hgrn_tail(HEADS, slot)
                        if slot == 0:
                            act.wait_ge(lvl_made, N_UNIT_HG * HEADS)
                        if slot == 5:
                            act.wait_ge(lvl_taken, N_UNIT_HG * HEADS)
                        if slot == 7:
                            act.wait_ge(oa_done, HEADS)
                        if slot == 12:
                            act.wait_ge(vb_done, 1)
                            act.wait_ge(oa_stored, 16 * HEADS)
                            for s in range(2):
                                act.wait_ge(gate_stored[s], 16 * HEADS)
                    if cur and slot >= 5 and hf == 1 and slot <= 15:
                        j = (slot - 5) // 2
                        act.wait_ge(rope_sum, i * 6 + j + 1)
                        if prev:
                            act.wait_ge(st_made, (i - 1) * N_UNITS + (8, 16, 20)[j // 2])
                        src = roped if j < 4 else qk_full[j % 2]
                        nc.scalar.activation(qk_hi[j // 2][j % 2][:], src[:], ACT.Copy).then_inc(qk_hi_done, 1)
                    if cur and slot in (15, 17, 19):
                        g = (slot - 15) // 2
                        act.wait_ge(avt_made, i * 3 + g + 1)
                        for b in range(2):
                            dst = vb[:, g, 4 * b:4 * b + 4, :].rearrange("p c (x e) -> p c x e", e=EDIM)[:, :, 0:3:2, :]
                            nc.scalar.activation(dst, pb[:, b, :].rearrange("p (c x e) -> p c x e", c=4, x=2), ACT.Copy).then_inc(av_taken, 1)
                    if prev and slot == 13:
                        act.wait_ge(ob_taken, i * N_SUMS)
                        nc.scalar.activation(r_den[0:EDIM, :], acc[0][EDIM:P, :], ACT.Ln).then_inc(den_ln, 1)
                        nc.scalar.activation(r_den[EDIM:P, :], acc[1][0:EDIM, :], ACT.Ln).then_inc(den_ln, 1)
                        act.wait_ge(den_ln, 2 * i)
                        nc.scalar.activation(r_den[:], r_den[:], ACT.Exp, scale=-1.0).then_inc(den_done, 1)
                    if cur:
                        if c < 6:
                            if not first(i) or c >= 2:
                                act.wait_ge(rope_sum, i * 6 + c - 1)
                            take(n, hf, zz[c % 2], ACT.Copy, scale=0.125 if c % 2 == 0 else 1.0)
                        elif c < 9:
                            g = c - 6
                            act.wait_ge(z_made[hf], n + 1)
                            if hf == 0 and (g or prev):
                                act.wait_ge(avt_made, i * 3 + g)
                            if g == 0 and hf == 0 and prev:
                                act.wait_ge(shift_done, i)
                            r = DILATIONS[g]
                            w = HALF // r
                            dst = v_t[:].rearrange("p (r i) -> p r i", r=r)[:, :, w * hf:w * (hf + 1)]
                            nc.scalar.activation(dst, z_ps[hf][:].rearrange("p (i r) -> p r i", r=r), ACT.Copy).then_inc(z_taken[hf], 1)
                        else:
                            if prev and hf == 0:
                                act.wait_ge(ob_done, 2 * i)
                            take(n, hf, s_ag, ACT.Silu)
                    if prev:
                        for u in UNIT_SLOTS.get(slot, ()):
                            act.wait_ge(st_made, (i - 1) * N_UNITS + u + 1)
                            cols = sum(P * k for _, _, k in unit_keys(UNITS[u][0], UNITS[u][2]))
                            if u >= 2:
                                act.wait_ge(pu_made, (i - 1) * N_UNITS + u - 1)
                            nc.scalar.activation(pt[u % 2][:, 0:cols], pb[:, u % 2, 0:cols], ACT.Exp).then_inc(pt_done, 1)
                    if not cur:
                        if 1 <= slot < N_BR:
                            branch_hi(slot - 1)
                        if slot == 12:
                            branch_w_hi(N_IN + 1)
                    if cur and slot == 18:
                        act.wait_ge(mt_made, i + 1)
                        if prev:
                            act.wait_ge(m_stored, 16 * i)
                        nc.scalar.activation(m_t[:], pc[0:2 * GROUPS * NB, 0, 0:P], ACT.Copy, scale=-1.0).then_inc(mt_taken, 1)

            def branch_hi(t):
                if t == 0:
                    act.wait_ge(z_made[1], N_IN)
                if t == HEADS:
                    act.wait_ge(st_made, (PAIRS - 1) * N_UNITS + 16)
                if t == N_BR - 1:
                    act.wait_ge(ob_done, 2 * PAIRS)
                    src = o_b
                else:
                    act.wait_ge(br_loaded[t % 4], 16 * (t // 4 + 1))
                    src = br_in[t % 4]
                dst = oa_hi[:, t, :] if t < HEADS else ob_hi[:, t - HEADS, :]
                nc.scalar.activation(dst, src[:], ACT.Copy).then_inc(br_hi_done, 1)

            def branch_w_hi(n):
                kt = HEADS if n % 2 == 0 else PAIRS
                act.wait_ge(z_made[1], n - 1)
                act.wait_ge(w_loaded[n % 2], w_count(n, n % 2))
                nc.scalar.activation(w_hi[n % 2][:, 0:kt, :], w_stage[n % 2][:, 0:kt, :], ACT.Copy).then_inc(w_hi_done, 1)

            attention(0, False, True)
            with act.Fori(1, PAIRS - 1) as i:
                attention(i, True, True)
            attention(PAIRS - 1, True, True)
            attention(PAIRS, True, False)

            branch_hi(N_BR - 1)

            def split_out_hi(n):
                c = n - N_IN - 16
                act.wait_ge(w_loaded[n % 2], w_count(n, n % 2))
                if c == 2:
                    act.wait_ge(z_made[1], N_IN + 16)
                dst = wq_hi if c < 2 else oa_hi
                nc.scalar.activation(dst[:, :, P * c:P * c + P], w_stage[n % 2][:], ACT.Copy).then_inc(w_hi_done, 1)

            for j in range(KT):
                for b in range(2):
                    n = N_IN + 2 * j + b + 1
                    if N_IN + 1 < n < N_IN + 16:
                        branch_w_hi(n)
                    elif n >= N_IN + 16:
                        split_out_hi(n)
                if j == KT - 1:
                    split_out_hi(N_IN + 17)
                act.wait_ge(mg_sum, j + 1)
                nc.scalar.activation(mg_hi[:, j, :], part[:], ACT.Copy).then_inc(mg_hi_done, 1)
            for c in range(2, 8):
                split_out_hi(N_IN + 16 + c)
            for t in range(NB):
                act.wait_ge(pb_taken, 2 * t + 2)
                nc.scalar.activation(g_in[0][:], yy[:, t, :], ACT.Square, accum_out=o_stat[:, 0, t:t + 1]).then_inc(oss_done, 1)
                act.wait_ge(oss_done, t + 1)
                nc.scalar.activation(o_stat[:, 1, t:t + 1], o_stat[:, 0, t:t + 1], ACT.Sqrt, scale=1.0 / D_MODEL, bias=col[:, 2:3]).then_inc(orms_done, 1)

        @block.vector
        def _(dve):
            dve.wait_ge(lb_loaded, 16)
            nc.vector.tensor_tensor(lb[:, 0, :], lb_in[:, 0, :], lb_in[:, 1, :], ALU.max).then_inc(lb_step, 1)
            dve.wait_ge(lb_step, 1)
            for r in range(2):
                nc.vector.tensor_tensor(lb[:, 1 + r, :], lb_in[:, r, :], lb[:, 0, :], ALU.subtract).then_inc(lb_step, 1)
            dve.wait_ge(const_in, 48)

            def split_lo(n, s):
                dve.wait_ge(w_hi_done, n + 1)
                nc.vector.tensor_tensor(w_lo[s][:], w_stage[s][:], w_hi[s][:].bitcast(f32), ALU.subtract).then_inc(w_lo_done, 1)

            def square(t):
                dve.wait_ge(x_loaded[t], 16)
                n = DVE_SQUARES.index(t)
                if n:
                    dve.wait_ge(ss_dve, n)
                nc.vector.tensor_tensor_reduce(out=dd[1][:], in0=x_in[:, t, :], in1=x_in[:, t, :], scale=1.0, scalar=0.0,
                                               op0=ALU.mult, op1=ALU.add, accum_out=x_ss[:, t:t + 1]).then_inc(ss_dve, 1)

            square(1)
            square(3)
            for hf in range(2):
                ts = slice(4 * hf, 4 * hf + 4)
                dve.wait_ge(rms_done, hf + 1)
                nc.vector.reciprocal(x_rs[:, ts], x_rms[:, ts]).then_inc(rs_done, 1)
                dve.wait_ge(rs_done, hf + 1)
                for t in (4 * hf, 4 * hf + 1):
                    nc.vector.tensor_scalar(x_in[:, t, :], x_in[:, t, :], x_rs[:, t:t + 1], None, ALU.mult).then_inc(xn_done, 1)
                if hf == 0:
                    split_lo(0, 0)
                for u in range(KT * hf, KT * hf + KT):
                    k, ts = u % KT, slice(HALF * hf, HALF * (hf + 1))
                    dve.wait_ge(h_hi_done, u + 1)
                    nc.vector.scalar_tensor_tensor(h_lo[:, k, ts], (pa, pb)[u // 2 % 2][:, u % 2, :], norm_w[:, k:k + 1],
                                                   h_hi[:, k, ts].bitcast(f32), ALU.mult, ALU.subtract).then_inc(h_lo_done, 1)
                    if u in (3, 7):
                        square(4 + u // 7)
            dve.wait_ge(lb_step, 4)
            nc.vector.tensor_tensor(lb[:, 3, :], lb[:, 1, :], lb[:, 2, :], ALU.add).then_inc(lb_step, 1)
            dve.wait_ge(lb_step, 5)
            nc.vector.reciprocal(lb[:, 3, :], lb[:, 3, :]).then_inc(lb_step, 1)
            dve.wait_ge(lb_step, 6)
            nc.vector.tensor_tensor(lb[:, 4, :], lb[:, 1, :], lb[:, 3, :], ALU.mult).then_inc(lb_step, 1)
            dve.wait_ge(lb_step, 7)
            nc.vector.tensor_scalar(lb[:, 5, :], lb[:, 4, :], -1.0, 1.0, ALU.mult, ALU.add).then_inc(lb_step, 1)
            dve.wait_ge(lb_step, 8)
            nc.vector.tensor_scalar(lb[:, 4, :], lb[:, 4, :], TINY, None, ALU.max).then_inc(lb_step, 1)
            dve.wait_ge(lb_step, 9)
            dve.wait_ge(hg_loaded, 32)
            dve.wait_ge(init_done, 3)

            def exponents(i, u):
                if u == 0:
                    b = bb[:].rearrange("p (c t) -> p c t", t=P)
                    nc.vector.tensor_tensor(dd[0][:].rearrange("p (c t) -> p c t", t=P), b[:, :, P - 1:P].to_broadcast([P, NB, P]), b, ALU.subtract).then_inc(d_done, 1)
                    return
                span = LEVELS[u - 1]
                n = HALF // span
                b = bb[:].rearrange("p (n two l) -> p n two l", two=2, l=span)
                mid = b[:, :, 0, span - 1:span].to_broadcast([P, n, span])
                dst = dd[u % 2][:].rearrange("p (two n l) -> p two n l", two=2, l=span)
                nc.vector.tensor_tensor(dst[:, 0], b[:, :, 1, :], mid, ALU.subtract)
                nc.vector.tensor_tensor(dst[:, 1], mid, b[:, :, 0, :], ALU.subtract).then_inc(d_done, 1)

            def level_factors(i, u):
                dve.wait_ge(e_done, i * 7 + u + 1)
                if u == 0:
                    nc.vector.tensor_tensor(k_out[:], kk[:], ee[0][:], ALU.mult).then_inc(k_out_done, 1)
                    return
                span = LEVELS[u - 1]
                s = (u - 1) % 2
                if u >= 3:
                    dve.wait_ge(lvl_made, i * N_UNIT_HG + u)
                e = ee[u % 2][:].rearrange("p (two n l) -> p two n l", two=2, l=span)
                cut = lambda t: t[:].rearrange("p (n two l) -> p n two l", two=2, l=span)
                nc.vector.tensor_tensor(q_lv[s][:].rearrange("p (n l) -> p n l", l=span), cut(qq)[:, :, 1, :], e[:, 0], ALU.mult)
                nc.vector.tensor_tensor(cut(k_lv[s])[:, :, 0, :], cut(kk)[:, :, 0, :], e[:, 1], ALU.mult).then_inc(lv_done, 1)

            def pick(i, j):
                made, taken = value(dve, i * N_UNIT_HG + j + 1), value(dve, i * N_UNIT_HG + j)
                span = LEVELS[j - 2] if j >= 2 else 1
                dve.wait_ge(mask_done, MASKS)
                dve.wait_ge(lvl_made, made)
                if not first(i) or j > 0:
                    dve.wait_ge(lvl_taken, taken)
                if 2 <= j < 4:
                    for g in range(64 // span):
                        rows = slice(2 * span * g, 2 * span * g + span)
                        dst = scores[rows, :, 2 * span * g + span:2 * span * (g + 1)]
                        src = pb[rows, j % 2, :].rearrange("p (c t) -> p c t", t=64)[:, :, span * g:span * (g + 1)]
                        last = nc.vector.tensor_copy(dst, src)
                    last.then_inc(lvl_taken, 1)
                    return
                dst = scores[:].rearrange("p c t -> p (c t)").rearrange("p (n two l) -> p n two l", two=2, l=span)[:, :, int(j != 1), :]
                src = pb[:, j % 2, :].rearrange("p (n l) -> p n l", l=span)
                mask = level_mask[:, j if j < 2 else j - 2, :].rearrange("p (n l) -> p n l", l=span)
                nc.vector.copy_predicated(dst, mask, src).then_inc(lvl_taken, 1)

            def hgrn_cur(i, slot):
                if slot == 2:
                    for s in range(2):
                        dve.wait_ge(z_taken[s], i * HG_CHUNKS + 1)
                    head = bass.ds(i, 1)
                    nc.vector.tensor_scalar(ff[:], ff[:], lb[:, 5, head], lb[:, 4, head], ALU.mult, ALU.add).then_inc(f_done, 1)
                    dve.wait_ge(f_done, i + 1)
                    nc.vector.tensor_scalar(kk[:], ff[:], -1.0, 1.0, ALU.mult, ALU.add).then_inc(k_done, 1)
                    dve.wait_ge(ln_done, i + 1)
                    nc.vector.tensor_tensor_scan(bb[:], reset[:], lf[:], 0.0, ALU.mult, ALU.add).then_inc(b_done, 1)
                    dve.wait_ge(b_done, i + 1)
                if slot == 4:
                    for s in range(2):
                        dve.wait_ge(z_taken[s], i * HG_CHUNKS + 2)
                    if not isinstance(i, int) or i > 0:
                        dve.wait_ge(pv_made, i)
                    dve.wait_ge(eb_done, i + 1)
                    nc.vector.tensor_tensor(q_in[:], qq[:], eb[:], ALU.mult).then_inc(q_in_done, 1)
                if slot == 3:
                    dve.wait_ge(k_done, i + 1)
                    if not first(i):
                        dve.wait_ge(lvl_made, i * N_UNIT_HG)
                    by_two = lambda t, a: t[:].rearrange("p (n two) -> p n two", two=2)[:, :, a]
                    nc.vector.tensor_copy(by_two(k_one, 1), by_two(kk, 1))
                    nc.vector.tensor_tensor(by_two(k_one, 0), by_two(kk, 0), by_two(ff, 1), ALU.mult).then_inc(k_one_done, 1)
                if 4 <= slot <= 10:
                    level_factors(i, slot - 4)
                if 3 <= slot <= 9:
                    exponents(i, slot - 3)
                if slot == 6:
                    pick(i, 0)
                    pick(i, 1)
                elif slot >= 7:
                    pick(i, slot - 5)
                if slot == 10:
                    dve.wait_ge(upd_made, i + 1)
                    for c in range(1, NB):
                        src = pc[:, (c - 1) // 4, P * ((c - 1) % 4):P * ((c - 1) % 4 + 1)]
                        if c == 1:
                            nc.vector.tensor_copy(state[:, c, :], src).then_inc(s_done, 1)
                        else:
                            dve.wait_ge(s_done, i * 7 + c - 1)
                            nc.vector.scalar_tensor_tensor(state[:, c, :], state[:, c - 1, :], eb[:, P * c - 1:P * c], src, ALU.mult, ALU.add).then_inc(s_done, 1)

            def hgrn_tail(i, slot):
                if slot == 0:
                    pick(i - 1, N_UNIT_HG - 1)
                if slot == 5:
                    dve.wait_ge(ors_done, i)
                    if not isinstance(i, int) or i > 1:
                        dve.wait_ge(oa_stored, 16 * i - 16)
                    for hf in range(2):
                        t = slice(HALF * hf, HALF * (hf + 1))
                        last = nc.vector.tensor_tensor(o_a[:, t], pc[:, hf, :], o_rs[:, t], ALU.mult)
                    last.then_inc(on_done, 1)
                    dve.wait_ge(on_done, i)
                    nc.vector.scalar_tensor_tensor(o_a[:], o_a[:], hgw[:], gg[:], ALU.mult, ALU.mult).then_inc(oa_done, 1)

            def hgrn(i, prev, cur):
                for slot in range(2 * HG_CHUNKS):
                    if cur and slot % 2 == 0:
                        split_lo(i * HG_CHUNKS + slot // 2 + 1, (slot // 2 + 1) % 2)
                    if prev:
                        hgrn_tail(i, slot)
                    if cur:
                        hgrn_cur(i, slot)

            hgrn(0, False, True)
            dve.wait_ge(rope_step, ROPE_STEPS)
            with dve.Fori(1, HEADS) as i:
                hgrn(i, True, True)

            def row_max(i, g, m, h):
                u = 2 * (g * 4 + m) + h
                todo = max_queries(g, m)
                for k, (blk, at, before) in enumerate(todo):
                    lo, w = (at, 2 * P) if before else (at if g == 2 else at + P, P)
                    mask = mask_n[:, 2 * P:] if g == 2 else mask_n[:, 2 * P - w:2 * P]
                    at_m = (h * GROUPS + g) * NB + blk
                    done = max_count(u) + k
                    made, written = value(dve, i * 20 + u + 1), value(dve, i * N_MAX + done - 1)
                    dve.wait_ge(mask_done, MASKS)
                    if k == 0:
                        dve.wait_ge(mx_made, made)
                    if not first(i) or done >= 2:
                        dve.wait_ge(mx_taken, written)
                    nc.vector.tensor_tensor_reduce(out=junk[:, done % 2, 0:w], in0=pa[:, h, lo:lo + w], in1=mask, scale=1.0, scalar=NEG,
                                                       op0=ALU.add, op1=ALU.max, accum_out=m_all[:, at_m:at_m + 1]).then_inc(mx_taken, 1)

            def attention(i, prev, cur):
                for slot in range(2 * AT_CHUNKS):
                    c, hf = slot // 2, slot % 2
                    n = N_HG + i * AT_CHUNKS + c
                    if prev:
                        for k in SUM_SLOTS.get(slot, ()):
                            g, h, b = k // 4, k // 2 % 2, k % 2
                            dve.wait_ge(pu_made, (i - 1) * N_UNITS + SUM_AFTER[k] + 1)
                            if g == 0:
                                nc.vector.tensor_copy(acc[h][:, HALF * b:HALF * (b + 1)], pc[:, b, :]).then_inc(ob_taken, 1)
                            else:
                                r = DILATIONS[g]
                                dst = by_residue(acc[h][:], g)[:, r // 2 * b:r // 2 * (b + 1), :]
                                dve.wait_ge(ob_taken, (i - 1) * N_SUMS + k)
                                nc.vector.tensor_tensor(dst, pc[:, b, :].rearrange("p (r i) -> p r i", r=r // 2), dst, ALU.add).then_inc(ob_taken, 1)
                    if cur and hf == 0:
                        split_lo(n + 1, (c + 1) % 2)
                    if first(i):
                        hgrn_tail(HEADS, slot)
                        if slot == 4:
                            dve.wait_ge(sin_done, 2)
                        if slot == 12:
                            dve.wait_ge(oa_stored, 16 * HEADS)
                            for s in range(2):
                                dve.wait_ge(gate_stored[s], 16 * HEADS)
                    if prev and slot == 0:
                        dve.wait_ge(m_loaded, 16 * i)
                        r4 = m_rows[:, 1, :].rearrange("p (r i) -> p i r", r=4)
                        r16 = m_rows[:, 2, :].rearrange("p (r i) -> p i r", r=16)
                        r1 = m_rows[:, 0, :]
                        nc.vector.tensor_tensor(r1.rearrange("p (i r) -> p i r", r=4), r1.rearrange("p (i r) -> p i r", r=4), r4, ALU.min).then_inc(mj_done, 1)
                        dve.wait_ge(mj_done, i)
                        nc.vector.tensor_tensor(shift[:].rearrange("p (i r) -> p i r", r=16), r1.rearrange("p (i r) -> p i r", r=16), r16, ALU.min).then_inc(shift_done, 1)
                    if cur:
                        for g, m in MAX_SLOTS.get(slot - 1, ()):
                            for h in range(2):
                                row_max(i, g, m, h)
                    if cur and 4 <= slot <= 14 and hf == 0:
                        j = (slot - 4) // 2
                        dve.wait_ge(swapped, (i * 6 + j + 1) * 64)
                        nc.vector.tensor_tensor(zz[j % 2][:], zz[j % 2][:], cos_t[:], ALU.mult).then_inc(rope_a, 1)
                        nc.vector.tensor_tensor(z_swap[:], z_swap[:], sin_t[:], ALU.mult).then_inc(rope_b, 1)
                        dve.wait_ge(rope_a, i * 6 + j + 1)
                        dve.wait_ge(rope_b, i * 6 + j + 1)
                        r = DILATIONS[j // 2]
                        nat = lambda t: t[:].rearrange("p (i r) -> p i r", r=r)
                        dst = roped if j < 4 else qk_full[j % 2]
                        if j >= 4 and prev:
                            dve.wait_ge(st_made, i * N_UNITS)
                        nc.vector.tensor_tensor(dst[:].rearrange("p (r i) -> p i r", r=r), nat(zz[j % 2]), nat(z_swap), ALU.add).then_inc(rope_sum, 1)
                    if cur and 5 <= slot <= 11 and hf == 1:
                        j = (slot - 5) // 2
                        dve.wait_ge(qk_hi_done, i * 6 + j + 1)
                        nc.vector.tensor_tensor(qk_lo[j // 2][j % 2][:], roped[:], qk_hi[j // 2][j % 2][:].bitcast(f32), ALU.subtract).then_inc(qk_lo_done, 1)
                    if not cur:
                        if 2 <= slot <= N_BR:
                            branch_lo(slot - 2)
                        if slot == 12:
                            branch_w_lo(N_IN + 1)
                    if prev and slot == 14:
                        dve.wait_ge(den_done, i)
                        nc.vector.tensor_tensor(r_den[:], r_den[:], s_ag[:], ALU.mult).then_inc(den_ag, 1)
                        dve.wait_ge(den_ag, i)
                        if not isinstance(i, int) or i > 1:
                            dve.wait_ge(ob_stored, 16 * i - 16)
                        for h in range(2):
                            rows = slice(EDIM * h, EDIM * (h + 1))
                            nc.vector.tensor_tensor(o_b[rows, :], acc[h][rows, :], r_den[rows, :], ALU.mult).then_inc(ob_done, 1)

            def branch_lo(t):
                dve.wait_ge(br_hi_done, t + 1)
                lo, hi = (oa_lo[:, t, :], oa_hi[:, t, :]) if t < HEADS else (ob_lo[:, t - HEADS, :], ob_hi[:, t - HEADS, :])
                src = o_b if t == N_BR - 1 else br_in[t % 4]
                nc.vector.tensor_tensor(lo, src[:], hi.bitcast(f32), ALU.subtract).then_inc(br_lo_done, 1)

            def branch_w_lo(n):
                kt, s = HEADS if n % 2 == 0 else PAIRS, n % 2
                dve.wait_ge(w_hi_done, n + 1)
                nc.vector.tensor_tensor(w_lo[s][:, 0:kt, :], w_stage[s][:, 0:kt, :], w_hi[s][:, 0:kt, :].bitcast(f32), ALU.subtract).then_inc(w_lo_done, 1)

            attention(0, False, True)
            with dve.Fori(1, PAIRS - 1) as i:
                attention(i, True, True)
            attention(PAIRS - 1, True, True)
            attention(PAIRS, True, False)

            branch_lo(N_BR - 1)
            dve.wait_ge(br_lo_done, N_BR)

            def split_out_lo(n):
                c = n - N_IN - 16
                dve.wait_ge(w_hi_done, n + 1)
                hi, lo = (wq_hi, wq_lo) if c < 2 else (oa_hi, oa_lo)
                cols = slice(P * c, P * c + P)
                nc.vector.tensor_tensor(lo[:, :, cols], w_stage[n % 2][:], hi[:, :, cols].bitcast(f32), ALU.subtract).then_inc(w_lo_done, 1)

            for j in range(KT):
                for b in range(2):
                    n = N_IN + 2 * j + b
                    if N_IN + 1 < n + 1 < N_IN + 16:
                        branch_w_lo(n + 1)
                    elif n + 1 >= N_IN + 16:
                        split_out_lo(n + 1)
                    dve.wait_ge(g_loaded[b], 16 * (j + 1))
                    if b == 0 and j:
                        dve.wait_ge(mg_lo_done, j)
                    for hf in range(2):
                        t = slice(HALF * hf, HALF * (hf + 1))
                        dve.wait_ge(z_made[hf], n + 1)
                        if b == 0:
                            nc.vector.tensor_tensor(part[:, t], z_ps[hf][:], g_in[0][:, t], ALU.mult).then_inc(z_taken[hf], 1)
                        else:
                            nc.vector.tensor_tensor(g_in[1][:, t], pa[:, hf, :], g_in[1][:, t], ALU.mult).then_inc(z_taken[hf], 1)
                if j == KT - 1:
                    split_out_lo(N_IN + 17)
                for hf in range(2):
                    dve.wait_ge(z_taken[hf], N_IN + 2 * j + 2)
                nc.vector.tensor_tensor(part[:], part[:], g_in[1][:], ALU.add).then_inc(mg_sum, 1)
                dve.wait_ge(mg_hi_done, j + 1)
                nc.vector.tensor_tensor(mg_lo[:, j, :], part[:], mg_hi[:, j, :].bitcast(f32), ALU.subtract).then_inc(mg_lo_done, 1)
            for t in range(NB):
                dve.wait_ge(qa_made, t + 1)
                dve.wait_ge(y_loaded[t], 16)
                nc.vector.tensor_tensor(yy[:, t, 0:2 * P], (z_ps[t % 4][:, 0:2 * P] if t % 4 < 2 else pb[:, t % 2, 0:2 * P]), yy[:, t, 0:2 * P], ALU.add).then_inc(qa_taken, 1)
                if t < 6:
                    split_out_lo(N_IN + 18 + t)
            dve.wait_ge(fnw_loaded, 16)
            for t in range(NB + 1):
                if t < NB:
                    src = (pc, pa, pb)[t % 3]
                    dve.wait_ge(pb_made, 2 * t + 1)
                    nc.vector.tensor_tensor(yy[:, t, 2 * P:6 * P], src[:, 0, :], yy[:, t, 2 * P:6 * P], ALU.add).then_inc(pb_taken, 1)
                    dve.wait_ge(pb_made, 2 * t + 2)
                    nc.vector.tensor_tensor(yy[:, t, 6 * P:], src[:, 1, 0:2 * P], yy[:, t, 6 * P:], ALU.add).then_inc(pb_taken, 1)
                if t:
                    dve.wait_ge(orms_done, t)
                    nc.vector.reciprocal(o_stat[:, 2, t - 1:t], o_stat[:, 1, t - 1:t]).then_inc(ors2_done, 1)
                    dve.wait_ge(ors2_done, t)
                    nc.vector.scalar_tensor_tensor(yy[:, t - 1, :], yy[:, t - 1, :], o_stat[:, 2, t - 1:t], fnw[:], ALU.mult, ALU.mult).then_inc(out_done, 1)


def kernel(**inputs):
    import concourse.bacc as bacc
    from concourse.bass_utils import run_bass_kernel_spmd

    f = {k: np.asarray(v) for k, v in inputs.items()}
    w = f["w_in"][0].reshape(KT, P, -1)
    arrays = {
        "x": f["x"][0],
        "positions": f["positions"],
        "norm_w": f["norm_w"][0].reshape(KT, P).T,
        "w_in": np.stack([w[:, :, c:c + P].transpose(1, 0, 2) for c in chunk_columns()]),
        "lb_logits": f["lb_logits"].reshape(2, HEADS, P).transpose(2, 0, 1),
        "hgrn_norm_w": f["hgrn_norm_w"][0].reshape(P, 1),
        "w_a": f["w_branch_a"][0].reshape(8, P, 8, P).transpose(2, 1, 0, 3),
        "w_b": f["w_branch_b"][0].reshape(4, P, 8, P).transpose(2, 1, 0, 3),
        "w_out": f["w_out"][0].reshape(8, P, 8, P).transpose(2, 1, 0, 3),
        "final_norm_w": f["final_norm_w"].reshape(1, D_MODEL),
    } | shape_constants()
    arrays = {k: np.ascontiguousarray(v) for k, v in arrays.items()}
    nc = bacc.Bacc("TRN2", target_bir_lowering=False, num_devices=1, dynamic_dma_scratch_size=1024)
    d = {k: nc.dram_tensor(k, v.shape, mybir.dt.from_np(v.dtype), kind="ExternalInput").ap() for k, v in arrays.items()}
    out = nc.dram_tensor("out", (SEQ, D_MODEL), mybir.dt.float32, kind="ExternalOutput").ap()
    build(nc, d, out)
    r = run_bass_kernel_spmd(nc, [arrays], core_ids=[0])
    return r.results[0]["out"].reshape(1, SEQ, D_MODEL)
```

```python
import numpy as np
from contextlib import ExitStack

import concourse.bass as bass
from concourse import mybir

P = 128
D_MODEL = 1024
SEQ = 1024
KT = D_MODEL // P
HEADS = 8
NB = SEQ // P
HALF = SEQ // 2
GROUPS = 3
DILATIONS = (1, 4, 16)
PAIRS = 4
EDIM = 64
HG_CHUNKS = 6
AT_CHUNKS = 10
N_HG = HEADS * HG_CHUNKS
N_AT = PAIRS * AT_CHUNKS
N_IN = N_HG + N_AT
LEVELS = (64, 32, 16, 8, 4, 2)
EPS = 1e-6
NEG = -1e30
ROPE_THETA = 10000.0
TINY = 2.0 ** -64


def chunk_columns():
    hq, hf, hi, hg = (n * D_MODEL for n in range(4))
    qkv = 4 * D_MODEL
    att = GROUPS * 8 * EDIM
    ag = qkv + 3 * att
    gates = ag + 8 * EDIM
    cols = []
    for h in range(HEADS):
        cols += [hf + P * h, hq + P * h, hi + P * h, hg + P * h, gates + P * h, gates + D_MODEL + P * h]
    for p in range(PAIRS):
        for g in range(GROUPS):
            cols += [qkv + s * att + g * 512 + P * p for s in (0, 1)]
        cols += [qkv + 2 * att + g * 512 + P * p for g in range(GROUPS)]
        cols += [ag + P * p]
    return cols


def shape_constants():
    s = np.arange(P)[:, None]
    level = np.zeros((2 + len(LEVELS[2:]), P, P), np.float32)
    c = np.arange(64)[None, :]
    level[0] = np.tile((s == 2 * c) | (s == 2 * c + 1), (1, 2))
    level[1] = np.tile(s == 2 * c, (1, 2))
    for j, span in enumerate(LEVELS[2:]):
        t = (c // span) * 2 * span + span + c % span
        level[j + 2] = np.tile((t // (2 * span) == s // (2 * span)) & (s % (2 * span) < span), (1, 2))
    i = np.arange(P)[None, :]
    own = np.where(i >= s, 0.0, NEG)
    after = np.where(s >= i, 0.0, NEG)
    same = np.where((i >= s) & (i // 64 == s // 64), 0.0, NEG)
    mask_t = np.concatenate([own, after, own, same], 1).astype(np.float32)
    mask_n = np.concatenate([after.T, own.T, same.T], 1).astype(np.float32)
    reset = np.ones((P, SEQ), np.float32)
    reset[:, ::P] = 0.0
    inv = (ROPE_THETA ** (-np.arange(0, EDIM, 2, dtype=np.float32) / np.float32(EDIM))).astype(np.float32)
    sign = np.where(np.arange(P) % EDIM < EDIM // 2, -1.0, 1.0)
    col = np.stack([np.tile(inv, 4), sign, np.full(P, EPS), np.full(P, 1.0 / P)], 1).astype(np.float32)
    sel = np.zeros((2, 2, P), np.float32)
    sel[0, 0] = sel[1, 1] = 1.0
    return {
        "c_level": np.ascontiguousarray(level.transpose(1, 0, 2)),
        "c_mask_t": mask_t, "c_mask_n": mask_n, "c_reset": reset, "c_col": col,
        "c_ident": np.eye(P, dtype=np.float32), "c_sel": sel,
    }



def build(nc, d, out):
    f32, f32r, bf16 = mybir.dt.float32, mybir.dt.float32r, mybir.dt.bfloat16
    u8, i32 = mybir.dt.uint8, mybir.dt.int32
    ACT = mybir.ActivationFunctionType
    ALU = mybir.AluOpType
    ctx = ExitStack()
    with ctx:
        sem = lambda name: ctx.enter_context(nc.semaphore(name))

        top = [0]

        def place(name, shape, dt=f32):
            n = int(np.prod(shape[1:])) * {f32: 4, f32r: 4, i32: 4, bf16: 2, u8: 1}[dt]
            t = nc.alloc_sbuf_tensor_at(name, shape, dt, offset=top[0])
            top[0] += (n + 31) // 32 * 32
            assert top[0] <= nc.sbuf_usable_end // 32 * 32, (name, top[0])
            return t

        top[0] = (nc.sbuf_base + 31) // 32 * 32
        ident = place("ident", [P, P])
        col = place("col", [P, 4])
        norm_w = place("norm_w", [P, KT])
        w_stage = [place(f"w_stage{s}", [P, KT, P]) for s in range(2)]
        w_hi_at = top[0]
        w_hi = [place(f"w_hi{s}", [P, KT, P], f32r) for s in range(2)]
        w_lo = [place(f"w_lo{s}", [P, KT, P], f32r) for s in range(2)]
        top[0] = w_hi_at
        out_stages = w_stage + [place(f"out_stage{s}", [P, KT, P]) for s in range(4)]
        cos_t = place("cos_t", [P, SEQ])
        sin_t = place("sin_t", [P, SEQ])
        mask_n = place("mask_n", [P, 3 * P])
        mask_b = place("mask_b", [P, 4 * P], bf16)
        ident_b = place("ident_b", [P, P], bf16)
        sel = place("sel", [2, 2, P], f32r)
        shift = place("shift", [2, SEQ], f32r)
        x_ss = place("x_ss", [P, NB])
        warm = place("warm", [P, 1])
        x_rms = place("x_rms", [P, NB])
        x_rs = place("x_rs", [P, NB])
        h_hi = place("h_hi", [P, KT, SEQ], f32r)
        h_lo = place("h_lo", [P, KT, SEQ], f32r)
        phase_base = top[0]
        level_mask = place("level_mask", [P, 6, HALF], u8)
        reset = place("reset", [P, SEQ])
        lb_in = place("lb_in", [P, 2, HEADS])
        lb = place("lb", [P, 6, HEADS])
        hgw = place("hgw", [P, 1])
        inv128 = place("inv128", [P, P], f32r)
        ff = place("ff", [P, SEQ])
        kk = place("kk", [P, SEQ])
        lf = place("lf", [P, SEQ])
        bb = place("bb", [P, SEQ])
        qq = place("qq", [P, SEQ])
        vt = place("vt", [P, SEQ])
        vv = place("vv", [P, NB, P])
        gg = place("gg", [P, SEQ])
        dd = [place(f"dd{s}", [P, SEQ]) for s in range(2)]
        ee = [place(f"ee{s}", [P, SEQ]) for s in range(2)]
        q_lv = [place(f"q_lv{s}", [P, HALF]) for s in range(2)]
        k_lv = [place(f"k_lv{s}", [P, SEQ]) for s in range(2)]
        k_one = place("k_one", [P, SEQ])
        eb = place("eb", [P, SEQ])
        q_in = place("q_in", [P, SEQ])
        late_base = top[0]
        k_out = place("k_out", [P, SEQ])
        k_tok = place("k_tok", [P, NB, P])
        scores = place("scores", [P, NB, P])
        state = place("state", [P, NB, P])
        o_sq = place("o_sq", [P, SEQ])
        sq_at = top[0]
        o_rs = place("o_rs", [P, SEQ])
        o_a = place("o_a", [P, SEQ])
        top[0] = sq_at
        sq_lo = place("sq_lo", [P, SEQ], f32r)
        sq_hi = place("sq_hi", [P, SEQ], f32r)
        gate = [place(f"gate{s}", [P, SEQ]) for s in range(2)]

        top[0] = late_base
        x_in = place("x_in", [P, NB, D_MODEL])
        x_sq = lf
        level_in, mask_t_in, sel_in = gg, vv, vv
        pos_in, turns, less = vt, o_sq, o_a

        top[0] = phase_base
        q_st = [[None, None], [None, None]]
        for g, h in ((0, 0), (1, 0), (1, 1), (0, 1)):
            q_st[g][h] = place(f"q_st{g}{h}", [P, SEQ], f32r)
        k_dup = [[place(f"k_dup{g}{h}", [P, SEQ], f32r) for h in range(2)] for g in range(2)]
        k_lo = [place(f"k_lo{g}", [P, SEQ], f32r) for g in range(2)]
        qk_hi = [place(f"qk_hi{s}", [P, SEQ], f32r) for s in range(2)]
        qk_full = [place(f"qk_full{s}", [P, SEQ]) for s in range(2)]
        zz = [place(f"zz{s}", [P, SEQ]) for s in range(2)]
        z_swap = place("z_swap", [P, SEQ])
        roped = place("roped", [P, SEQ])
        vb = place("vb", [P, GROUPS, NB, 3 * EDIM])
        m_all = place("m_all", [P, 2 * GROUPS * NB])
        m_t = place("m_t", [2 * GROUPS * NB, P])
        junk = place("junk", [P, 2, 2 * P])
        pt_at = top[0]
        pt = [place(f"pt{s}", [P, HALF]) for s in range(2)]
        acc = [place(f"acc{h}", [P, SEQ]) for h in range(2)]
        s_ag = place("s_ag", [P, SEQ])
        o_b = place("o_b", [P, SEQ])
        v_t_at = top[0]
        v_t = place("v_t", [P, SEQ])
        top[0] = pt_at
        r_den = place("r_den", [P, SEQ])
        top[0] = pt_at
        m_rows = place("m_rows", [2, GROUPS, SEQ])
        oa_hi, oa_lo = h_hi, h_lo
        top[0] = phase_base
        ob_hi = place("ob_hi", [P, PAIRS, SEQ], f32r)
        ob_lo = place("ob_lo", [P, PAIRS, SEQ], f32r)
        mg_hi = place("mg_hi", [P, KT, SEQ], f32r)
        mg_lo = place("mg_lo", [P, KT, SEQ], f32r)
        wq_hi = place("wq_hi", [P, KT, 2 * P], f32r)
        wq_lo = place("wq_lo", [P, KT, 2 * P], f32r)
        assert top[0] <= v_t_at
        top[0] = v_t_at
        part = place("part", [P, SEQ])
        o_stat = place("o_stat", [P, 3, NB])
        g_in = [cos_t, sin_t]
        br_in = [cos_t, sin_t, zz[0], zz[1]]
        top[0] = phase_base
        yy = place("yy", [P, NB, D_MODEL])
        fnw = part

        z_ps = [ctx.enter_context(nc.psum_tensor(f"z_ps{s}", [P, HALF], f32)) for s in range(2)]
        pa, pb, pc = (ctx.enter_context(nc.psum_tensor(n, [P, 2, HALF], f32)) for n in ("pa", "pb", "pc"))

        gate_d = nc.dram_tensor("gate_d", [2, HEADS, P, SEQ], f32).ap()
        o_a_d = nc.dram_tensor("o_a_d", [HEADS, P, SEQ], f32).ap()

        o_b_d = nc.dram_tensor("o_b_d", [PAIRS, P, SEQ], f32).ap()
        m_d = nc.dram_tensor("m_d", [PAIRS, 2 * GROUPS * NB, P], f32).ap()

        col_in = sem("col_in")
        const_in, lb_loaded, hg_loaded, pos_loaded, mask_loaded = (sem(n) for n in ("const_in", "lb_loaded", "hg_loaded", "pos_loaded", "mask_loaded"))
        x_loaded = [sem(f"x_loaded{t}") for t in range(NB)]
        ss_act, ss_dve, rms_done, rs_done, xn_done = (sem(n) for n in ("ss_act", "ss_dve", "rms_done", "rs_done", "xn_done"))
        xt_made, h_hi_done, h_lo_done = sem("xt_made"), sem("h_hi_done"), sem("h_lo_done")
        w_loaded = [sem(f"w_loaded{s}") for s in range(2)]
        w_hi_done, w_lo_done = sem("w_hi_done"), sem("w_lo_done")
        z_made = [sem(f"z_made{s}") for s in range(2)]
        z_taken = [sem(f"z_taken{s}") for s in range(2)]
        mask_done = sem("mask_done")
        lb_step, init_done = sem("lb_step"), sem("init_done")
        f_done, k_done, ln_done, b_done = sem("f_done"), sem("k_done"), sem("ln_done"), sem("b_done")
        eb_done, d_done, e_done = sem("eb_done"), sem("d_done"), sem("e_done")
        q_in_done, k_one_done, lv_done = sem("q_in_done"), sem("k_one_done"), sem("lv_done")
        k_out_done, kt_made, kt_taken = sem("k_out_done"), sem("kt_made"), sem("kt_taken")
        vt_made, v_taken, upd_made = sem("vt_made"), sem("v_taken"), sem("upd_made")
        lvl_made, lvl_taken, s_done = sem("lvl_made"), sem("lvl_taken"), sem("s_done")
        pv_made, sq_done, ms_made, ms_ln = sem("pv_made"), sem("sq_done"), sem("ms_made"), sem("ms_ln")
        ors_done, on_done, oa_done = sem("ors_done"), sem("on_done"), sem("oa_done")
        sq_lo_done, oa_stored = sem("sq_lo_done"), sem("oa_stored")
        gate_stored = [sem(f"gate_stored{s}") for s in range(2)]

        rope_step, sin_done = sem("rope_step"), sem("sin_done")
        swapped, rope_a, rope_b, rope_sum = sem("swapped"), sem("rope_a"), sem("rope_b"), sem("rope_sum")
        qk_hi_done, qk_lo_done, k_dupped = sem("qk_hi_done"), sem("qk_lo_done"), sem("k_dupped")
        avt_made, av_taken = sem("avt_made"), sem("av_taken")
        mx_made, mx_taken, mt_made, mt_taken = sem("mx_made"), sem("mx_taken"), sem("mt_made"), sem("mt_taken")
        m_stored, m_loaded, mj_done, shift_done = sem("m_stored"), sem("m_loaded"), sem("mj_done"), sem("shift_done")
        st_made, pt_done, pu_made = sem("st_made"), sem("pt_done"), sem("pu_made")
        ob_taken = sem("ob_taken")
        den_ln, den_done, den_ag, ob_done, ob_stored = sem("den_ln"), sem("den_done"), sem("den_ag"), sem("ob_done"), sem("ob_stored")
        br_loaded = [sem(f"br_loaded{s}") for s in range(4)]
        br_hi_done, br_lo_done = sem("br_hi_done"), sem("br_lo_done")
        g_loaded = [sem(f"g_loaded{s}") for s in range(2)]
        mg_sum, mg_hi_done, mg_lo_done = sem("mg_sum"), sem("mg_hi_done"), sem("mg_lo_done")
        y_loaded = [sem(f"y_loaded{t}") for t in range(NB)]
        fnw_loaded = sem("fnw_loaded")
        wo_loaded = [sem(f"wo_loaded{c}") for c in range(2, 8)]
        qa_made, qa_taken, pb_made, pb_taken = sem("qa_made"), sem("qa_taken"), sem("pb_made"), sem("pb_taken")
        oss_done, orms_done, ors2_done, out_done = sem("oss_done"), sem("orms_done"), sem("ors2_done"), sem("out_done")
        out_stored = sem("out_stored")

        block = ctx.enter_context(nc.Block())
        ACT_SQUARES, DVE_SQUARES = (0, 2, 6, 7), (1, 3, 4, 5)
        first = lambda i: isinstance(i, int) and i == 0

        def value(eng, v):
            return v if isinstance(v, int) else eng.to_reg(v)


        UNITS = [(g, h, m) for g in range(GROUPS) for h in range(2) for m in range(4 if g < 2 else 2)]
        N_UNITS = len(UNITS)
        UNIT_SLOTS = {1: (0,), 2: (1, 2, 3), 3: (4, 5), 4: (6, 7), 5: (8, 9), 6: (10, 11), 7: (12, 13), 8: (14, 15),
                      9: (16, 17), 10: (18, 19)}
        SUM_AFTER = [1, 3, 5, 7, 9, 11, 13, 15, 16, 17, 18, 19]
        SUM_SLOTS = {3: (0,), 4: (1,), 5: (2,), 6: (3,), 7: (4,), 8: (5,), 9: (6,), 10: (7, 8), 11: (9, 10), 12: (11,)}
        N_SUMS = len(SUM_AFTER)
        ROPE_STEPS = 22
        MASKS = 10
        N_BR = HEADS + PAIRS
        N_UNIT_HG = 2 + len(LEVELS)
        MAX_SLOTS = {8 + u: ((u // 4, u % 4),) for u in range(8)} | {16: ((2, 0), (2, 1))}
        N_MAX = 2 * GROUPS * NB
        max_count = lambda u: 2 * u if u <= 16 else 32 + 4 * (u - 16)

        def branch_tiles(n):
            return slice(0, HEADS) if n % 2 == 0 else slice(PAIRS * (n // 2 % 2), PAIRS * (n // 2 % 2 + 1))

        def out_stage(c):
            return out_stages[c if c < 6 else c - 6][:]

        max_bank = lambda g, m: pc if (g, m) == (2, 1) else pa

        def unit_keys(g, m):
            if g == 0:
                return [(c, 256 * (c - 2 * m), 2 if c < NB - 1 else 1) for c in (2 * m, 2 * m + 1)]
            if g == 1:
                return [(2 * m, 0, 2), (2 * m + 1, 256, 1)]
            return [(4 * m + c, P * c, 1) for c in range(4)]

        def max_queries(g, m):
            if g == 2:
                return [(4 * m + c, P * c, False) for c in range(4)]
            return [(c, 256 * (c % 2), c > 0 if g == 0 else c % 2 == 1) for c in (2 * m, 2 * m + 1)]

        def by_residue(ap, g):
            return ap.rearrange("p (i r) -> p r i", r=DILATIONS[g])

        @block.sync
        def _(sp):
            def load_w(n, s, src):
                sp.dma_start(w_stage[s][:, 0:src.shape[1], :], src).then_inc(w_loaded[s], 16)

            def load_x(t):
                sp.dma_start(x_in[:, t, :], d["x"][P * t:P * (t + 1), :]).then_inc(x_loaded[t], 16)

            sp.dma_start(lb_in[:], d["lb_logits"]).then_inc(lb_loaded, 16)
            sp.dma_start(col[:], d["c_col"]).then_inc(col_in, 16)
            load_x(0)
            for s, src in ((ident, "c_ident"), (norm_w, "norm_w")):
                sp.dma_start(s[:], d[src]).then_inc(const_in, 16)
            for t in range(1, 4):
                load_x(t)
            load_w(0, 0, d["w_in"][0])
            for t in range(4, NB):
                load_x(t)
            load_w(1, 1, d["w_in"][1])
            sp.dma_start(pos_in[:].bitcast(i32), d["positions"].to_broadcast([P, SEQ])).then_inc(pos_loaded, 16)
            for s, src in ((reset, "c_reset"), (hgw, "hgrn_norm_w")):
                sp.dma_start(s[:], d[src]).then_inc(hg_loaded, 16)
            sp.dma_start(level_in[:, 0:6 * P].rearrange("p (m c) -> p m c", c=P), d["c_level"]).then_inc(mask_loaded, 16)
            sp.dma_start(mask_t_in[:, 0:4, :].rearrange("p a b -> p (a b)"), d["c_mask_t"]).then_inc(mask_loaded, 16)
            sp.dma_start(sel_in[0:2, 4:6, :], d["c_sel"]).then_inc(mask_loaded, 16)
            sp.dma_start(mask_n[:], d["c_mask_n"]).then_inc(mask_loaded, 16)

            def hgrn(i, prev, cur):
                for c in range(HG_CHUNKS):
                    if cur:
                        n = i * HG_CHUNKS + c
                        split = value(sp, n + 1)
                        sp.wait_ge(const_in, 32)
                        sp.wait_ge(w_lo_done, split)
                        sp.dma_start(w_stage[c % 2][:], d["w_in"][bass.ds(n + 2, 1)].rearrange("a p k c -> (a p) k c")).then_inc(w_loaded[c % 2], 16)
                    if prev and c == 1:
                        taken = value(sp, i * HG_CHUNKS)
                        sp.wait_ge(const_in, 32)
                        for s in range(2):
                            sp.wait_ge(z_taken[s], taken)
                        sp.dma_start(gate_d[1, bass.ds(i - 1, 1)].rearrange("a p t -> (a p) t"), gate[1][:]).then_inc(gate_stored[1], 16)
                    if prev and c == 4:
                        sp.wait_ge(const_in, 32)
                        sp.wait_ge(oa_done, i)
                        sp.dma_start(o_a_d[bass.ds(i - 1, 1)].rearrange("a p t -> (a p) t"), o_a[:]).then_inc(oa_stored, 16)
                    if cur and c == 5:
                        taken = value(sp, i * HG_CHUNKS + 5)
                        sp.wait_ge(const_in, 32)
                        for s in range(2):
                            sp.wait_ge(z_taken[s], taken)
                        sp.dma_start(gate_d[0, bass.ds(i, 1)].rearrange("a p t -> (a p) t"), gate[0][:]).then_inc(gate_stored[0], 16)

            hgrn(0, False, True)
            with sp.Fori(1, HEADS) as i:
                hgrn(i, True, True)
            def load_stage(n, s):
                if isinstance(n, int) and n >= N_IN:
                    n -= N_IN
                    if n < 16:
                        src = d["w_a"][n // 2] if n % 2 == 0 else d["w_b"][n // 2]
                    else:
                        src = d["w_out"][n - 16]
                    sp.dma_start(w_stage[s][:, 0:src.shape[1], :], src).then_inc(w_loaded[s], 16)
                else:
                    sp.dma_start(w_stage[s][:], d["w_in"][bass.ds(n, 1)].rearrange("a p k c -> (a p) k c")).then_inc(w_loaded[s], 16)

            def attention(i, prev, cur):
                for c in range(AT_CHUNKS):
                    n = N_HG + i * AT_CHUNKS + c
                    if cur:
                        split = value(sp, n + 1)
                        sp.wait_ge(const_in, 32)
                        sp.wait_ge(w_lo_done, split)
                        load_stage(n + 2, c % 2)
                    if first(i) and c == 1:
                        for s in range(2):
                            sp.wait_ge(z_taken[s], N_HG)
                        sp.dma_start(gate_d[1, HEADS - 1], gate[1][:]).then_inc(gate_stored[1], 16)
                        sp.wait_ge(lvl_made, N_UNIT_HG * HEADS)
                    if first(i) and c == 4:
                        sp.wait_ge(oa_done, HEADS)
                        sp.dma_start(o_a_d[HEADS - 1], o_a[:]).then_inc(oa_stored, 16)
                    if cur and c == 9:
                        if first(i):
                            sp.wait_ge(oa_stored, 16 * HEADS)
                            for s in range(2):
                                sp.wait_ge(gate_stored[s], 16 * HEADS)
                        maxed = value(sp, i + 1)
                        sp.wait_ge(const_in, 32)
                        sp.wait_ge(mt_taken, maxed)
                        sp.dma_start(m_d[bass.ds(i, 1)].rearrange("a m q -> (a m) q"), m_t[:]).then_inc(m_stored, 16)
                        stored, normed = value(sp, 16 * i + 16), value(sp, 2 * i)
                        sp.wait_ge(const_in, 32)
                        sp.wait_ge(m_stored, stored)
                        if prev:
                            sp.wait_ge(ob_done, normed)
                        sp.dma_start(m_rows[:], m_d[bass.ds(i, 1)].rearrange("a (h g b) q -> (a h) g (b q)", h=2, g=GROUPS)).then_inc(m_loaded, 16)
                    if cur and 1 <= c <= 6:
                        taken, rotated = value(sp, n), value(sp, i * 6 + c - 1)
                        sp.wait_ge(const_in, 32)
                        for s in range(2):
                            sp.wait_ge(z_taken[s], taken)
                        if c > 1 or not first(i):
                            sp.wait_ge(rope_sum, rotated)
                        for q in range(4):
                            o = q ^ 1
                            sp.dma_start(z_swap[32 * q:32 * q + 32, :], zz[(c - 1) % 2][32 * o:32 * o + 32, :]).then_inc(swapped, 16)
                    if prev and cur and c == 8:
                        done = value(sp, 2 * i)
                        sp.wait_ge(const_in, 32)
                        sp.wait_ge(ob_done, done)
                        sp.dma_start(o_b_d[bass.ds(i - 1, 1)].rearrange("a p t -> (a p) t"), o_b[:]).then_inc(ob_stored, 16)

            attention(0, False, True)
            with sp.Fori(1, PAIRS - 1) as i:
                attention(i, True, True)
            attention(PAIRS - 1, True, True)

            sp.wait_ge(rope_sum, 6 * PAIRS)
            for t in range(N_BR - 1):
                if t >= 4:
                    sp.wait_ge(br_lo_done, t - 3)
                src = o_a_d[t] if t < HEADS else o_b_d[t - HEADS]
                sp.dma_start(br_in[t % 4][:], src).then_inc(br_loaded[t % 4], 16)
            for j in range(KT):
                n = N_IN + 2 * j
                for c in range(2):
                    sp.wait_ge(w_lo_done, n + c + 1)
                    load_stage(n + c + 2, c)
                    if j == c == 0:
                        sp.wait_ge(br_lo_done, N_BR - 1)
                    if j:
                        sp.wait_ge(mg_sum, 2 * j)
                    sp.dma_start(g_in[c][:], gate_d[c, j]).then_inc(g_loaded[c], 16)

            def load_out(c):
                sp.dma_start(out_stage(c), d["w_out"][c]).then_inc(wo_loaded[c - 2], 16)

            def load_y(t):
                sp.dma_start(yy[:, t, :], d["x"][P * t:P * (t + 1), :]).then_inc(y_loaded[t], 16)

            for c in (6, 7):
                sp.wait_ge(w_lo_done, N_IN + 16 + c - 5)
                load_out(c)
            for s in range(2):
                sp.wait_ge(z_made[s], N_IN + 16)
            load_y(0)
            for c in range(2, 6):
                load_out(c)
                if c % 2:
                    load_y(c // 2)
            for t in range(3, NB):
                load_y(t)
            sp.wait_ge(mg_lo_done, 2 * KT)
            sp.dma_start(fnw[:], d["final_norm_w"].to_broadcast([P, D_MODEL])).then_inc(fnw_loaded, 16)
            for t in range(NB):
                sp.wait_ge(out_done, t + 1)
                sp.dma_start(out[P * t:P * (t + 1), :], yy[:, t, :]).then_inc(out_stored, 16)
            sp.wait_ge(out_stored, 16 * NB)

        @block.gpsimd
        def _(pool):
            for t in k_lv:
                nc.gpsimd.memset(t[:], 0.0).then_inc(init_done, 1)
            nc.gpsimd.memset(inv128[:].bitcast(f32), 1.0 / P).then_inc(init_done, 1)
            for n in range(2):
                pool.wait_ge(w_hi_done, n + 1)
                nc.gpsimd.tensor_tensor(w_lo[n][:], w_stage[n][:], w_hi[n][:].bitcast(f32), ALU.subtract).then_inc(w_lo_done, 1)
            steps = [0]

            def link(ins):
                steps[0] += 1
                ins.then_inc(rope_step, 1)
                pool.wait_ge(rope_step, steps[0])

            pool.wait_ge(const_in, 32)
            pool.wait_ge(col_in, 16)
            pool.wait_ge(pos_loaded, 16)
            link(nc.gpsimd.tensor_copy(cos_t[:], pos_in[:].bitcast(i32)))
            link(nc.gpsimd.tensor_scalar(cos_t[:], cos_t[:], col[:, 0:1], None, ALU.mult))
            pool.wait_ge(mask_loaded, 4 * 16)
            for m in range(6):
                src = level_in[:, P * m:P * (m + 1)].rearrange("p (a c) -> p a c", a=1).to_broadcast([P, 4, P])
                nc.gpsimd.tensor_copy(level_mask[:, m, :].rearrange("p (a c) -> p a c", c=P), src).then_inc(mask_done, 1)
            pool.wait_ge(xt_made, 2 * KT)
            nc.gpsimd.memset(scores[:], 0.0).then_inc(mask_done, 1)
            nc.gpsimd.tensor_copy(mask_b[:], mask_t_in[:, 0:4, :].rearrange("p a b -> p (a b)")).then_inc(mask_done, 1)
            nc.gpsimd.tensor_copy(sel[:], sel_in[0:2, 4:6, :]).then_inc(mask_done, 1)
            nc.gpsimd.tensor_copy(ident_b[:], ident[:]).then_inc(mask_done, 1)

            two_pi = 2 * np.pi
            parts = [6.28125, float(np.float32(np.floor((two_pi - 6.28125) * 2 ** 20) / 2 ** 20))]
            parts.append(float(np.float32(two_pi - parts[0] - parts[1])))
            magic = 1.5 * 2 ** 23
            lim = float(np.nextafter(np.float32(np.pi), np.float32(0)))
            for s, dst in ((0, sin_t), (1, cos_t)):
                link(nc.gpsimd.tensor_scalar(turns[:], cos_t[:], 1.0 / two_pi, 0.25 * s, ALU.mult, ALU.add))
                link(nc.gpsimd.tensor_scalar(turns[:], turns[:], magic, magic, ALU.add, ALU.subtract))
                for n, part_of_turn in enumerate(parts):
                    link(nc.gpsimd.tensor_scalar(less[:], turns[:], -part_of_turn, None, ALU.mult))
                    link(nc.gpsimd.tensor_tensor(dst[:], less[:], (dst if n else cos_t)[:], ALU.add))
                if s:
                    link(nc.gpsimd.tensor_scalar(dst[:], dst[:], float(np.pi / 2), None, ALU.add))
                link(nc.gpsimd.tensor_scalar(dst[:], dst[:], lim, -lim, ALU.min, ALU.max))
                if s == 0:
                    link(nc.gpsimd.tensor_scalar(dst[:], dst[:], col[:, 1:2], None, ALU.mult))
            assert steps[0] == ROPE_STEPS
            pool.wait_ge(pv_made, HEADS)
            pool.wait_ge(lvl_made, N_UNIT_HG * HEADS)
            nc.gpsimd.memset(vb[:], 1.0).then_inc(k_dupped, 1)

            with pool.Fori(0, PAIRS) as i:
                for g in range(2):
                    for h in range(2):
                        split, copied = value(pool, i * 6 + 2 * g + 2), value(pool, i * 4 + 2 * g + h + 1)
                        pool.wait_ge(const_in, 32)
                        pool.wait_ge(qk_hi_done, split)
                        pool.wait_ge(k_dupped, copied)
                        own, other = slice(EDIM * h, EDIM * (h + 1)), slice(EDIM * (1 - h), EDIM * (2 - h))
                        nc.gpsimd.tensor_copy(k_dup[g][h][other, :], k_dup[g][h][own, :].bitcast(f32)).then_inc(k_dupped, 1)

        @block.tensor
        def _(pe):
            def x_transpose(u):
                k, hf = u % KT, u // KT
                if u >= 4:
                    pe.wait_ge(h_lo_done, u - 3)
                for t in range(4):
                    last = nc.tensor.transpose((pa, pb)[u // 2 % 2][:, u % 2, P * t:P * (t + 1)],
                                               x_in[:, 4 * hf + t, P * k:P * (k + 1)], ident[:])
                last.then_inc(xt_made, 1)

            pe.wait_ge(const_in, 32)
            for hf in range(2):
                t = slice(HALF * hf, HALF * (hf + 1))
                pe.wait_ge(xn_done, 4 * hf + 4)
                for k in range(4):
                    x_transpose(KT * hf + k)
                pe.wait_ge(w_lo_done, 1)
                for k in range(KT):
                    pe.wait_ge(h_lo_done, KT * hf + k + 1)
                    nc.tensor.matmul(z_ps[hf][:], w_hi[0][:, k, :], h_hi[:, k, t], start=k == 0, stop=False)
                    nc.tensor.matmul(z_ps[hf][:], w_hi[0][:, k, :], h_lo[:, k, t], start=False, stop=False)
                    last = nc.tensor.matmul(z_ps[hf][:], w_lo[0][:, k, :], h_hi[:, k, t], start=False, stop=k == KT - 1)
                    if k < 4:
                        x_transpose(KT * hf + k + 4)
                last.then_inc(z_made[hf], 1)

            def project(n, s, hf):
                if hf == 0:
                    pe.wait_ge(w_lo_done, n + 1)
                pe.wait_ge(z_taken[hf], n)
                t = slice(HALF * hf, HALF * (hf + 1))
                for k in range(KT):
                    nc.tensor.matmul(z_ps[hf][:], w_hi[s][:, k, :], h_hi[:, k, t], start=k == 0, stop=False)
                    nc.tensor.matmul(z_ps[hf][:], w_hi[s][:, k, :], h_lo[:, k, t], start=False, stop=False)
                    last = nc.tensor.matmul(z_ps[hf][:], w_lo[s][:, k, :], h_hi[:, k, t], start=False, stop=k == KT - 1)
                last.then_inc(z_made[hf], 1)

            def level_product(i, j):
                dst = pb[:, j % 2, :]
                if j >= 2 or not first(i):
                    pe.wait_ge(lvl_taken, i * N_UNIT_HG + (j - 1))
                if j == 0:
                    pe.wait_ge(k_one_done, i + 1)
                    for s in range(2):
                        pe.wait_ge(z_taken[s], i * HG_CHUNKS + 2)
                elif j >= 2:
                    pe.wait_ge(lv_done, i * 6 + (j - 1))
                for c in range(NB):
                    if j < 2:
                        k_side = (k_one, kk)[j][:, P * c:P * c + P]
                        q_side = qq[:, P * c:P * c + P].rearrange("p (n two) -> p n two", two=2)[:, :, 1 - j]
                    else:
                        k_side, q_side = k_lv[j % 2][:, P * c:P * c + P], q_lv[j % 2][:, 64 * c:64 * c + 64]
                    if 2 <= j < 4:
                        span = LEVELS[j - 2]
                        for g in range(64 // span):
                            last = nc.tensor.matmul(dst[2 * span * g:2 * span * g + span, 64 * c + span * g:64 * c + span * (g + 1)],
                                                    k_side[:, 2 * span * g:2 * span * g + span], q_side[:, span * g:span * (g + 1)],
                                                    start=True, stop=True)
                        continue
                    last = nc.tensor.matmul(dst[:, 64 * c:64 * c + 64], k_side, q_side, start=True, stop=True)
                last.then_inc(lvl_made, 1)

            def hgrn_cur(i, slot):
                if slot == 5:
                    pe.wait_ge(k_out_done, i + 1)
                    if not isinstance(i, int) or i > 0:
                        pe.wait_ge(ms_ln, i * 2)
                    for c in range(NB):
                        last = nc.tensor.transpose(pa[:, c // 4, P * (c % 4):P * (c % 4 + 1)], k_out[:, P * c:P * c + P], ident[:])
                    last.then_inc(kt_made, 1)
                    level_product(i, 0)
                    level_product(i, 1)
                elif slot >= 6:
                    level_product(i, slot - 4)
                if slot == 7:
                    pe.wait_ge(kt_taken, i * 2 + 2)
                    for s in range(2):
                        pe.wait_ge(z_taken[s], i * HG_CHUNKS + 3)
                    for c in range(NB):
                        last = nc.tensor.transpose(pa[:, c // 4, P * (c % 4):P * (c % 4 + 1)], vt[:, P * c:P * c + P], ident[:])
                    last.then_inc(vt_made, 1)
                if slot == 9:
                    pe.wait_ge(v_taken, i * 2 + 2)
                    if not isinstance(i, int) or i > 0:
                        pe.wait_ge(on_done, i)
                    for c in range(NB - 1):
                        last = nc.tensor.matmul(pc[:, c // 4, P * (c % 4):P * (c % 4 + 1)], k_tok[:, c, :], vv[:, c, :], start=True, stop=True)
                    last.then_inc(upd_made, 1)

            def hgrn_tail(i, slot):
                if slot == 1:
                    pe.wait_ge(lvl_taken, i * N_UNIT_HG)
                    pe.wait_ge(s_done, i * 7)
                    for c in range(NB):
                        o = pc[:, c // 4, P * (c % 4):P * (c % 4 + 1)]
                        last = nc.tensor.matmul(o, vv[:, c, :], scores[:, c, :], start=True, stop=c == 0)
                        if c:
                            last = nc.tensor.matmul(o, state[:, c, :], q_in[:, P * c:P * c + P], start=False, stop=True)
                    last.then_inc(pv_made, 1)
                if slot == 3:
                    pe.wait_ge(sq_lo_done, i)
                    for hf in range(2):
                        t = slice(HALF * hf, HALF * (hf + 1))
                        nc.tensor.matmul(pa[:, hf, :], inv128[:], sq_hi[:, t], start=True, stop=False)
                        last = nc.tensor.matmul(pa[:, hf, :], inv128[:], sq_lo[:, t], start=False, stop=True)
                    last.then_inc(ms_made, 1)

            pe.wait_ge(init_done, 3)

            def hgrn(i, prev, cur):
                for slot in range(2 * HG_CHUNKS):
                    if cur:
                        if not first(i) or slot >= 2:
                            project(i * HG_CHUNKS + slot // 2, slot // 2 % 2, slot % 2)
                        hgrn_cur(i, slot)
                    if prev:
                        hgrn_tail(i, slot)

            hgrn(0, False, True)
            with pe.Fori(1, HEADS) as i:
                hgrn(i, True, True)

            def maxima(i, g, m, h):
                u = 2 * (g * 4 + m) + h
                rows = slice(EDIM * h, EDIM * (h + 1))
                if max_bank(g, m) is pc:
                    if not first(i):
                        pe.wait_ge(ob_taken, i * N_SUMS)
                elif u >= 2:
                    pe.wait_ge(mx_taken, i * N_MAX + max_count(u - 1))
                elif not first(i):
                    pe.wait_ge(mx_taken, i * N_MAX)
                pe.wait_ge(qk_hi_done, i * 6 + 2 * g + 2)
                for blk, at, before in max_queries(g, m):
                    lo = blk - 1 if before else blk
                    at += 0 if before or g == 2 else P
                    q_hi, k_hi = (q_st[g][h], k_dup[g][h]) if g < 2 else qk_hi
                    last = nc.tensor.matmul(max_bank(g, m)[:, h, at:at + P * (blk + 1 - lo)], q_hi[rows, P * blk:P * blk + P],
                                            k_hi[rows, P * lo:P * blk + P], start=True, stop=True)
                last.then_inc(mx_made, 1)

            def scores_t(i, u):
                g, h, m = UNITS[u]
                rows = slice(EDIM * h, EDIM * (h + 1))
                base = (i - 1) * N_UNITS
                if u == 0:
                    pe.wait_ge(shift_done, i)
                    pe.wait_ge(av_taken, i * 6)
                if u >= 2:
                    pe.wait_ge(pt_done, base + u - 1)
                pe.wait_ge(qk_lo_done, i * 4)
                pe.wait_ge(k_dupped, i * 4 + 1)
                pe.wait_ge(rope_sum, i * 6)
                units = unit_keys(g, m)
                cols = sum(P * n for _, _, n in units)
                bank = pb[:, u % 2, 0:cols]
                twice = lambda ap, n: ap.rearrange("p (a c) -> p a c", a=1).to_broadcast([P, n, ap.shape[1]])
                mask = twice(mask_b[:, 3 * P:], 4) if g == 2 else mask_b[:, 0:cols] if cols == 3 * P else twice(mask_b[:, 0:2 * P], 2)
                nc.tensor.matmul(bank, ident_b[:], mask, start=True, stop=False)
                if g == 2:
                    row = shift[:].rearrange("p (i r) -> p r i", r=16)[:, 8 * m:8 * m + 8, :]
                    nc.tensor.matmul(bank, sel[:, h, :], row, start=False, stop=False)
                for blk, at, n in units:
                    dst = pb[:, u % 2, at:at + P * n]
                    ks, qs = slice(P * blk, P * blk + P), slice(P * blk, P * (blk + n))
                    if g == 2:
                        last = nc.tensor.matmul(dst, qk_full[1][rows, ks], qk_full[0][rows, qs], start=False, stop=blk == units[-1][0])
                        continue
                    nc.tensor.matmul(dst, k_dup[g][h][:, ks], q_st[g][h][:, qs], start=False, stop=False)
                    nc.tensor.matmul(dst, k_lo[g][rows, ks], q_st[g][h][rows, qs], start=False, stop=False)
                    row = shift[:, qs]
                    if g == 1:
                        row = shift[:].rearrange("p (n i r) -> p n r i", n=2, r=4)[:, blk % 2:blk % 2 + n, blk // 2, :]
                    last = nc.tensor.matmul(dst, sel[:, h, :], row, start=False, stop=blk == units[-1][0])
                last.then_inc(st_made, 1)

            def weighted(i, u):
                g, h, m = UNITS[u]
                pe.wait_ge(pt_done, (i - 1) * N_UNITS + u + 1)
                made = (i - 1) * N_SUMS
                for blk, at, n in unit_keys(g, m):
                    for q in range(n):
                        bank = (blk + q) // 4
                        opens = (blk + q) % 4 == 0 and q == (1 if g == 0 and blk else 0)
                        closes = (blk + q) % 4 == 3 and q == 0
                        if opens:
                            k = (2 * g + h) * 2 + bank
                            if k >= 2:
                                pe.wait_ge(ob_taken, made + k - 1)
                        last = nc.tensor.matmul(pc[:, bank, P * ((blk + q) % 4):P * ((blk + q) % 4 + 1)], vb[:, g, blk, EDIM * h:EDIM * h + P],
                                                pt[u % 2][:, at + P * q:at + P * q + P], start=opens, stop=closes)
                last.then_inc(pu_made, 1)

            def attention(i, prev, cur):
                for slot in range(2 * AT_CHUNKS):
                    c = slot // 2
                    if cur:
                        project(N_HG + i * AT_CHUNKS + c, c % 2, slot % 2)
                    if first(i):
                        hgrn_tail(HEADS, slot)
                        if slot == 6:
                            pe.wait_ge(on_done, HEADS)
                    if prev:
                        for u in UNIT_SLOTS.get(slot, ()):
                            scores_t(i, u)
                            if u:
                                weighted(i, u - 1)
                        if slot == 11:
                            weighted(i, N_UNITS - 1)
                    if not cur:
                        for hf in range(2):
                            if 3 <= slot < 7:
                                branch(0, 0, hf, (slot - 3,))
                            elif slot == 12:
                                branch(0, 0, hf, (4, 5, 6, 7))
                            elif slot == 13:
                                branch(0, 1, hf, (0, 1, 2))
                    if cur:
                        for g, m in MAX_SLOTS.get(slot, ()):
                            for h in range(2):
                                maxima(i, g, m, h)
                    if cur and slot == 17:
                        maxed, summed = value(pe, i * N_MAX + N_MAX), value(pe, i * N_SUMS)
                        pe.wait_ge(const_in, 32)
                        pe.wait_ge(mx_taken, maxed)
                        if prev:
                            pe.wait_ge(ob_taken, summed)
                        nc.tensor.transpose(pc[0:2 * GROUPS * NB, 0, 0:P], m_all[:], ident[:]).then_inc(mt_made, 1)
                    if cur and slot in (14, 16, 18):
                        g = (slot - 14) // 2
                        for s in range(2):
                            pe.wait_ge(z_taken[s], N_HG + i * AT_CHUNKS + 7 + g)
                        if g:
                            pe.wait_ge(av_taken, i * 6 + 2 * g)
                        for b in range(NB):
                            last = nc.tensor.transpose(pb[:, b // 4, P * (b % 4):P * (b % 4 + 1)], v_t[:, P * b:P * b + P], ident[:])
                        last.then_inc(avt_made, 1)

            def branch(j, b, hf, ks=None):
                n = N_IN + 2 * j + b
                src_hi, src_lo = ((oa_hi, oa_lo), (ob_hi, ob_lo))[b]
                kt = (HEADS, PAIRS)[b]
                t = slice(HALF * hf, HALF * (hf + 1))
                dst = z_ps[hf][:] if b == 0 else pa[:, hf, :]
                for k in ks or range(kt):
                    if j == 0:
                        pe.wait_ge(br_lo_done, HEADS * b + k + 1)
                    if k == 0:
                        pe.wait_ge(w_lo_done, n + 1)
                        pe.wait_ge(z_taken[hf], n - b if j == 0 else n - 1)
                    wk = branch_tiles(n).start + k
                    nc.tensor.matmul(dst, w_hi[b][:, wk, :], src_hi[:, k, t], start=k == 0, stop=False)
                    nc.tensor.matmul(dst, w_hi[b][:, wk, :], src_lo[:, k, t], start=False, stop=False)
                    last = nc.tensor.matmul(dst, w_lo[b][:, wk, :], src_hi[:, k, t], start=False, stop=k == kt - 1)
                if k == kt - 1 and (j, b) != (1, 0):
                    last.then_inc(z_made[hf], 2 if (j, b) == (0, 1) else 1)

            pe.wait_ge(mask_done, MASKS)
            attention(0, False, True)
            with pe.Fori(1, PAIRS - 1) as i:
                attention(i, True, True)
            attention(PAIRS - 1, True, True)
            attention(PAIRS, True, False)

            for hf in range(2):
                branch(1, 0, hf)
            for hf in range(2):
                branch(0, 1, hf, (PAIRS - 1,))
            for j in range(1, KT):
                for b in range(2):
                    for hf in range(2):
                        if (j, b) != (1, 0):
                            branch(j, b, hf)

            def out_product(dst, t, w_h, w_l, cols, ks=range(KT)):
                tt = slice(P * t, P * t + P)
                for k in ks:
                    nc.tensor.matmul(dst, mg_hi[:, k, tt], w_h[:, k, cols], start=k == 0, stop=False)
                    nc.tensor.matmul(dst, mg_hi[:, k, tt], w_l[:, k, cols], start=False, stop=False)
                    last = nc.tensor.matmul(dst, mg_lo[:, k, tt], w_h[:, k, cols], start=False, stop=k == KT - 1)
                return last

            quarter = slice(0, 2 * P)
            pe.wait_ge(w_lo_done, N_IN + 18)
            pe.wait_ge(mg_lo_done, 2 * KT - 2)
            qa_bank = (z_ps[0][:, quarter], z_ps[1][:, quarter], pb[:, 0, quarter], pb[:, 1, quarter])
            for t in range(4):
                if t < 2:
                    pe.wait_ge(z_taken[t], N_IN + 16)
                out_product(qa_bank[t], t, wq_hi, wq_lo, quarter, range(KT - 1))
            pe.wait_ge(mg_lo_done, 2 * KT - 1)
            for t in range(NB):
                if t == 4:
                    pe.wait_ge(mg_lo_done, 2 * KT)
                if t >= 4:
                    pe.wait_ge(qa_taken, t - 3)
                out_product(qa_bank[t % 4], t, wq_hi, wq_lo, quarter, range(KT - 1 if t < 4 else 0, KT)).then_inc(qa_made, 1)
            pe.wait_ge(w_lo_done, N_IN + 22)
            pe.wait_ge(ob_taken, N_SUMS * PAIRS)
            for t in range(NB):
                dst = (pc, pa, pb)[t % 3]
                if t == 2:
                    pe.wait_ge(qa_taken, NB)
                if t >= 3:
                    pe.wait_ge(pb_taken, 2 * t - 4)
                out_product(dst[:, 0, :], t, oa_hi, oa_lo, slice(2 * P, 6 * P)).then_inc(pb_made, 1)
                if t == 0:
                    pe.wait_ge(w_lo_done, N_IN + 24)
                out_product(dst[:, 1, 0:2 * P], t, oa_hi, oa_lo, slice(6 * P, 8 * P)).then_inc(pb_made, 1)

        @block.scalar
        def _(act):
            act.wait_ge(lb_step, 3)
            nc.scalar.activation(lb[:, 1:3, :], lb[:, 1:3, :], ACT.Exp).then_inc(lb_step, 1)
            act.wait_ge(col_in, 16)
            nc.scalar.activation(warm[:], col[:, 2:3], ACT.Sqrt)
            act.wait_ge(const_in, 32)
            def square(t):
                act.wait_ge(x_loaded[t], 16)
                if t:
                    act.wait_ge(ss_act, ACT_SQUARES.index(t))
                nc.scalar.activation(x_sq[:], x_in[:, t, :], ACT.Square, accum_out=x_ss[:, t:t + 1]).then_inc(ss_act, 1)

            def normalise(hf):
                ts = slice(4 * hf, 4 * hf + 4)
                act.wait_ge(ss_act, 2 * hf + 2)
                act.wait_ge(ss_dve, 2 * hf + 2)
                nc.scalar.activation(x_rms[:, ts], x_ss[:, ts], ACT.Sqrt, scale=1.0 / D_MODEL, bias=col[:, 2:3]).then_inc(rms_done, 1)
                split_hi(hf, hf)
                act.wait_ge(rs_done, hf + 1)
                for t in (4 * hf + 3,):
                    nc.scalar.activation(x_in[:, t, :], x_in[:, t, :], ACT.Copy, scale=x_rs[:, t:t + 1]).then_inc(xn_done, 1)

            def take_x(u):
                k, hf = u % KT, u // KT
                act.wait_ge(xt_made, u + 1)
                nc.scalar.activation(h_hi[:, k, HALF * hf:HALF * (hf + 1)], (pa, pb)[u // 2 % 2][:, u % 2, :], ACT.Copy,
                                     scale=norm_w[:, k:k + 1]).then_inc(h_hi_done, 1)

            def split_hi(n, s):
                if not isinstance(n, int) or n >= 2:
                    act.wait_ge(z_made[1], n - 1)
                act.wait_ge(w_loaded[s], w_count(n, s))
                nc.scalar.activation(w_hi[s][:], w_stage[s][:], ACT.Copy).then_inc(w_hi_done, 1)

            def w_count(n, s):
                return 16 * (n // 2 + 1) if isinstance(n, int) else (n - s) * 8 + 16

            def take(n, hf, dst, func, **kw):
                act.wait_ge(z_made[hf], n + 1)
                nc.scalar.activation(dst[:, HALF * hf:HALF * (hf + 1)], z_ps[hf][:], func, **kw).then_inc(z_taken[hf], 1)

            square(0)
            square(2)
            normalise(0)
            for u in range(KT):
                take_x(u)
                if u in (2, 5):
                    square(6 + u // 5)
            normalise(1)
            for u in range(KT, 2 * KT):
                take_x(u)

            def level_exp(i, u):
                act.wait_ge(d_done, i * 7 + u + 1)
                nc.scalar.activation(ee[u % 2][:], dd[u % 2][:], ACT.Exp).then_inc(e_done, 1)

            def hgrn_cur(i, slot):
                if slot == 2:
                    act.wait_ge(f_done, i + 1)
                    nc.scalar.activation(lf[:], ff[:], ACT.Ln).then_inc(ln_done, 1)
                if slot == 3:
                    act.wait_ge(b_done, i + 1)
                    nc.scalar.activation(eb[:], bb[:], ACT.Exp).then_inc(eb_done, 1)
                if 4 <= slot <= 10:
                    level_exp(i, slot - 4)
                if slot == 6:
                    act.wait_ge(kt_made, i + 1)
                    for hf in range(2):
                        nc.scalar.activation(k_tok[:, 4 * hf:4 * hf + 4, :], pa[:, hf, :].rearrange("p (c k) -> p c k", k=P), ACT.Copy).then_inc(kt_taken, 1)
                if slot == 8:
                    act.wait_ge(vt_made, i + 1)
                    for hf in range(2):
                        nc.scalar.activation(vv[:, 4 * hf:4 * hf + 4, :], pa[:, hf, :].rearrange("p (c k) -> p c k", k=P), ACT.Copy).then_inc(v_taken, 1)

            def hgrn_tail(i, slot):
                if slot == 2:
                    act.wait_ge(rope_step, ROPE_STEPS)
                    act.wait_ge(pv_made, i)
                    if not isinstance(i, int) or i > 1:
                        act.wait_ge(oa_stored, 16 * i - 16)
                    for hf in range(2):
                        t = slice(HALF * hf, HALF * (hf + 1))
                        nc.scalar.activation(sq_hi[:, t], pc[:, hf, :], ACT.Square)
                        nc.scalar.activation(o_sq[:, t], pc[:, hf, :], ACT.Square).then_inc(sq_done, 1)
                if slot == 4:
                    act.wait_ge(ms_made, i)
                    for hf in range(2):
                        nc.scalar.activation(o_rs[:, HALF * hf:HALF * (hf + 1)], pa[:, hf, :], ACT.Ln, bias=col[:, 2:3]).then_inc(ms_ln, 1)
                    act.wait_ge(ms_ln, i * 2)
                    nc.scalar.activation(o_rs[:], o_rs[:], ACT.Exp, scale=-0.5).then_inc(ors_done, 1)

            evacs = ((ff, ACT.Sigmoid), (qq, ACT.Silu), (vt, ACT.Copy), (gg, ACT.Silu), (gate[0], ACT.Sigmoid), (gate[1], ACT.Sigmoid))

            def hgrn(i, prev, cur):
                for slot in range(2 * HG_CHUNKS):
                    c, hf = slot // 2, slot % 2
                    if cur and hf == 0 and not (first(i) and c == 0):
                        split_hi(i * HG_CHUNKS + c + 1, (c + 1) % 2)
                    if prev:
                        hgrn_tail(i, slot)
                    if cur:
                        hgrn_cur(i, slot)
                        if first(i) and slot == 4:
                            act.wait_ge(rope_step, 1)
                        if first(i) and slot == 6:
                            act.wait_ge(mask_done, MASKS)
                        if slot == 6 and prev:
                            act.wait_ge(oa_done, i)
                        if c >= 4 and hf == 0 and prev:
                            act.wait_ge(gate_stored[c - 4], 16 * i)
                        take(i * HG_CHUNKS + c, hf, *evacs[c])

            hgrn(0, False, True)
            with act.Fori(1, HEADS) as i:
                hgrn(i, True, True)
            nc.scalar.activation(cos_t[:], cos_t[:], ACT.Sin).then_inc(sin_done, 1)
            nc.scalar.activation(sin_t[:], sin_t[:], ACT.Sin).then_inc(sin_done, 1)

            def attention(i, prev, cur):
                for slot in range(2 * AT_CHUNKS):
                    c, hf = slot // 2, slot % 2
                    n = N_HG + i * AT_CHUNKS + c
                    if cur and hf == 0:
                        split_hi(n + 1, (c + 1) % 2)
                    if first(i):
                        hgrn_tail(HEADS, slot)
                        if slot == 0:
                            act.wait_ge(lvl_made, N_UNIT_HG * HEADS)
                        if slot == 5:
                            act.wait_ge(lvl_taken, N_UNIT_HG * HEADS)
                        if slot == 7:
                            act.wait_ge(oa_done, HEADS)
                        if slot == 12:
                            act.wait_ge(k_dupped, 1)
                            act.wait_ge(oa_stored, 16 * HEADS)
                            for s in range(2):
                                act.wait_ge(gate_stored[s], 16 * HEADS)
                    if cur and slot >= 5 and hf == 1 and slot <= 15:
                        j = (slot - 5) // 2
                        act.wait_ge(rope_sum, i * 6 + j + 1)
                        if prev:
                            act.wait_ge(st_made, (i - 1) * N_UNITS + (8, 16, 20)[j // 2])
                        if j < 4:
                            for h in range(2):
                                rows = slice(EDIM * h, EDIM * (h + 1))
                                last = nc.scalar.activation((q_st, k_dup)[j % 2][j // 2][h][rows, :], roped[rows, :], ACT.Copy)
                            last.then_inc(qk_hi_done, 1)
                        else:
                            nc.scalar.activation(qk_hi[j % 2][:], qk_full[j % 2][:], ACT.Copy).then_inc(qk_hi_done, 1)
                    if cur and slot in (15, 17, 19):
                        g = (slot - 15) // 2
                        act.wait_ge(avt_made, i * 3 + g + 1)
                        for b in range(2):
                            dst = vb[:, g, 4 * b:4 * b + 4, :].rearrange("p c (x e) -> p c x e", e=EDIM)[:, :, 0:3:2, :]
                            nc.scalar.activation(dst, pb[:, b, :].rearrange("p (c x e) -> p c x e", c=4, x=2), ACT.Copy).then_inc(av_taken, 1)
                    if cur:
                        if c < 6:
                            if not first(i) or c >= 2:
                                act.wait_ge(rope_sum, i * 6 + c - 1)
                            take(n, hf, zz[c % 2], ACT.Copy, scale=0.125 if c % 2 == 0 else 1.0)
                        elif c < 9:
                            g = c - 6
                            act.wait_ge(z_made[hf], n + 1)
                            if hf == 0 and (g or prev):
                                act.wait_ge(avt_made, i * 3 + g)
                            if g == 0 and hf == 0 and prev:
                                act.wait_ge(shift_done, i)
                            r = DILATIONS[g]
                            w = HALF // r
                            dst = v_t[:].rearrange("p (r i) -> p r i", r=r)[:, :, w * hf:w * (hf + 1)]
                            nc.scalar.activation(dst, z_ps[hf][:].rearrange("p (i r) -> p r i", r=r), ACT.Copy).then_inc(z_taken[hf], 1)
                        else:
                            if prev and hf == 0:
                                act.wait_ge(ob_done, 2 * i)
                            take(n, hf, s_ag, ACT.Silu)
                    if prev and slot == 13:
                        act.wait_ge(ob_taken, i * N_SUMS)
                        nc.scalar.activation(r_den[0:EDIM, :], acc[0][EDIM:P, :], ACT.Ln).then_inc(den_ln, 1)
                        nc.scalar.activation(r_den[EDIM:P, :], acc[1][0:EDIM, :], ACT.Ln).then_inc(den_ln, 1)
                        act.wait_ge(den_ln, 2 * i)
                        nc.scalar.activation(r_den[:], r_den[:], ACT.Exp, scale=-1.0).then_inc(den_done, 1)
                    if prev:
                        for u in UNIT_SLOTS.get(slot, ()):
                            act.wait_ge(st_made, (i - 1) * N_UNITS + u + 1)
                            cols = sum(P * k for _, _, k in unit_keys(UNITS[u][0], UNITS[u][2]))
                            if u >= 2:
                                act.wait_ge(pu_made, (i - 1) * N_UNITS + u - 1)
                            nc.scalar.activation(pt[u % 2][:, 0:cols], pb[:, u % 2, 0:cols], ACT.Exp).then_inc(pt_done, 1)
                    if not cur:
                        if 1 <= slot < N_BR:
                            branch_hi(slot - 1)
                        if slot in (12, 14):
                            branch_w_hi(N_IN + slot // 2 - 5)
                    if cur and slot == 17:
                        act.wait_ge(mt_made, i + 1)
                        if prev:
                            act.wait_ge(m_stored, 16 * i)
                        nc.scalar.activation(m_t[:], pc[0:2 * GROUPS * NB, 0, 0:P], ACT.Copy, scale=-1.0).then_inc(mt_taken, 1)

            def branch_hi(t):
                if t == 0:
                    act.wait_ge(z_made[1], N_IN)
                if t == HEADS:
                    act.wait_ge(st_made, (PAIRS - 1) * N_UNITS + 16)
                if t == N_BR - 1:
                    act.wait_ge(ob_done, 2 * PAIRS)
                    src = o_b
                else:
                    act.wait_ge(br_loaded[t % 4], 16 * (t // 4 + 1))
                    src = br_in[t % 4]
                dst = oa_hi[:, t, :] if t < HEADS else ob_hi[:, t - HEADS, :]
                nc.scalar.activation(dst, src[:], ACT.Copy).then_inc(br_hi_done, 1)

            def branch_w_hi(n):
                kt = HEADS if n % 2 == 0 else PAIRS
                act.wait_ge(z_made[1], n - 1 if n % 2 == 0 or n < N_IN + 2 else n - 3)
                act.wait_ge(w_loaded[n % 2], w_count(n, n % 2))
                nc.scalar.activation(w_hi[n % 2][:, branch_tiles(n), :], w_stage[n % 2][:, 0:kt, :], ACT.Copy).then_inc(w_hi_done, 1)

            attention(0, False, True)
            with act.Fori(1, PAIRS - 1) as i:
                attention(i, True, True)
            attention(PAIRS - 1, True, True)
            attention(PAIRS, True, False)

            branch_hi(N_BR - 1)
            branch_w_hi(N_IN + 3)

            def split_out_hi(n):
                c = n - N_IN - 16
                if c < 2:
                    act.wait_ge(w_loaded[n % 2], w_count(n, n % 2))
                else:
                    act.wait_ge(wo_loaded[c - 2], 16)
                if c == 2:
                    act.wait_ge(z_made[1], N_IN + 16)
                dst = wq_hi if c < 2 else oa_hi
                nc.scalar.activation(dst[:, :, P * c:P * c + P], out_stage(c), ACT.Copy).then_inc(w_hi_done, 1)

            for j in range(KT):
                for b in range(2):
                    n = N_IN + 2 * j + b + 1
                    if (j, b) == (0, 0):
                        branch_w_hi(N_IN + 4)
                    elif N_IN + 4 < n < N_IN + 16:
                        branch_w_hi(n)
                    elif n >= N_IN + 16:
                        split_out_hi(n)
                if j == KT - 1:
                    split_out_hi(N_IN + 17)
                for hf in range(2):
                    t = slice(HALF * hf, HALF * (hf + 1))
                    act.wait_ge(mg_sum, 2 * j + hf + 1)
                    nc.scalar.activation(mg_hi[:, j, t], part[:, t], ACT.Copy).then_inc(mg_hi_done, 1)
            for c in range(2, 8):
                split_out_hi(N_IN + 16 + c)
            for t in range(NB):
                act.wait_ge(pb_taken, 2 * t + 2)
                nc.scalar.activation(g_in[0][:], yy[:, t, :], ACT.Square, accum_out=o_stat[:, 0, t:t + 1]).then_inc(oss_done, 1)
                act.wait_ge(oss_done, t + 1)
                nc.scalar.activation(o_stat[:, 1, t:t + 1], o_stat[:, 0, t:t + 1], ACT.Sqrt, scale=1.0 / D_MODEL, bias=col[:, 2:3]).then_inc(orms_done, 1)

        @block.vector
        def _(dve):
            dve.wait_ge(lb_loaded, 16)
            nc.vector.tensor_tensor(lb[:, 0, :], lb_in[:, 0, :], lb_in[:, 1, :], ALU.max).then_inc(lb_step, 1)
            dve.wait_ge(lb_step, 1)
            for r in range(2):
                nc.vector.tensor_tensor(lb[:, 1 + r, :], lb_in[:, r, :], lb[:, 0, :], ALU.subtract).then_inc(lb_step, 1)
            dve.wait_ge(const_in, 32)

            def split_lo(n, s):
                dve.wait_ge(w_hi_done, n + 1)
                if isinstance(n, int) and n == 2:
                    dve.wait_ge(w_lo_done, 2)
                nc.vector.tensor_tensor(w_lo[s][:], w_stage[s][:], w_hi[s][:].bitcast(f32), ALU.subtract).then_inc(w_lo_done, 1)

            def square(t):
                dve.wait_ge(x_loaded[t], 16)
                n = DVE_SQUARES.index(t)
                if n:
                    dve.wait_ge(ss_dve, n)
                nc.vector.tensor_tensor_reduce(out=dd[1][:], in0=x_in[:, t, :], in1=x_in[:, t, :], scale=1.0, scalar=0.0,
                                               op0=ALU.mult, op1=ALU.add, accum_out=x_ss[:, t:t + 1]).then_inc(ss_dve, 1)

            square(1)
            square(3)
            for hf in range(2):
                ts = slice(4 * hf, 4 * hf + 4)
                dve.wait_ge(rms_done, hf + 1)
                nc.vector.reciprocal(x_rs[:, ts], x_rms[:, ts]).then_inc(rs_done, 1)
                dve.wait_ge(rs_done, hf + 1)
                for t in (4 * hf, 4 * hf + 1, 4 * hf + 2):
                    nc.vector.tensor_scalar(x_in[:, t, :], x_in[:, t, :], x_rs[:, t:t + 1], None, ALU.mult).then_inc(xn_done, 1)
                for u in range(KT * hf, KT * hf + KT):
                    k, ts = u % KT, slice(HALF * hf, HALF * (hf + 1))
                    dve.wait_ge(h_hi_done, u + 1)
                    nc.vector.scalar_tensor_tensor(h_lo[:, k, ts], (pa, pb)[u // 2 % 2][:, u % 2, :], norm_w[:, k:k + 1],
                                                   h_hi[:, k, ts].bitcast(f32), ALU.mult, ALU.subtract).then_inc(h_lo_done, 1)
                    if u in (2, 5):
                        square(4 + u // 5)
            dve.wait_ge(hg_loaded, 32)
            dve.wait_ge(init_done, 3)

            def exponents(i, u):
                if u == 0:
                    b = bb[:].rearrange("p (c t) -> p c t", t=P)
                    nc.vector.tensor_tensor(dd[0][:].rearrange("p (c t) -> p c t", t=P), b[:, :, P - 1:P].to_broadcast([P, NB, P]), b, ALU.subtract).then_inc(d_done, 1)
                    return
                span = LEVELS[u - 1]
                n = HALF // span
                b = bb[:].rearrange("p (n two l) -> p n two l", two=2, l=span)
                mid = b[:, :, 0, span - 1:span].to_broadcast([P, n, span])
                dst = dd[u % 2][:].rearrange("p (two n l) -> p two n l", two=2, l=span)
                nc.vector.tensor_tensor(dst[:, 0], b[:, :, 1, :], mid, ALU.subtract)
                nc.vector.tensor_tensor(dst[:, 1], mid, b[:, :, 0, :], ALU.subtract).then_inc(d_done, 1)

            def level_factors(i, u):
                dve.wait_ge(e_done, i * 7 + u + 1)
                if u == 0:
                    nc.vector.tensor_tensor(k_out[:], kk[:], ee[0][:], ALU.mult).then_inc(k_out_done, 1)
                    return
                span = LEVELS[u - 1]
                s = (u - 1) % 2
                if u >= 3:
                    dve.wait_ge(lvl_made, i * N_UNIT_HG + u)
                e = ee[u % 2][:].rearrange("p (two n l) -> p two n l", two=2, l=span)
                cut = lambda t: t[:].rearrange("p (n two l) -> p n two l", two=2, l=span)
                nc.vector.tensor_tensor(q_lv[s][:].rearrange("p (n l) -> p n l", l=span), cut(qq)[:, :, 1, :], e[:, 0], ALU.mult)
                nc.vector.tensor_tensor(cut(k_lv[s])[:, :, 0, :], cut(kk)[:, :, 0, :], e[:, 1], ALU.mult).then_inc(lv_done, 1)

            def pick(i, j):
                made, taken = value(dve, i * N_UNIT_HG + j + 1), value(dve, i * N_UNIT_HG + j)
                span = LEVELS[j - 2] if j >= 2 else 1
                dve.wait_ge(mask_done, MASKS)
                dve.wait_ge(lvl_made, made)
                if not first(i) or j > 0:
                    dve.wait_ge(lvl_taken, taken)
                if 2 <= j < 4:
                    for g in range(64 // span):
                        rows = slice(2 * span * g, 2 * span * g + span)
                        dst = scores[rows, :, 2 * span * g + span:2 * span * (g + 1)]
                        src = pb[rows, j % 2, :].rearrange("p (c t) -> p c t", t=64)[:, :, span * g:span * (g + 1)]
                        last = nc.vector.tensor_copy(dst, src)
                    last.then_inc(lvl_taken, 1)
                    return
                dst = scores[:].rearrange("p c t -> p (c t)").rearrange("p (n two l) -> p n two l", two=2, l=span)[:, :, int(j != 1), :]
                src = pb[:, j % 2, :].rearrange("p (n l) -> p n l", l=span)
                mask = level_mask[:, j if j < 2 else j - 2, :].rearrange("p (n l) -> p n l", l=span)
                nc.vector.copy_predicated(dst, mask, src).then_inc(lvl_taken, 1)

            def hgrn_cur(i, slot):
                if slot == 2:
                    for s in range(2):
                        dve.wait_ge(z_taken[s], i * HG_CHUNKS + 1)
                    head = bass.ds(i, 1)
                    nc.vector.tensor_scalar(ff[:], ff[:], lb[:, 5, head], lb[:, 4, head], ALU.mult, ALU.add).then_inc(f_done, 1)
                    dve.wait_ge(f_done, i + 1)
                    nc.vector.tensor_scalar(kk[:], ff[:], -1.0, 1.0, ALU.mult, ALU.add).then_inc(k_done, 1)
                    dve.wait_ge(ln_done, i + 1)
                    nc.vector.tensor_tensor_scan(bb[:], reset[:], lf[:], 0.0, ALU.mult, ALU.add).then_inc(b_done, 1)
                    dve.wait_ge(b_done, i + 1)
                if slot == 4:
                    for s in range(2):
                        dve.wait_ge(z_taken[s], i * HG_CHUNKS + 2)
                    if not isinstance(i, int) or i > 0:
                        dve.wait_ge(pv_made, i)
                    dve.wait_ge(eb_done, i + 1)
                    nc.vector.tensor_tensor(q_in[:], qq[:], eb[:], ALU.mult).then_inc(q_in_done, 1)
                if slot == 3:
                    dve.wait_ge(k_done, i + 1)
                    if not first(i):
                        dve.wait_ge(lvl_made, i * N_UNIT_HG)
                    by_two = lambda t, a: t[:].rearrange("p (n two) -> p n two", two=2)[:, :, a]
                    nc.vector.tensor_copy(by_two(k_one, 1), by_two(kk, 1))
                    nc.vector.tensor_tensor(by_two(k_one, 0), by_two(kk, 0), by_two(ff, 1), ALU.mult).then_inc(k_one_done, 1)
                if 4 <= slot <= 10:
                    level_factors(i, slot - 4)
                if 3 <= slot <= 9:
                    exponents(i, slot - 3)
                if slot == 6:
                    pick(i, 0)
                    pick(i, 1)
                elif slot >= 7:
                    pick(i, slot - 5)
                if slot == 10:
                    dve.wait_ge(upd_made, i + 1)
                    for c in range(1, NB):
                        src = pc[:, (c - 1) // 4, P * ((c - 1) % 4):P * ((c - 1) % 4 + 1)]
                        if c == 1:
                            nc.vector.tensor_copy(state[:, c, :], src).then_inc(s_done, 1)
                        else:
                            dve.wait_ge(s_done, i * 7 + c - 1)
                            nc.vector.scalar_tensor_tensor(state[:, c, :], state[:, c - 1, :], eb[:, P * c - 1:P * c], src, ALU.mult, ALU.add).then_inc(s_done, 1)

            def hgrn_tail(i, slot):
                if slot == 0:
                    pick(i - 1, N_UNIT_HG - 1)
                if slot == 3:
                    dve.wait_ge(sq_done, 2 * i)
                    nc.vector.tensor_tensor(sq_lo[:], o_sq[:], sq_hi[:].bitcast(f32), ALU.subtract).then_inc(sq_lo_done, 1)
                if slot == 5:
                    dve.wait_ge(ors_done, i)
                    if not isinstance(i, int) or i > 1:
                        dve.wait_ge(oa_stored, 16 * i - 16)
                    for hf in range(2):
                        t = slice(HALF * hf, HALF * (hf + 1))
                        last = nc.vector.tensor_tensor(o_a[:, t], pc[:, hf, :], o_rs[:, t], ALU.mult)
                    last.then_inc(on_done, 1)
                    dve.wait_ge(on_done, i)
                    nc.vector.scalar_tensor_tensor(o_a[:], o_a[:], hgw[:], gg[:], ALU.mult, ALU.mult).then_inc(oa_done, 1)

            def lower_bound():
                dve.wait_ge(lb_step, 4)
                nc.vector.tensor_tensor(lb[:, 3, :], lb[:, 1, :], lb[:, 2, :], ALU.add).then_inc(lb_step, 1)
                dve.wait_ge(lb_step, 5)
                nc.vector.reciprocal(lb[:, 3, :], lb[:, 3, :]).then_inc(lb_step, 1)
                dve.wait_ge(lb_step, 6)
                nc.vector.tensor_tensor(lb[:, 4, :], lb[:, 1, :], lb[:, 3, :], ALU.mult).then_inc(lb_step, 1)
                dve.wait_ge(lb_step, 7)
                nc.vector.tensor_scalar(lb[:, 5, :], lb[:, 4, :], -1.0, 1.0, ALU.mult, ALU.add).then_inc(lb_step, 1)
                dve.wait_ge(lb_step, 8)
                nc.vector.tensor_scalar(lb[:, 4, :], lb[:, 4, :], TINY, None, ALU.max).then_inc(lb_step, 1)
                dve.wait_ge(lb_step, 9)

            def hgrn(i, prev, cur):
                for slot in range(2 * HG_CHUNKS):
                    if cur and slot % 2 == 0 and not (first(i) and slot == 0):
                        split_lo(i * HG_CHUNKS + slot // 2 + 1, (slot // 2 + 1) % 2)
                    if first(i) and slot == 0:
                        lower_bound()
                    if prev:
                        hgrn_tail(i, slot)
                    if cur:
                        hgrn_cur(i, slot)

            hgrn(0, False, True)
            with dve.Fori(1, HEADS) as i:
                hgrn(i, True, True)

            def row_max(i, g, m, h):
                u = 2 * (g * 4 + m) + h
                todo = max_queries(g, m)
                for k, (blk, at, before) in enumerate(todo):
                    lo, w = (at, 2 * P) if before else (at if g == 2 else at + P, P)
                    mask = mask_n[:, 2 * P:] if g == 2 else mask_n[:, 2 * P - w:2 * P]
                    at_m = (h * GROUPS + g) * NB + blk
                    done = max_count(u) + k
                    made, written = value(dve, i * 20 + u + 1), value(dve, i * N_MAX + done - 1)
                    dve.wait_ge(mask_done, MASKS)
                    if k == 0:
                        dve.wait_ge(mx_made, made)
                    if not first(i) or done >= 2:
                        dve.wait_ge(mx_taken, written)
                    nc.vector.tensor_tensor_reduce(out=junk[:, done % 2, 0:w], in0=max_bank(g, m)[:, h, lo:lo + w], in1=mask, scale=1.0, scalar=NEG,
                                                       op0=ALU.add, op1=ALU.max, accum_out=m_all[:, at_m:at_m + 1]).then_inc(mx_taken, 1)

            def attention(i, prev, cur):
                for slot in range(2 * AT_CHUNKS):
                    c, hf = slot // 2, slot % 2
                    n = N_HG + i * AT_CHUNKS + c
                    if prev:
                        for k in SUM_SLOTS.get(slot, ()):
                            g, h, b = k // 4, k // 2 % 2, k % 2
                            dve.wait_ge(pu_made, (i - 1) * N_UNITS + SUM_AFTER[k] + 1)
                            if g == 0:
                                nc.vector.tensor_copy(acc[h][:, HALF * b:HALF * (b + 1)], pc[:, b, :]).then_inc(ob_taken, 1)
                            else:
                                r = DILATIONS[g]
                                dst = by_residue(acc[h][:], g)[:, r // 2 * b:r // 2 * (b + 1), :]
                                dve.wait_ge(ob_taken, (i - 1) * N_SUMS + k)
                                nc.vector.tensor_tensor(dst, pc[:, b, :].rearrange("p (r i) -> p r i", r=r // 2), dst, ALU.add).then_inc(ob_taken, 1)
                    if cur:
                        for g, m in MAX_SLOTS.get(slot - 1, ()):
                            for h in range(2):
                                row_max(i, g, m, h)
                    if cur and hf == 0:
                        split_lo(n + 1, (c + 1) % 2)
                    if first(i):
                        hgrn_tail(HEADS, slot)
                        if slot == 4:
                            dve.wait_ge(sin_done, 2)
                        if slot == 12:
                            dve.wait_ge(oa_stored, 16 * HEADS)
                            for s in range(2):
                                dve.wait_ge(gate_stored[s], 16 * HEADS)
                    if prev and slot == 0:
                        dve.wait_ge(m_loaded, 16 * i)
                        r4 = m_rows[:, 1, :].rearrange("p (r i) -> p i r", r=4)
                        r16 = m_rows[:, 2, :].rearrange("p (r i) -> p i r", r=16)
                        r1 = m_rows[:, 0, :]
                        nc.vector.tensor_tensor(r1.rearrange("p (i r) -> p i r", r=4), r1.rearrange("p (i r) -> p i r", r=4), r4, ALU.min).then_inc(mj_done, 1)
                        dve.wait_ge(mj_done, i)
                        nc.vector.tensor_tensor(shift[:].rearrange("p (i r) -> p i r", r=16), r1.rearrange("p (i r) -> p i r", r=16), r16, ALU.min).then_inc(shift_done, 1)
                    if cur and 4 <= slot <= 14 and hf == 0:
                        j = (slot - 4) // 2
                        dve.wait_ge(swapped, (i * 6 + j + 1) * 64)
                        nc.vector.tensor_tensor(zz[j % 2][:], zz[j % 2][:], cos_t[:], ALU.mult).then_inc(rope_a, 1)
                        nc.vector.tensor_tensor(z_swap[:], z_swap[:], sin_t[:], ALU.mult).then_inc(rope_b, 1)
                        dve.wait_ge(rope_a, i * 6 + j + 1)
                        dve.wait_ge(rope_b, i * 6 + j + 1)
                        r = DILATIONS[j // 2]
                        nat = lambda t: t[:].rearrange("p (i r) -> p i r", r=r)
                        dst = roped if j < 4 else qk_full[j % 2]
                        if j >= 4 and prev:
                            dve.wait_ge(st_made, i * N_UNITS)
                        nc.vector.tensor_tensor(dst[:].rearrange("p (r i) -> p i r", r=r), nat(zz[j % 2]), nat(z_swap), ALU.add).then_inc(rope_sum, 1)
                    if cur and 5 <= slot <= 11 and hf == 1:
                        j = (slot - 5) // 2
                        dve.wait_ge(qk_hi_done, i * 6 + j + 1)
                        g = j // 2
                        for h in range(2):
                            own, other = slice(EDIM * h, EDIM * (h + 1)), slice(EDIM * (1 - h), EDIM * (2 - h))
                            dst, hi = (q_st[g][h][other, :], q_st[g][h]) if j % 2 == 0 else (k_lo[g][own, :], k_dup[g][h])
                            last = nc.vector.tensor_tensor(dst, roped[own, :], hi[own, :].bitcast(f32), ALU.subtract)
                        last.then_inc(qk_lo_done, 1)
                    if not cur:
                        if 2 <= slot <= N_BR:
                            branch_lo(slot - 2)
                        if slot == 12:
                            branch_w_lo(N_IN + 1)
                        if slot == 13:
                            gated(0, 0)
                            branch_w_lo(N_IN + 2)
                    if prev and slot == (16 if cur else 14):
                        dve.wait_ge(den_done, i)
                        nc.vector.tensor_tensor(r_den[:], r_den[:], s_ag[:], ALU.mult).then_inc(den_ag, 1)
                        dve.wait_ge(den_ag, i)
                        if not isinstance(i, int) or i > 1:
                            dve.wait_ge(ob_stored, 16 * i - 16)
                        for h in range(2):
                            rows = slice(EDIM * h, EDIM * (h + 1))
                            nc.vector.tensor_tensor(o_b[rows, :], acc[h][rows, :], r_den[rows, :], ALU.mult).then_inc(ob_done, 1)

            def branch_lo(t):
                dve.wait_ge(br_hi_done, t + 1)
                lo, hi = (oa_lo[:, t, :], oa_hi[:, t, :]) if t < HEADS else (ob_lo[:, t - HEADS, :], ob_hi[:, t - HEADS, :])
                src = o_b if t == N_BR - 1 else br_in[t % 4]
                nc.vector.tensor_tensor(lo, src[:], hi.bitcast(f32), ALU.subtract).then_inc(br_lo_done, 1)

            def branch_w_lo(n):
                kt, s = HEADS if n % 2 == 0 else PAIRS, n % 2
                dve.wait_ge(w_hi_done, n + 1)
                ks = branch_tiles(n)
                nc.vector.tensor_tensor(w_lo[s][:, ks, :], w_stage[s][:, 0:kt, :], w_hi[s][:, ks, :].bitcast(f32), ALU.subtract).then_inc(w_lo_done, 1)

            def gated(j, b):
                n = N_IN + 2 * j + b
                dve.wait_ge(g_loaded[b], 16 * (j + 1))
                if b == 0 and j:
                    dve.wait_ge(mg_lo_done, 2 * j)
                for hf in range(2):
                    t = slice(HALF * hf, HALF * (hf + 1))
                    dve.wait_ge(z_made[hf], n + 1)
                    if b == 0:
                        nc.vector.tensor_tensor(part[:, t], z_ps[hf][:], g_in[0][:, t], ALU.mult).then_inc(z_taken[hf], 1)
                    else:
                        nc.vector.tensor_tensor(g_in[1][:, t], pa[:, hf, :], g_in[1][:, t], ALU.mult).then_inc(z_taken[hf], 1)

            attention(0, False, True)
            with dve.Fori(1, PAIRS - 1) as i:
                attention(i, True, True)
            attention(PAIRS - 1, True, True)
            attention(PAIRS, True, False)

            branch_lo(N_BR - 1)
            branch_w_lo(N_IN + 3)
            def split_out_lo(n):
                c = n - N_IN - 16
                dve.wait_ge(w_hi_done, n + 1)
                hi, lo = (wq_hi, wq_lo) if c < 2 else (oa_hi, oa_lo)
                cols = slice(P * c, P * c + P)
                nc.vector.tensor_tensor(lo[:, :, cols], out_stage(c), hi[:, :, cols].bitcast(f32), ALU.subtract).then_inc(w_lo_done, 1)

            for j in range(KT):
                for b in range(2):
                    n = N_IN + 2 * j + b
                    if N_IN + 4 < n + 1 < N_IN + 16:
                        branch_w_lo(n + 1)
                    elif n + 1 >= N_IN + 16:
                        split_out_lo(n + 1)
                        split_out_lo(n + 2)
                    if j or b:
                        gated(j, b)
                    if (j, b) == (0, 1):
                        branch_w_lo(N_IN + 4)
                for hf in range(2):
                    t = slice(HALF * hf, HALF * (hf + 1))
                    dve.wait_ge(z_taken[hf], N_IN + 2 * j + 2)
                    nc.vector.tensor_tensor(part[:, t], part[:, t], g_in[1][:, t], ALU.add).then_inc(mg_sum, 1)
                for hf in range(2):
                    t = slice(HALF * hf, HALF * (hf + 1))
                    dve.wait_ge(mg_hi_done, 2 * j + hf + 1)
                    nc.vector.tensor_tensor(mg_lo[:, j, t], part[:, t], mg_hi[:, j, t].bitcast(f32), ALU.subtract).then_inc(mg_lo_done, 1)
            for t in range(NB):
                dve.wait_ge(qa_made, t + 1)
                dve.wait_ge(y_loaded[t], 16)
                nc.vector.tensor_tensor(yy[:, t, 0:2 * P], (z_ps[t % 4][:, 0:2 * P] if t % 4 < 2 else pb[:, t % 2, 0:2 * P]), yy[:, t, 0:2 * P], ALU.add).then_inc(qa_taken, 1)
                if t < 6:
                    split_out_lo(N_IN + 18 + t)
            dve.wait_ge(fnw_loaded, 16)
            for t in range(NB + 1):
                if t < NB:
                    src = (pc, pa, pb)[t % 3]
                    dve.wait_ge(pb_made, 2 * t + 1)
                    nc.vector.tensor_tensor(yy[:, t, 2 * P:6 * P], src[:, 0, :], yy[:, t, 2 * P:6 * P], ALU.add).then_inc(pb_taken, 1)
                    dve.wait_ge(pb_made, 2 * t + 2)
                    nc.vector.tensor_tensor(yy[:, t, 6 * P:], src[:, 1, 0:2 * P], yy[:, t, 6 * P:], ALU.add).then_inc(pb_taken, 1)
                if t:
                    dve.wait_ge(orms_done, t)
                    nc.vector.reciprocal(o_stat[:, 2, t - 1:t], o_stat[:, 1, t - 1:t]).then_inc(ors2_done, 1)
                    dve.wait_ge(ors2_done, t)
                    nc.vector.scalar_tensor_tensor(yy[:, t - 1, :], yy[:, t - 1, :], o_stat[:, 2, t - 1:t], fnw[:], ALU.mult, ALU.mult).then_inc(out_done, 1)


def kernel(**inputs):
    import concourse.bacc as bacc
    from concourse.bass_utils import run_bass_kernel_spmd

    f = {k: np.asarray(v) for k, v in inputs.items()}
    w = f["w_in"][0].reshape(KT, P, -1)
    arrays = {
        "x": f["x"][0],
        "positions": f["positions"],
        "norm_w": f["norm_w"][0].reshape(KT, P).T,
        "w_in": np.stack([w[:, :, c:c + P].transpose(1, 0, 2) for c in chunk_columns()]),
        "lb_logits": f["lb_logits"].reshape(2, HEADS, P).transpose(2, 0, 1),
        "hgrn_norm_w": f["hgrn_norm_w"][0].reshape(P, 1),
        "w_a": f["w_branch_a"][0].reshape(8, P, 8, P).transpose(2, 1, 0, 3),
        "w_b": f["w_branch_b"][0].reshape(4, P, 8, P).transpose(2, 1, 0, 3),
        "w_out": f["w_out"][0].reshape(8, P, 8, P).transpose(2, 1, 0, 3),
        "final_norm_w": f["final_norm_w"].reshape(1, D_MODEL),
    } | shape_constants()
    arrays = {k: np.ascontiguousarray(v) for k, v in arrays.items()}
    nc = bacc.Bacc("TRN2", target_bir_lowering=False, num_devices=1, dynamic_dma_scratch_size=1024)
    d = {k: nc.dram_tensor(k, v.shape, mybir.dt.from_np(v.dtype), kind="ExternalInput").ap() for k, v in arrays.items()}
    out = nc.dram_tensor("out", (SEQ, D_MODEL), mybir.dt.float32, kind="ExternalOutput").ap()
    build(nc, d, out)
    r = run_bass_kernel_spmd(nc, [arrays], core_ids=[0])
    return r.results[0]["out"].reshape(1, SEQ, D_MODEL)
```
